# Optimizing a Trainium2 kernel written in Bass

```python
import jax, jax.numpy as jnp
from jax import lax
import numpy as np

D_MODEL = 1024
BATCH = 1
SEQ = 256
DEPTH = 1

SSD_EXPAND = 2
D_INNER = SSD_EXPAND * D_MODEL
SSD_HEAD_DIM = 64
SSD_HEADS = D_INNER // SSD_HEAD_DIM
SSD_GROUPS = 4
SSD_HEADS_PER_GROUP = SSD_HEADS // SSD_GROUPS
SSD_STATE = 128
SSD_CONV = 4
SSD_CHUNK = 128
SSD_CONV_DIM = D_INNER + 2 * SSD_GROUPS * SSD_STATE
MLA_HEADS = 16
MLA_Q_LORA = 256
MLA_KV_LORA = 128
MLA_NOPE = 64
MLA_ROPE = 32
MLA_QK_DIM = MLA_NOPE + MLA_ROPE
MLA_V_DIM = 64
MLA_WIDTH = MLA_HEADS * MLA_V_DIM
ROPE_THETA = 10000.0
ATTN_Q_BLOCK = 128
D_FF = 2816
FFN_CONV = 3
NORM_EPS = 1e-6

OFF_Z = D_INNER
OFF_XBC = OFF_Z + SSD_CONV_DIM
OFF_DT = OFF_XBC + SSD_HEADS
OFF_QA = OFF_DT + MLA_Q_LORA
OFF_KVA = OFF_QA + MLA_KV_LORA
OFF_KR = OFF_KVA + MLA_ROPE
IN_COLS = OFF_KR + 2 * D_MODEL


def rms_norm(x, g):
    xf = x.astype(jnp.float32)
    xf = xf * lax.rsqrt(jnp.mean(xf * xf, axis=-1, keepdims=True) + NORM_EPS)
    return (xf * g.astype(jnp.float32)).astype(x.dtype)

def causal_depthwise_conv(x, w, b):
    k, c = w.shape
    y = lax.conv_general_dilated(x, w[:, None, :].astype(x.dtype), window_strides=(1,),
                                 padding=[(k - 1, 0)], dimension_numbers=('NWC', 'WIO', 'NWC'),
                                 feature_group_count=c)
    return y + b

def rope_tables(seq, dim):
    inv = 1.0 / (ROPE_THETA ** (jnp.arange(0, dim, 2, dtype=jnp.float32) / dim))
    ang = jnp.arange(seq, dtype=jnp.float32)[:, None] * inv[None, :]
    return jnp.cos(ang)[None, :, None, :], jnp.sin(ang)[None, :, None, :]

def apply_rope(x, cos, sin):
    x1, x2 = jnp.split(x.astype(jnp.float32), 2, axis=-1)
    return jnp.concatenate([x1 * cos - x2 * sin, x1 * sin + x2 * cos], axis=-1).astype(x.dtype)

def ssd_chunked_scan(xdt, a, bm, cm):
    b, l, h, p = xdt.shape
    nc = l // SSD_CHUNK
    f32 = jnp.float32
    xc = xdt.astype(f32).reshape(b, nc, SSD_CHUNK, SSD_GROUPS, SSD_HEADS_PER_GROUP, p)
    bc = bm.astype(f32).reshape(b, nc, SSD_CHUNK, SSD_GROUPS, SSD_STATE)
    cc = cm.astype(f32).reshape(b, nc, SSD_CHUNK, SSD_GROUPS, SSD_STATE)
    ac = a.astype(f32).reshape(b, nc, SSD_CHUNK, SSD_GROUPS, SSD_HEADS_PER_GROUP).transpose(0, 1, 3, 4, 2)
    a_cum = jnp.cumsum(ac, axis=-1)
    causal = jnp.tril(jnp.ones((SSD_CHUNK, SSD_CHUNK), dtype=bool))
    seg = a_cum[..., :, None] - a_cum[..., None, :]
    decay_in = jnp.exp(jnp.where(causal, seg, -jnp.inf))
    scores = jnp.einsum('bclgn,bcsgn->bcgls', cc, bc)
    y_diag = jnp.einsum('bcgls,bcgels,bcsgep->bclgep', scores, decay_in, xc)
    decay_to_end = jnp.exp(a_cum[..., -1:] - a_cum)
    chunk_states = jnp.einsum('bclgn,bcgel,bclgep->bcgepn', bc, decay_to_end, xc)
    chunk_decay = jnp.exp(a_cum[..., -1])

    def carry_state(state, inp):
        new_states, decay = inp
        return state * decay[..., None, None] + new_states, state

    init = jnp.zeros_like(chunk_states[:, 0])
    _, prev = lax.scan(carry_state, init,
                       (jnp.moveaxis(chunk_states, 1, 0), jnp.moveaxis(chunk_decay, 1, 0)))
    y_off = jnp.einsum('bclgn,cbgepn,bcgel->bclgep', cc, prev, jnp.exp(a_cum))
    return (y_diag + y_off).reshape(b, l, h, p).astype(xdt.dtype)

def ssd_mixer(z, xbc, dt_raw, conv_w, conv_b, dt_bias, a_log, d_skip, norm_g):
    b, l, _ = z.shape
    xbc = jax.nn.silu(causal_depthwise_conv(xbc, conv_w, conv_b))
    xs, bm, cm = jnp.split(xbc, [D_INNER, D_INNER + SSD_GROUPS * SSD_STATE], axis=-1)
    xs = xs.reshape(b, l, SSD_HEADS, SSD_HEAD_DIM)
    bm = bm.reshape(b, l, SSD_GROUPS, SSD_STATE)
    cm = cm.reshape(b, l, SSD_GROUPS, SSD_STATE)
    dt = jax.nn.softplus(dt_raw.astype(jnp.float32) + dt_bias.astype(jnp.float32))
    a = -jnp.exp(a_log.astype(jnp.float32))
    y = ssd_chunked_scan(xs * dt[..., None].astype(xs.dtype), dt * a, bm, cm)
    y = y + xs * d_skip[:, None]
    y = y.reshape(b, l, D_INNER) * jax.nn.silu(z)
    y = rms_norm(y.reshape(b, l, SSD_GROUPS, D_INNER // SSD_GROUPS),
                 norm_g.reshape(SSD_GROUPS, D_INNER // SSD_GROUPS))
    return y.reshape(b, l, D_INNER)

def blocked_causal_attention(q, k, v):
    b, l, h, dk = q.shape
    scale = dk ** -0.5
    key_pos = jnp.arange(l)

    def one_block(i):
        start = i * ATTN_Q_BLOCK
        qb = lax.dynamic_slice_in_dim(q, start, ATTN_Q_BLOCK, axis=1)
        s = jnp.einsum('bqhd,bkhd->bhqk', qb, k).astype(jnp.float32) * scale
        qpos = start + jnp.arange(ATTN_Q_BLOCK)
        s = jnp.where(qpos[:, None] >= key_pos[None, :], s, -jnp.inf)
        p = jax.nn.softmax(s, axis=-1).astype(v.dtype)
        return jnp.einsum('bhqk,bkhd->bqhd', p, v)

    out = lax.map(one_block, jnp.arange(l // ATTN_Q_BLOCK))
    return jnp.moveaxis(out, 0, 1).reshape(b, l, h * v.shape[-1])

def mla_mixer(q_a, kv_a, k_rope_raw, q_a_norm_g, w_uq, kv_a_norm_g, w_ukv, q_norm_g, k_norm_g, cos, sin):
    b, l, _ = q_a.shape
    q = (rms_norm(q_a, q_a_norm_g) @ w_uq).reshape(b, l, MLA_HEADS, MLA_QK_DIM)
    kv = (rms_norm(kv_a, kv_a_norm_g) @ w_ukv).reshape(b, l, MLA_HEADS, MLA_NOPE + MLA_V_DIM)
    k_nope, v = jnp.split(kv, [MLA_NOPE], axis=-1)
    k_rope = jnp.broadcast_to(k_rope_raw[:, :, None, :], (b, l, MLA_HEADS, MLA_ROPE))
    k = jnp.concatenate([k_nope, k_rope], axis=-1)
    q = rms_norm(q, q_norm_g)
    k = rms_norm(k, k_norm_g)
    q = jnp.concatenate([q[..., :MLA_NOPE], apply_rope(q[..., MLA_NOPE:], cos, sin)], axis=-1)
    k = jnp.concatenate([k[..., :MLA_NOPE], apply_rope(k[..., MLA_NOPE:], cos, sin)], axis=-1)
    return blocked_causal_attention(q, k, v)

def first_inputs(seed: int = 0) -> dict:
    key = jax.random.key(seed)
    ks = jax.random.split(key, 24)
    f32 = jnp.float32

    def dense(k, shape, fan_in):
        return jax.random.normal(k, (DEPTH,) + shape, f32) * fan_in ** -0.5

    def gain(k, n):
        return 1.0 + 0.02 * jax.random.normal(k, (DEPTH, n), f32)

    def bias(k, n):
        return 0.02 * jax.random.normal(k, (DEPTH, n), f32)

    dt0 = jnp.exp(jax.random.uniform(ks[5], (DEPTH, SSD_HEADS), f32, np.log(1e-3), np.log(1e-1)))
    return {
        "x": jax.random.normal(ks[0], (BATCH, SEQ, D_MODEL), f32),
        "norm_mix_g": gain(ks[1], D_MODEL),
        "w_in": dense(ks[2], (D_MODEL, IN_COLS), D_MODEL),
        "conv_ssd_w": dense(ks[3], (SSD_CONV, SSD_CONV_DIM), SSD_CONV),
        "conv_ssd_b": bias(ks[4], SSD_CONV_DIM),
        "dt_bias": dt0 + jnp.log(-jnp.expm1(-dt0)),
        "a_log": jnp.log(jax.random.uniform(ks[6], (DEPTH, SSD_HEADS), f32, 1.0, 16.0)),
        "d_skip": 1.0 + 0.1 * jax.random.normal(ks[7], (DEPTH, SSD_HEADS), f32),
        "ssd_norm_g": gain(ks[8], D_INNER),
        "w_ssd_proj": dense(ks[9], (D_INNER, D_MODEL), D_INNER),
        "q_a_norm_g": gain(ks[10], MLA_Q_LORA),
        "w_uq": dense(ks[11], (MLA_Q_LORA, MLA_HEADS * MLA_QK_DIM), MLA_Q_LORA),
        "kv_a_norm_g": gain(ks[12], MLA_KV_LORA),
        "w_ukv": dense(ks[13], (MLA_KV_LORA, MLA_HEADS * (MLA_NOPE + MLA_V_DIM)), MLA_KV_LORA),
        "q_norm_g": gain(ks[14], MLA_QK_DIM),
        "k_norm_g": gain(ks[15], MLA_QK_DIM),
        "w_mla_proj": dense(ks[16], (MLA_WIDTH, D_MODEL), MLA_WIDTH),
        "gate_b": bias(ks[17], 2 * D_MODEL),
        "w_o": dense(ks[18], (D_MODEL, D_MODEL), D_MODEL),
        "norm_ffn_g": gain(ks[19], D_MODEL),
        "w_up": dense(ks[20], (D_MODEL, 2 * D_FF), D_MODEL),
        "conv_ffn_w": dense(ks[21], (FFN_CONV, 2 * D_FF), FFN_CONV),
        "conv_ffn_b": bias(ks[22], 2 * D_FF),
        "w_down": dense(ks[23], (D_FF, D_MODEL), D_FF),
    }

def first_block(x, norm_mix_g, w_in, conv_ssd_w, conv_ssd_b, dt_bias, a_log, d_skip, ssd_norm_g,
              w_ssd_proj, q_a_norm_g, w_uq, kv_a_norm_g, w_ukv, q_norm_g, k_norm_g, w_mla_proj,
              gate_b, w_o, norm_ffn_g, w_up, conv_ffn_w, conv_ffn_b, w_down):
    cos, sin = rope_tables(x.shape[1], MLA_ROPE)
    for i in range(DEPTH):
        h = rms_norm(x, norm_mix_g[i])
        proj = h @ w_in[i]
        z, xbc, dt_raw, q_a, kv_a, k_rope_raw, gates = jnp.split(
            proj, [OFF_Z, OFF_XBC, OFF_DT, OFF_QA, OFF_KVA, OFF_KR], axis=-1)
        y_ssd = ssd_mixer(z, xbc, dt_raw, conv_ssd_w[i], conv_ssd_b[i], dt_bias[i], a_log[i],
                          d_skip[i], ssd_norm_g[i]) @ w_ssd_proj[i]
        y_mla = mla_mixer(q_a, kv_a, k_rope_raw, q_a_norm_g[i], w_uq[i], kv_a_norm_g[i], w_ukv[i],
                          q_norm_g[i], k_norm_g[i], cos, sin) @ w_mla_proj[i]
        g_ssd, g_mla = jnp.split(jax.nn.sigmoid(gates + gate_b[i]), 2, axis=-1)
        x = x + (g_ssd * y_ssd + g_mla * y_mla) @ w_o[i]
        h = rms_norm(x, norm_ffn_g[i])
        u = causal_depthwise_conv(h @ w_up[i], conv_ffn_w[i], conv_ffn_b[i])
        u_gate, u_val = jnp.split(u, 2, axis=-1)
        x = x + (jax.nn.silu(u_gate) * u_val) @ w_down[i]
    return x


HEAD_DIM = 64
NEG = -1e30
NSA_HEADS = 12
NSA_KV_GROUPS = 3
NSA_HPG = NSA_HEADS // NSA_KV_GROUPS
CMP_BLOCK = 32
CMP_STRIDE = 16
CMP_HIDDEN = 256
SLC_BLOCK = 64
SLC_TOPK = 16
WIN_SIZE = 512
SLC_Q_BLOCK = 64
WIN_Q_BLOCK = 128
DIL_PAIRS = ((128, 1), (512, 4), (2048, 16))
DIL_GROUPS = len(DIL_PAIRS)
DIL_HPG = 4
DIL_HEADS = DIL_GROUPS * DIL_HPG
DIL_NKEYS = max(w // d + 1 for w, d in DIL_PAIRS)
DIL_Q_BLOCK = 128
D_FF_2 = 4 * D_MODEL
Q_A_COLS = NSA_HEADS * HEAD_DIM
KV_A_COLS = NSA_KV_GROUPS * HEAD_DIM
GATE_A_COLS = 3 * NSA_HEADS
QKV_B_COLS = DIL_HEADS * HEAD_DIM
IN_SIZES = (Q_A_COLS, KV_A_COLS, KV_A_COLS, KV_A_COLS, KV_A_COLS, KV_A_COLS, KV_A_COLS,
            GATE_A_COLS, QKV_B_COLS, QKV_B_COLS, QKV_B_COLS, D_MODEL, D_MODEL)
IN_COLS_2 = sum(IN_SIZES)
SPLIT_POINTS = tuple(int(c) for c in np.cumsum(IN_SIZES)[:-1])


def _rmsnorm(x, g):
    xf = x.astype(jnp.float32)
    y = xf * lax.rsqrt(jnp.mean(xf * xf, axis=-1, keepdims=True) + NORM_EPS)
    return (y * g.astype(jnp.float32)).astype(x.dtype)

def _rope(x, pos):
    half = HEAD_DIM // 2
    inv_freq = jnp.power(ROPE_THETA, -jnp.arange(half, dtype=jnp.float32) / half)
    ang = jnp.asarray(pos, jnp.float32)[:, None] * inv_freq[None, :]
    shape = (1, ang.shape[0]) + (1,) * (x.ndim - 3) + (half,)
    cos = jnp.cos(ang).reshape(shape)
    sin = jnp.sin(ang).reshape(shape)
    xf = x.astype(jnp.float32)
    x1, x2 = xf[..., :half], xf[..., half:]
    return jnp.concatenate([x1 * cos - x2 * sin, x2 * cos + x1 * sin], axis=-1).astype(x.dtype)

def _masked_softmax(s, mask):
    s = jnp.where(mask, s.astype(jnp.float32), NEG)
    return jax.nn.softmax(s, axis=-1) * mask

def _compress(kv, pos_emb, w1, w2):
    B, S, G, dh = kv.shape
    n_cmp = (S - CMP_BLOCK) // CMP_STRIDE + 1
    idx = np.arange(n_cmp)[:, None] * CMP_STRIDE + np.arange(CMP_BLOCK)[None, :]
    blocks = kv[:, idx] + pos_emb[None, None, :, None, :]
    blocks = jnp.transpose(blocks, (0, 1, 3, 2, 4)).reshape(B, n_cmp, G, CMP_BLOCK * dh)
    return jax.nn.gelu(blocks @ w1) @ w2

def _cmp_to_slc_overlap(n_cmp, n_slc):
    cs = np.arange(n_cmp)[:, None] * CMP_STRIDE
    ss = np.arange(n_slc)[None, :] * SLC_BLOCK
    ov = np.minimum(cs + CMP_BLOCK, ss + SLC_BLOCK) - np.maximum(cs, ss)
    return (np.clip(ov, 0, None) / CMP_BLOCK).astype(np.float32)

def _nsa_mixer(q, k_cmp, v_cmp, k_slc, v_slc, k_win, v_win, gate,
               k_norm_cmp, cmp_k_pos, cmp_k_w1, cmp_k_w2, cmp_v_pos, cmp_v_w1, cmp_v_w2):
    B, S = q.shape[0], q.shape[1]
    G, R, dh = NSA_KV_GROUPS, NSA_HPG, HEAD_DIM
    scale = dh ** -0.5
    t = np.arange(S)

    kc = _compress(k_cmp, cmp_k_pos, cmp_k_w1, cmp_k_w2)
    vc = _compress(v_cmp, cmp_v_pos, cmp_v_w1, cmp_v_w2)
    n_cmp = kc.shape[1]
    c_end = np.arange(n_cmp) * CMP_STRIDE + CMP_BLOCK - 1
    kc = _rope(_rmsnorm(kc, k_norm_cmp), c_end)
    s_cmp = jnp.einsum("bsgrd,bcgd->bgrsc", q, kc) * scale
    p_cmp = _masked_softmax(s_cmp, c_end[None, :] <= t[:, None])
    o_cmp = jnp.einsum("bgrsc,bcgd->bsgrd", p_cmp.astype(vc.dtype), vc)

    n_slc = S // SLC_BLOCK
    top_n = min(SLC_TOPK, n_slc)
    overlap = jnp.asarray(_cmp_to_slc_overlap(n_cmp, n_slc))
    imp = jnp.einsum("bgrsc,cn->bgsn", p_cmp, overlap)
    blk = np.arange(n_slc)[None, :]
    cur = (t // SLC_BLOCK)[:, None]
    forced = (blk == 0) | (blk == cur) | (blk == cur - 1)
    score = jnp.where(forced, jnp.inf, jnp.where(blk <= cur, imp, -jnp.inf))
    top_score, top_idx = lax.top_k(score, top_n)
    top_ok = top_score > -jnp.inf

    kb = jnp.transpose(k_slc.reshape(B, n_slc, SLC_BLOCK, G, dh), (0, 3, 1, 2, 4))
    vb = jnp.transpose(v_slc.reshape(B, n_slc, SLC_BLOCK, G, dh), (0, 3, 1, 2, 4))
    gather_blocks = jax.vmap(jax.vmap(lambda kk, ii: kk[ii]))
    nqs = S // SLC_Q_BLOCK

    def slc_block(xs):
        qc, idx, ok, tq = xs
        ks = gather_blocks(kb, idx)
        vs = gather_blocks(vb, idx)
        s = jnp.einsum("bqgrd,bgqnkd->bgrqnk", qc, ks) * scale
        kpos = idx[..., None] * SLC_BLOCK + np.arange(SLC_BLOCK)
        mask = ok[..., None] & (kpos <= tq[:, None, None])
        s = s.reshape(B, G, R, SLC_Q_BLOCK, top_n * SLC_BLOCK)
        mask = mask.reshape(B, G, 1, SLC_Q_BLOCK, top_n * SLC_BLOCK)
        p = _masked_softmax(s, mask)
        vs = vs.reshape(B, G, SLC_Q_BLOCK, top_n * SLC_BLOCK, dh)
        return jnp.einsum("bgrqj,bgqjd->bqgrd", p.astype(vs.dtype), vs)

    qs = jnp.moveaxis(q.reshape(B, nqs, SLC_Q_BLOCK, G, R, dh), 1, 0)
    idx_s = jnp.moveaxis(top_idx.reshape(B, G, nqs, SLC_Q_BLOCK, top_n), 2, 0)
    ok_s = jnp.moveaxis(top_ok.reshape(B, G, nqs, SLC_Q_BLOCK, top_n), 2, 0)
    tq_s = jnp.arange(S, dtype=jnp.int32).reshape(nqs, SLC_Q_BLOCK)
    o_slc = lax.map(slc_block, (qs, idx_s, ok_s, tq_s))
    o_slc = jnp.moveaxis(o_slc, 0, 1).reshape(B, S, G, R, dh)

    span = WIN_SIZE + WIN_Q_BLOCK
    kw_pad = jnp.pad(k_win, ((0, 0), (WIN_SIZE, 0), (0, 0), (0, 0)))
    vw_pad = jnp.pad(v_win, ((0, 0), (WIN_SIZE, 0), (0, 0), (0, 0)))
    nqw = S // WIN_Q_BLOCK

    def win_block(xs):
        qc, start = xs
        ks = lax.dynamic_slice_in_dim(kw_pad, start, span, axis=1)
        vs = lax.dynamic_slice_in_dim(vw_pad, start, span, axis=1)
        s = jnp.einsum("bqgrd,bkgd->bgrqk", qc, ks) * scale
        tq = start + jnp.arange(WIN_Q_BLOCK)
        kp = start - WIN_SIZE + jnp.arange(span)
        diff = tq[:, None] - kp[None, :]
        mask = (diff >= 0) & (diff < WIN_SIZE) & (kp[None, :] >= 0)
        p = _masked_softmax(s, mask)
        return jnp.einsum("bgrqk,bkgd->bqgrd", p.astype(vs.dtype), vs)

    qw = jnp.moveaxis(q.reshape(B, nqw, WIN_Q_BLOCK, G, R, dh), 1, 0)
    starts = jnp.arange(nqw, dtype=jnp.int32) * WIN_Q_BLOCK
    o_win = lax.map(win_block, (qw, starts))
    o_win = jnp.moveaxis(o_win, 0, 1).reshape(B, S, G, R, dh)

    y = gate[..., 0:1] * o_cmp + gate[..., 1:2] * o_slc + gate[..., 2:3] * o_win
    return y.reshape(B, S, G * R * dh)

def _dilated_mixer(q, k, v):
    B, S = q.shape[0], q.shape[1]
    dh = HEAD_DIM
    scale = dh ** -0.5
    dil = np.array([d for _, d in DIL_PAIRS])
    win = np.array([w for w, _ in DIL_PAIRS])
    j = np.arange(DIL_NKEYS)
    in_window = (j[None, :] * dil[:, None]) <= win[:, None]
    kg = jnp.transpose(k, (2, 0, 1, 3, 4))
    vg = jnp.transpose(v, (2, 0, 1, 3, 4))
    gather_stride = jax.vmap(lambda kk, ii: kk[:, ii])
    nq = S // DIL_Q_BLOCK

    def dil_block(xs):
        qc, tq = xs
        kpos = tq[None, :, None] - j[None, None, :] * dil[:, None, None]
        mask = (kpos >= 0) & in_window[:, None, :]
        idx = jnp.maximum(kpos, 0)
        ks = gather_stride(kg, idx)
        vs = gather_stride(vg, idx)
        s = jnp.einsum("gbqhd,gbqjhd->gbhqj", qc, ks).astype(jnp.float32) * scale
        s = jnp.where(mask[:, None, None], s, NEG)
        m = jnp.max(s, axis=-1, keepdims=True)
        e = jnp.exp(s - m)
        den = jnp.sum(e, axis=-1, keepdims=True)
        o = jnp.einsum("gbhqj,gbqjhd->gbqhd", (e / den).astype(vs.dtype), vs)
        lse = (m + jnp.log(den))[..., 0]
        w = jax.nn.softmax(lse, axis=0)
        return jnp.einsum("gbhq,gbqhd->bqhd", w.astype(o.dtype), o)

    qd = jnp.moveaxis(jnp.transpose(q, (2, 0, 1, 3, 4)).reshape(DIL_GROUPS, B, nq, DIL_Q_BLOCK, DIL_HPG, dh), 2, 0)
    tq_d = jnp.arange(S, dtype=jnp.int32).reshape(nq, DIL_Q_BLOCK)
    o = lax.map(dil_block, (qd, tq_d))
    return jnp.moveaxis(o, 0, 1).reshape(B, S, DIL_HPG * dh)

def second_inputs(seed: int = 0) -> dict:
    key = jax.random.key(seed)
    ks = jax.random.split(key, 21)
    L = DEPTH

    def nrm(k, shape, scale):
        return scale * jax.random.normal(k, shape, jnp.float32)

    def gain(k, n):
        return 1.0 + 0.02 * jax.random.normal(k, (L, n), jnp.float32)

    return {
        "x": jax.random.normal(ks[0], (BATCH, SEQ, D_MODEL), jnp.float32),
        "norm1_g": gain(ks[1], D_MODEL),
        "w_in": nrm(ks[2], (L, D_MODEL, IN_COLS_2), D_MODEL ** -0.5),
        "q_norm_a": gain(ks[3], HEAD_DIM),
        "k_norm_cmp": gain(ks[4], HEAD_DIM),
        "k_norm_slc": gain(ks[5], HEAD_DIM),
        "k_norm_win": gain(ks[6], HEAD_DIM),
        "cmp_k_pos": nrm(ks[7], (L, CMP_BLOCK, HEAD_DIM), 0.2),
        "cmp_k_w1": nrm(ks[8], (L, CMP_BLOCK * HEAD_DIM, CMP_HIDDEN), (CMP_BLOCK * HEAD_DIM) ** -0.5),
        "cmp_k_w2": nrm(ks[9], (L, CMP_HIDDEN, HEAD_DIM), CMP_HIDDEN ** -0.5),
        "cmp_v_pos": nrm(ks[10], (L, CMP_BLOCK, HEAD_DIM), 0.2),
        "cmp_v_w1": nrm(ks[11], (L, CMP_BLOCK * HEAD_DIM, CMP_HIDDEN), (CMP_BLOCK * HEAD_DIM) ** -0.5),
        "cmp_v_w2": nrm(ks[12], (L, CMP_HIDDEN, HEAD_DIM), CMP_HIDDEN ** -0.5),
        "q_norm_b": gain(ks[13], HEAD_DIM),
        "k_norm_b": gain(ks[14], HEAD_DIM),
        "w_o_a": nrm(ks[15], (L, Q_A_COLS, D_MODEL), Q_A_COLS ** -0.5),
        "w_o_b": nrm(ks[16], (L, DIL_HPG * HEAD_DIM, D_MODEL), (DIL_HPG * HEAD_DIM) ** -0.5),
        "w_out": nrm(ks[17], (L, D_MODEL, D_MODEL), D_MODEL ** -0.5),
        "norm2_g": gain(ks[18], D_MODEL),
        "w_up": nrm(ks[19], (L, D_MODEL, D_FF_2), D_MODEL ** -0.5),
        "w_down": nrm(ks[20], (L, D_FF_2, D_MODEL), D_FF_2 ** -0.5),
    }

def second_block(x, norm1_g, w_in, q_norm_a, k_norm_cmp, k_norm_slc, k_norm_win,
              cmp_k_pos, cmp_k_w1, cmp_k_w2, cmp_v_pos, cmp_v_w1, cmp_v_w2,
              q_norm_b, k_norm_b, w_o_a, w_o_b, w_out, norm2_g, w_up, w_down):
    B, S = x.shape[0], x.shape[1]
    G, R, dh = NSA_KV_GROUPS, NSA_HPG, HEAD_DIM
    pos = np.arange(S)
    for i in range(DEPTH):
        h = _rmsnorm(x, norm1_g[i])
        proj = h @ w_in[i]
        (q_a, k_c, v_c, k_s, v_s, k_w, v_w, g_nsa,
         q_b, k_b, v_b, g_ma, g_mb) = jnp.split(proj, SPLIT_POINTS, axis=-1)

        q_a = _rope(_rmsnorm(q_a.reshape(B, S, NSA_HEADS, dh), q_norm_a[i]), pos).reshape(B, S, G, R, dh)
        k_c = k_c.reshape(B, S, G, dh)
        v_c = v_c.reshape(B, S, G, dh)
        k_s = _rope(_rmsnorm(k_s.reshape(B, S, G, dh), k_norm_slc[i]), pos)
        v_s = v_s.reshape(B, S, G, dh)
        k_w = _rope(_rmsnorm(k_w.reshape(B, S, G, dh), k_norm_win[i]), pos)
        v_w = v_w.reshape(B, S, G, dh)
        g_nsa = jax.nn.sigmoid(g_nsa).reshape(B, S, G, R, 3)
        y_a = _nsa_mixer(q_a, k_c, v_c, k_s, v_s, k_w, v_w, g_nsa,
                         k_norm_cmp[i], cmp_k_pos[i], cmp_k_w1[i], cmp_k_w2[i],
                         cmp_v_pos[i], cmp_v_w1[i], cmp_v_w2[i])

        q_b = _rope(_rmsnorm(q_b.reshape(B, S, DIL_HEADS, dh), q_norm_b[i]), pos)
        k_b = _rope(_rmsnorm(k_b.reshape(B, S, DIL_HEADS, dh), k_norm_b[i]), pos)
        y_b = _dilated_mixer(q_b.reshape(B, S, DIL_GROUPS, DIL_HPG, dh),
                             k_b.reshape(B, S, DIL_GROUPS, DIL_HPG, dh),
                             v_b.reshape(B, S, DIL_GROUPS, DIL_HPG, dh))

        mixed = jax.nn.sigmoid(g_ma) * (y_a @ w_o_a[i]) + jax.nn.sigmoid(g_mb) * (y_b @ w_o_b[i])
        x = x + mixed @ w_out[i]

        h2 = _rmsnorm(x, norm2_g[i])
        x = x + jnp.square(jax.nn.relu(h2 @ w_up[i])) @ w_down[i]
    return x


def setup_inputs(seed=0):
    out = dict(first_inputs(seed))
    for name, value in second_inputs(seed + 1).items():
        if name != "x":
            out[name + "_2"] = value
    return out


def reference(
    x, norm_mix_g, w_in, conv_ssd_w, conv_ssd_b, dt_bias, a_log, d_skip, ssd_norm_g, w_ssd_proj,
    q_a_norm_g, w_uq, kv_a_norm_g, w_ukv, q_norm_g, k_norm_g, w_mla_proj, gate_b, w_o,
    norm_ffn_g, w_up, conv_ffn_w, conv_ffn_b, w_down, norm1_g_2, w_in_2, q_norm_a_2,
    k_norm_cmp_2, k_norm_slc_2, k_norm_win_2, cmp_k_pos_2, cmp_k_w1_2, cmp_k_w2_2, cmp_v_pos_2,
    cmp_v_w1_2, cmp_v_w2_2, q_norm_b_2, k_norm_b_2, w_o_a_2, w_o_b_2, w_out_2, norm2_g_2,
    w_up_2, w_down_2,
):
    x = first_block(
        x, norm_mix_g, w_in, conv_ssd_w, conv_ssd_b, dt_bias, a_log, d_skip, ssd_norm_g,
        w_ssd_proj, q_a_norm_g, w_uq, kv_a_norm_g, w_ukv, q_norm_g, k_norm_g, w_mla_proj,
        gate_b, w_o, norm_ffn_g, w_up, conv_ffn_w, conv_ffn_b, w_down,
    )
    return second_block(
        x, norm1_g_2, w_in_2, q_norm_a_2, k_norm_cmp_2, k_norm_slc_2, k_norm_win_2, cmp_k_pos_2,
        cmp_k_w1_2, cmp_k_w2_2, cmp_v_pos_2, cmp_v_w1_2, cmp_v_w2_2, q_norm_b_2, k_norm_b_2,
        w_o_a_2, w_o_b_2, w_out_2, norm2_g_2, w_up_2, w_down_2,
    )


_drawn_inputs = setup_inputs


def setup_inputs(seed=0):
    import zlib

    import numpy as np

    out = dict(_drawn_inputs(seed))
    spreads = {}
    factors = {'norm_mix_g': 2.873,
     'conv_ssd_b': 3.523,
     'ssd_norm_g': 4.988,
     'q_a_norm_g': 8.0,
     'kv_a_norm_g': 8.0,
     'q_norm_g': 8.0,
     'k_norm_g': 8.0,
     'gate_b': 8.0,
     'norm_ffn_g': 3.823,
     'conv_ffn_b': 3.987,
     'norm1_g_2': 8.0,
     'q_norm_a_2': 8.0,
     'k_norm_cmp_2': 33.671,
     'k_norm_slc_2': 8.0,
     'k_norm_win_2': 8.0,
     'cmp_k_pos_2': 7.266,
     'q_norm_b_2': 8.0,
     'k_norm_b_2': 8.0,
     'norm2_g_2': 11.682,
     'd_skip': 3.253,
     'cmp_v_pos_2': 8.0}
    for name, (base, spread) in spreads.items():
        noise = np.random.default_rng([zlib.crc32(name.encode()), seed]).standard_normal(out[name].shape)
        drawn = base * np.exp(spread * noise) if base else spread * noise
        out[name] = __import__('jax').numpy.asarray(drawn.astype(out[name].dtype))
    for name, factor in factors.items():
        out[name] = (out[name] * factor).astype(out[name].dtype)
    return out
```

```python
from contextlib import ExitStack

import concourse.bass as bass
import numpy as np
from concourse import mybir

F32 = mybir.dt.float32
F32R = mybir.dt.float32r
ALU = mybir.AluOpType
ACT = mybir.ActivationFunctionType
AX_X = mybir.AxisListType.X

P = 128
T = 256
TT = T // P
D = 1024
KD = D // P
EPS = 1e-6
NEG = -1e30

DI, NH_SSD, HD_SSD, NG_SSD, NS = 2048, 32, 64, 4, 128
XBC = DI + 2 * NG_SSD * NS
QL, KVL, H_MLA, NOPE, ROPE, VD = 256, 128, 16, 64, 32, 64
QK = NOPE + ROPE
FF = 2816
OFF_XBC, OFF_DT = DI, DI + XBC
OFF_QA = OFF_DT + NH_SSD
OFF_KVA = OFF_QA + QL
OFF_KR = OFF_KVA + KVL
OFF_G = OFF_KR + ROPE

H_NSA, G_NSA, HPG, HD = 12, 3, 4, 64
NC = 15
CG = 16
H_DIL, DG, DH = 12, 3, 4
FF2 = 4096
DIL = ((128, 1), (512, 4), (2048, 16))

SLOT = 2048
RAW_SLOTS, SPLIT_SLOTS = 4, 2
BW = 384

_SIZES = [("A", 1, 1536), ("QA", 1, 2048), ("XBC", 12, 2048), ("Z", 8, 2048), ("GATE_A", 1, 2048),
          ("UQ", 2, 1536), ("UKV", 1, 2048), ("GATE_B", 7, 2048), ("SSDP", 8, 2048), ("MLAP", 4, 2048), ("WO", 4, 2048), ("UP", 22, 2048),
          ("DOWN", 16, 1408), ("CKV", 2, 2048), ("TM_A", 6, 2048), ("TM_G", 1, 512), ("CW1", 4, 2048),
          ("TM_B", 9, 2048), ("GATE2", 8, 2048),
          ("OAB", 4, 2048), ("WOUT", 4, 2048), ("UP2", 16, 2048), ("DOWN2", 16, 2048)]
SEC = {}
_c = 0
for _name, _n, _used in _SIZES:
    SEC[_name] = (_c, _n, _used)
    _c += _n
NCHUNK = _c


def _rows(w, kt):
    return w.reshape(kt, P, -1).transpose(1, 0, 2)


def _chunks(w, kt, cols):
    r = _rows(w, kt)
    n = r.shape[2] // cols
    return r.reshape(P, kt, n, cols).transpose(2, 0, 1, 3).reshape(n, P, kt * cols)


def pack_stream(a):
    w1, w2 = a["w_in"][0], a["w_in_2"][0]
    out = np.zeros((NCHUNK, P, SLOT), np.float32)

    def put(sec, part, at=0):
        c0 = SEC[sec][0] + at
        out[c0:c0 + part.shape[0], :, :part.shape[2]] = part

    first = np.concatenate([w1[:, OFF_DT:OFF_QA], w1[:, OFF_KR:OFF_G], w1[:, OFF_KVA:OFF_KR]], axis=1)
    put("A", _chunks(first, KD, 192))
    put("QA", _chunks(w1[:, OFF_QA:OFF_KVA], KD, 256))
    put("XBC", _chunks(w1[:, OFF_XBC:OFF_DT], KD, 256))
    put("Z", _chunks(w1[:, :DI], KD, 256))
    put("UQ", _chunks(a["w_uq"][0], 2, 768))
    put("UKV", _chunks(a["w_ukv"][0], 1, 2048))
    gates = _chunks(w1[:, OFF_G:], KD, 256)
    put("GATE_A", gates[:1])
    put("GATE_B", gates[1:])
    put("SSDP", _chunks(a["w_ssd_proj"][0], 16, 128))
    put("MLAP", _chunks(a["w_mla_proj"][0], KD, 256))
    put("WO", _chunks(a["w_o"][0], KD, 256))
    up = a["w_up"][0].reshape(D, 2, FF // P, P).transpose(0, 2, 1, 3).reshape(D, 2 * FF)
    put("UP", _chunks(up, KD, 256))
    dn = _rows(a["w_down"][0], 22).reshape(P, 2, 11, KD, P).transpose(3, 1, 0, 2, 4).reshape(16, P, 11 * P)
    put("DOWN", dn)
    put("CKV", _chunks(w2[:, 768:1024], KD, 256))
    put("CKV", _chunks(w2[:, 1024:1152], KD, 128), 1)
    put("CW1", _chunks(a["cmp_k_w1_2"][0], 16, 128))
    put("CW1", _chunks(a["cmp_v_w1_2"][0], 16, 128), 2)
    tm = np.concatenate([w2[:, 0:768], w2[:, 1152:1344], w2[:, 1536:1728], w2[:, 1344:1536], w2[:, 1728:1920],
                         w2[:, 1956:4260]], axis=1)
    tm = _chunks(tm, KD, 256)
    put("TM_A", tm[:6])
    put("TM_B", tm[6:])
    g = np.zeros((D, 64), np.float32)
    g[:, :36] = w2[:, 1920:1956]
    put("TM_G", _chunks(g, KD, 64))
    put("GATE2", _chunks(w2[:, 4260:], KD, 256))
    put("OAB", _chunks(np.concatenate([a["w_o_a_2"][0], a["w_o_b_2"][0]], axis=0), KD, 256))
    put("WOUT", _chunks(a["w_out_2"][0], KD, 256))
    put("UP2", _chunks(a["w_up_2"][0], KD, 256))
    dn = _rows(a["w_down_2"][0], 32).reshape(P, 2, 16, KD, P).transpose(3, 1, 0, 2, 4).reshape(16, P, 16 * P)
    put("DOWN2", dn)
    return out


def _col(v, tiles):
    return v.reshape(tiles, P).T


def _bc(v):
    return np.broadcast_to(v.reshape(1, -1), (P, v.size))


def _tables(dim, pos, power=False):
    inv = np.float32(1.0) / (np.float32(10000.0) ** (np.arange(0, dim, 2, dtype=np.float32) / np.float32(dim)))
    if power:
        inv = np.power(np.float32(10000.0), -np.arange(dim // 2, dtype=np.float32) / np.float32(dim // 2))
    ang = np.asarray(pos, np.float32)[:, None] * inv[None, :].astype(np.float32)
    return np.cos(ang).astype(np.float32), np.sin(ang).astype(np.float32)


def _tok(t):
    return t.reshape(TT, P, -1).transpose(1, 0, 2).reshape(P, -1)


def _blocks(m):
    return np.concatenate([m[:P, :P], m[P:, :]], axis=1)


PA, PB = {}, {}


def pack_params(a):
    q, k = np.arange(T)[:, None], np.arange(T)[None, :]
    tri = (np.arange(P)[:, None] <= np.arange(P)[None, :]).astype(np.float32)
    one = np.ones((P, P), np.float32)
    c16, s16 = _tables(ROPE, np.arange(T))
    add = lambda ok: np.where(ok, 0.0, NEG).astype(np.float32)
    cw = a["conv_ssd_w"][0].reshape(4, 24, P).transpose(2, 1, 0).reshape(P, -1)
    fw = a["conv_ffn_w"][0].reshape(3, 2, 22, P).transpose(3, 2, 1, 0).reshape(P, -1)
    fb = a["conv_ffn_b"][0].reshape(2, 22, P).transpose(2, 1, 0).reshape(P, -1)
    ds = np.repeat(a["d_skip"][0], HD_SSD)
    early = [
        ("g_mix", _col(a["norm_mix_g"][0], KD)), ("ones", one), ("ident", np.eye(P, dtype=np.float32)),
        ("cw", cw), ("cb", _col(a["conv_ssd_b"][0], 24)), ("g_qa", _col(a["q_a_norm_g"][0], 2)),
        ("g_kva", _col(a["kv_a_norm_g"][0], 1)), ("dtb", _bc(a["dt_bias"][0])), ("alog", _bc(a["a_log"][0])),
        ("keep", np.concatenate([tri, one, tri], axis=1)), ("dskip", _col(ds, 16)),
        ("g_ssd", _col(a["ssd_norm_g"][0], 16)), ("gate_b", _col(a["gate_b"][0], 16)),
        ("g_q", _bc(a["q_norm_g"][0])), ("g_k", _bc(a["k_norm_g"][0])), ("cos16", _tok(c16)), ("sin16", _tok(s16)),
        ("causal", _blocks(add(k <= q))), ("g_ffn", _col(a["norm_ffn_g"][0], KD)), ("fw", fw), ("fb", fb),
        ("g1", _col(a["norm1_g_2"][0], KD)), ("g2", _col(a["norm2_g_2"][0], KD)),
    ]
    cend = np.arange(CG) * 16 + 31
    ok = (cend[None, :] <= np.arange(T)[:, None]) & (np.arange(CG)[None, :] < NC)
    c32, s32 = _tables(HD, np.arange(T), True)
    cc, sc = _tables(HD, cend, True)
    pad = lambda t: np.concatenate([t, np.zeros((P - CG, t.shape[1]), np.float32)], axis=0)
    pos = lambda v: v.reshape(16, 2 * HD).T
    late = [
        ("pos_k", pos(a["cmp_k_pos_2"][0])), ("pos_v", pos(a["cmp_v_pos_2"][0])),
        ("w2_k", _rows(a["cmp_k_w2_2"][0], 2).reshape(P, -1)), ("w2_v", _rows(a["cmp_v_w2_2"][0], 2).reshape(P, -1)),
        ("g_kc", _bc(a["k_norm_cmp_2"][0])), ("g_qa2", _bc(a["q_norm_a_2"][0])), ("g_k", _bc(np.concatenate(
            [np.tile(a["k_norm_slc_2"][0], 3), np.tile(a["k_norm_win_2"][0], 3)]))), ("g_qb", _bc(a["q_norm_b_2"][0])), ("g_kb", _bc(a["k_norm_b_2"][0])),
        ("cos32", _tok(c32)), ("sin32", _tok(s32)), ("cosc", pad(cc)), ("sinc", pad(sc)),
        ("cmp_add", _tok(add(ok))), ("cmp_any", _tok(ok.any(1, keepdims=True).astype(np.float32))),
        ("cmp_none", _tok((~ok.any(1, keepdims=True)).astype(np.float32))),
        ("dil", np.concatenate([_blocks(add((k <= q) & (q - k <= w) & ((q - k) % d == 0))) for w, d in DIL], axis=1)),
    ]
    packed = []
    for parts, where in ((early, PA), (late, PB)):
        at = 0
        for name, p in parts:
            where[name] = (at, p.shape[1])
            at += p.shape[1]
        packed.append(np.ascontiguousarray(np.concatenate([p for _, p in parts], axis=1), dtype=np.float32))
    return packed


NORMS = {"x": (8, 8, 2, 8), "qa": (2, 2, 2, 4), "kva": (1, 1, 1, 4), "y": (16, 4, 2, 4), "ffn": (8, 8, 2, 8),
         "x2": (8, 8, 2, 8), "ffn2": (8, 8, 2, 8)}
NORM_AT = {}
_p = _g = 0
for _name, (_t, _gw, _w, _s) in NORMS.items():
    NORM_AT[_name] = (_p, _g)
    _p += _t // _w
    _g += _t // _gw


def norm_groups(name):
    t, gw, _, _ = NORMS[name]
    return NORM_AT[name][1] + t // gw


def norm_end(name):
    t, _, w, _ = NORMS[name]
    return NORM_AT[name][0] + t // w


class Tally:

    def __init__(self, eng, sem):
        self.eng, self.sem, self.n = eng, sem, 0

    def sig(self, ins):
        ins.then_inc(self.sem, 1)
        self.n = self.n + 1

    def wait(self):
        self.eng.wait_ge(self.sem, self.n)

    def link(self, ins):
        self.sig(ins)
        self.wait()


FFN_LINKS = 6


def blocks_kernel(nc, wstream, x_t, params_a, params_b, out_t):
    with ExitStack() as ctx:
        def sem(name):
            return ctx.enter_context(nc.semaphore(name))

        cursor = [(nc.sbuf_base + 63) // 64 * 64]

        def fixed(name, shape, dt=F32):
            t = nc.alloc_sbuf_tensor_at(name, shape, dt, offset=cursor[0])
            cursor[0] += (int(np.prod(shape[1:])) * 4 + 31) // 32 * 32
            return t

        raw = fixed("raw", [P, RAW_SLOTS, SLOT])
        w_hi = fixed("w_hi", [P, SPLIT_SLOTS, SLOT], F32R)
        w_lo = fixed("w_lo", [P, SPLIT_SLOTS, SLOT], F32R)
        xT = fixed("xT", [P, KD, T])
        h_hi = fixed("h_hi", [P, KD, T], F32R)
        h_lo = fixed("h_lo", [P, KD, T], F32R)
        pa = fixed("pa", [P, params_a.shape[1]])
        rs = fixed("rs", [P, 4, T])
        small = cursor[0]
        expa = fixed("expa", [P, NH_SSD])
        a_tok = fixed("a_tok", [P, TT, NH_SSD])
        acum = fixed("acum", [P, TT, NH_SSD])
        krr = fixed("krr", [P, TT, ROPE])
        sskr = fixed("sskr", [P, TT])
        ssq = fixed("ssq", [P, 2, TT, H_MLA])
        rqk = fixed("rqk", [P, 2, TT, H_MLA])
        qsc = fixed("qsc", [P, 2, TT, H_MLA])
        mx = fixed("mx", [P, 2, 8])
        cwh = fixed("cwh", [P, 24, 5])
        fwh = fixed("fwh", [P, 44, 4])
        gbh = fixed("gbh", [P, 16])
        end_first, cursor[0] = cursor[0], small
        ss2 = fixed("ss2", [P, TT, 42])
        r2 = fixed("r2", [P, TT, 42])
        qs2 = fixed("qs2", [P, 2, TT, 42])
        m2 = fixed("m2", [P, 2, 4, 6])
        md = fixed("md", [P, 2, 2])
        ssc = fixed("ssc", [CG, 2, 3])
        vc = fixed("vc", [CG, 3, HD])
        kcT = fixed("kcT", [HD, 3, CG])
        cursor[0] = max(cursor[0], end_first)
        ARENA, LIMIT = cursor[0], nc.sbuf_usable_end

        def at(name, kib, shape, dt=F32):
            off = ARENA + int(kib * 1024)
            assert off + int(np.prod(shape[1:])) * 4 <= LIMIT, (name, off, LIMIT)
            return nc.alloc_sbuf_tensor_at(name, shape, dt, offset=off)

        def A(name):
            o, n = PA[name]
            return pa[:, o:o + n]

        xbcT = at("xbcT", 0, [P, 24, T])
        xdt = at("xdt", 24, [P, TT, DI])
        scM = at("scM", 40, [P, NG_SSD, BW])
        Rb = at("Rb", 46, [P, 2, 4, T])
        seg = at("seg", 54, [P, 4, BW])
        Mt = at("Mt", 60, [P, 2, 4, BW])
        ub = at("ub", 72, [P, 2, 2, T])
        zs = at("zs", 78, [P, 2, 2, T])
        cacc = at("cacc", 98, [P, 2, 2, T])
        qn_hi = at("qn_hi", 84, [P, 3, T], F32R)
        qn_lo = at("qn_lo", 87, [P, 3, T], F32R)
        qaT = at("qaT", 90, [P, 3, T])
        tb = at("tb", 93, [P, 2, 2, T])
        dtw = at("dtw", 76, [P, 8, 2 * NH_SSD])
        acumT = at("acumT", 97, [NH_SSD, T])
        kr = at("kr", 82, [P, TT, ROPE])
        krg = at("krg", 82.25, [P, TT, ROPE])
        krt = at("krt", 82.5, [P, 4, TT, ROPE // 2])
        ohi = at("ohi", 0, [P, 8, T], F32R)
        olo = at("olo", 8, [P, 8, T], F32R)
        vS = at("vS", 16, [P, TT, H_MLA, VD])
        y_hi = at("y_hi", 24, [P, 16, T], F32R)
        y_lo = at("y_lo", 40, [P, 16, T], F32R)
        k96 = at("k96", 56, [P, TT, H_MLA, QK])
        q96 = at("q96", 68, [P, TT, H_MLA, QK])
        sqt = at("sqt", 80, [P, 2, 384])
        qkT = at("qkT", 80, [P, 2, 2 * T])
        rot = at("rot", 84, [P, 2, TT, H_MLA, ROPE // 2])
        Sm = at("Sm", 84, [P, 2, BW])
        PTs = at("PTs", 87, [P, 2, BW])
        gT = at("gT", 90, [P, 16, T])
        mixa = at("mixa", 56, [P, KD, T])
        g_hi = at("g_hi", 0, [P, 22, T], F32R)
        g_lo = at("g_lo", 22, [P, 22, T], F32R)
        fub = at("fub", 80, [P, 2, 2, T])
        facc = at("facc", 84, [P, 2, 2, T])
        ftg = at("ftg", 88, [P, 2, T])
        fg = at("fg", 90, [P, 2, T])
        tm = at("tm", 0, [P, TT, 3840])
        gnsa = at("gnsa", 30, [P, TT, 3 * H_NSA])
        gT2 = at("gT2", 31, [P, 16, T])
        o2_hi = at("o2_hi", 47, [P, 8, T], F32R)
        o2_lo = at("o2_lo", 55, [P, 8, T], F32R)
        ckv = at("ckv", 63, [P, 3, T])
        cblk = at("cblk", 66, [P, 6, T])
        bT_hi = at("bT_hi", 72, [P, 2, 16, 3, CG], F32R)
        bT_lo = at("bT_lo", 78, [P, 2, 16, 3, CG], F32R)
        bT = at("bT", 84, [P, 2, 16, 3, CG])
        hid = at("hid", 84, [P, 3, 2, 2, 3 * CG])
        cn = at("cn", 86.25, [CG, 5, 3, HD])
        kswT = at("kswT", 63, [HD, 6, T])
        S2 = at("S2", 69, [P, 2, 1152])
        PT2 = at("PT2", 78, [P, 4, BW])
        qkT2 = at("qkT2", 84, [HD, 2, 2 * T])
        pcT = at("pcT", 88, [CG, 2, T])
        rt = at("rt", 90, [P, 2, TT, 4, HD // 2])
        sqt2 = at("sqt2", 92, [P, 2, TT * 4, HD])
        pb = at("pb", 96.5, [P, params_b.shape[1]])
        mix2 = at("mix2", 0, [P, KD, T])
        s_hi = at("s_hi", 0, [P, 32, T], F32R)
        s_lo = at("s_lo", 32, [P, 32, T], F32R)
        srl = at("srl", 80, [P, 2, 2, T])
        ssqr = at("ssqr", 84, [P, 2, 2, T])

        def Bp(name):
            o, n = PB[name]
            return pb[:, o:o + n]

        sqb = {"x": at("sq_x", 0, [P, 8, T]), "qa": at("sq_qa", 24, [P, 4, T]), "y": at("sq_y", 98, [P, 4, T]),
               "ffn": at("sq_ffn", 64, [P, 8, T]), "x2": at("sq_x2", 47, [P, 8, T]),
               "ffn2": at("sq_ffn2", 64, [P, 8, T])}
        hfb = {"x": at("hf_x", 8, [P, 8, T]), "qa": at("hf_qa", 28, [P, 4, T]), "y": at("hf_y", 102, [P, 4, T]),
               "ffn": at("hf_ffn", 72, [P, 8, T]), "x2": at("hf_x2", 55, [P, 8, T]),
               "ffn2": at("hf_ffn2", 72, [P, 8, T])}
        sqb["kva"], hfb["kva"] = sqb["qa"], hfb["qa"]
        NORM_IO = {"x": (xT, 0, "g_mix", h_hi, h_lo), "qa": (qaT, 0, "g_qa", qn_hi, qn_lo),
                   "kva": (qaT, 2, "g_kva", qn_hi, qn_lo), "y": (xbcT, 0, "g_ssd", y_hi, y_lo),
                   "ffn": (xT, 0, "g_ffn", h_hi, h_lo), "x2": (xT, 0, "g1", h_hi, h_lo),
                   "ffn2": (xT, 0, "g2", h_hi, h_lo)}

        banks = [ctx.enter_context(nc.psum_tensor(f"bank{i}", [P, 512], F32)) for i in range(8)]
        G = banks[0:2]
        B = banks[2:8]

        NORM_BANK = {"x": (0,), "qa": (0,), "kva": (1,), "y": (0, 1), "ffn": (0,), "x2": (0,), "ffn2": (0,)}

        scr = nc.dram_tensor("acum_rows", [NH_SSD, T], F32, kind="Internal").ap()

        landed = [sem(f"landed{r}") for r in range(RAW_SLOTS)]
        hi_done, lo_done, chunk_used, bank_free = sem("hi_done"), sem("lo_done"), sem("chunk_used"), sem("bank_free")
        x_in, pa_in = sem("x_in"), sem("pa_in")
        n_sq, n_sum, n_var, n_rs, n_f, n_hi, n_lo = (sem("norm_" + s) for s in
                                                     ("sq", "sum", "var", "root", "f", "hi", "lo"))
        act_own, dve_own = sem("act_own"), sem("dve_own")
        dtr_ready, sp_exp, sp_u, sp_ln = sem("dtr_ready"), sem("sp_exp"), sem("sp_u"), sem("sp_ln")
        a_ready, cum_ps, acumT_sb, rows_out = sem("a_ready"), sem("cum_ps"), sem("acumT_sb"), sem("rows_out")
        conv_u, conv_acc, conv_t, xbc_ready = sem("conv_u"), sem("conv_acc"), sem("conv_t"), sem("xbc_ready")
        xs_tr, xdt_ready = sem("xs_tr"), sem("xdt_ready")
        score_ps, score_sb = sem("score_ps"), sem("score_sb")
        rows_in = [sem("rows_in0"), sem("rows_in1")]
        seg_ready, decay_ready, m_ready, y_ps, y_ready = (sem("seg_ready"), sem("decay_ready"), sem("m_ready"),
                                                          sem("y_ps"), sem("y_ready"))
        z_t = sem("z_t")
        u_sq, kq_ss, kq_rs, kq_ready = sem("u_sq"), sem("kq_ss"), sem("kq_rs"), sem("kq_ready")
        qkT_ps, qkT_sb, s_ps, sm_ready, p_exp, p_ready = (sem("qkT_ps"), sem("qkT_sb"), sem("s_ps"), sem("sm_ready"),
                                                          sem("p_exp"), sem("p_ready"))
        pt_ps, pt_sb, o_ps, o_hi, o_lo = sem("pt_ps"), sem("pt_sb"), sem("o_ps"), sem("o_hi"), sem("o_lo")
        gate_t, mix_ready, mix_hi, mix_lo, x1_ready = (sem("gate_t"), sem("mix_ready"), sem("mix_hi"), sem("mix_lo"),
                                                       sem("x1_ready"))
        f_u, f_acc, f_t, f_g, f_hi, f_lo = (sem("f_u"), sem("f_acc"), sem("f_t"), sem("f_g"), sem("f_hi"),
                                            sem("f_lo"))
        pb_in, ckv_sb, cblk_in, b_ready, b_hi, b_lo = (sem("pb_in"), sem("ckv_sb"), sem("cblk_in"), sem("b_ready"),
                                                       sem("b_hi"), sem("b_lo"))
        t_sq, t_free, tm_done = sem("t_sq"), sem("t_free"), sem("tm_done")
        ge_in, ge_t, ge_done, c_ps, c_ss, c_rs, cn_ready, cT_ps, cT_sb = (
            sem("ge_in"), sem("ge_t"), sem("ge_done"), sem("c_ps"), sem("c_ss"), sem("c_rs"), sem("cn_ready"),
            sem("cT_ps"), sem("cT_sb"))
        ss_ready, rs_ready, k_ready, kT_ps, kT_sb = (sem("ss_ready"), sem("rs_ready"), sem("k_ready"), sem("kT_ps"),
                                                     sem("kT_sb"))
        nq_ps, nq_sb, ns_ps, nm_ready, n_exp, np_ready, npt_ps, npt_sb, no_ps, no_hi, no_lo = (
            sem("nsa_" + s) for s in ("qT_ps", "qT_sb", "s_ps", "max_ready", "exp", "p_ready", "pT_ps", "pT_sb",
                                      "o_ps", "o_hi", "o_lo"))
        dq_ps, dq_sb, ds_ps, dm_part, dm_ready, d_exp, dp_ready, dpt_ps, dpt_sb, do_ps, do_hi, do_lo = (
            sem("dil_" + s) for s in ("qkT_ps", "qkT_sb", "s_ps", "max_part", "max_ready", "exp", "p_ready", "pT_ps",
                                      "pT_sb", "o_ps", "o_hi", "o_lo"))
        mix2_ready, mix2_hi, mix2_lo, sq_relu, sq_f, sq_hi, sq_lo = (
            sem(s) for s in ("mix2_ready", "mix2_hi", "mix2_lo", "sq_relu", "sq_f", "sq_hi", "sq_lo"))
        u_ps, oab_ps, out_done = sem("u_ps"), sem("oab_ps"), sem("out_done")

        USES = [("A", 1), ("QA", 1), ("XBC", 12), ("Z", 8), ("GATE_A", 1), ("UQ", 8), ("UKV", 8), ("GATE_B", 7),
                ("SSDP", 8), ("MLAP", 4), ("WO", 4), ("UP", 22), ("DOWN", 8), ("CKV", 2), ("TM_A", 6), ("TM_G", 1),
                ("CW1", 4), ("TM_B", 9), ("GATE2", 8), ("OAB", 8), ("WOUT", 4), ("UP2", 16), ("DOWN2", 8)]
        use0, at_use = {}, 0
        for s, n in USES:
            use0[s] = at_use
            at_use += n

        block = ctx.enter_context(nc.Block())

        @block.sync
        def _(sp):
            def load(c, slot, used):
                if not isinstance(c, int) or c >= RAW_SLOTS:
                    sp.wait_ge(lo_done, c - RAW_SLOTS + 1)
                sp.dma_start(raw[:, slot, 0:used], wstream[c, :, 0:used]).then_inc(landed[slot], 16)

            for name, (c0, n, used) in SEC.items():
                loops = n // 4 if n >= 8 and c0 >= RAW_SLOTS else 0
                if loops:
                    with sp.Fori(0, loops, 1) as i:
                        for j in range(4):
                            load(i * 4 + (c0 + j), (c0 + j) % RAW_SLOTS, used)
                for c in range(c0 + 4 * loops, c0 + n):
                    load(c, c % RAW_SLOTS, used)
            sp.wait_ge(bank_free, at_use)
            sp.dma_start(out_t, xT[:, :, :]).then_inc(out_done, 16)
            sp.wait_ge(out_done, 16)

        @block.gpsimd
        def _(pool):
            def split_lo(c, raw_slot, slot, used):
                pool.wait_ge(hi_done, c + 1)
                nc.gpsimd.tensor_tensor(w_lo[:, slot, 0:used], raw[:, raw_slot, 0:used], w_hi[:, slot, 0:used],
                                        ALU.subtract).then_inc(lo_done, 1)

            for name, (c0, n, used) in SEC.items():
                loops = n // 4 if n >= 8 else 0
                if loops:
                    with pool.Fori(0, loops, 1) as i:
                        for j in range(4):
                            split_lo(i * 4 + (c0 + j), (c0 + j) % RAW_SLOTS, (c0 + j) % SPLIT_SLOTS, used)
                for c in range(c0 + 4 * loops, c0 + n):
                    split_lo(c, c % RAW_SLOTS, c % SPLIT_SLOTS, used)

        @block.tensor
        def _(pe):
            mm = nc.tensor.matmul

            def split_mm(out, w, x, kts, w_first, start=True, stop=True):
                last = None
                for n, (wp, xp) in enumerate(((0, 0), (1, 0), (0, 1))):
                    for kt in kts:
                        l, r = w(wp, kt), x(xp, kt)
                        if not w_first:
                            l, r = r, l
                        last = mm(out, l, r, start=start and n == 0 and kt == kts[0],
                                  stop=stop and n == 2 and kt == kts[-1])
                return last

            def wt(slot, cols, lo, width):
                return lambda part, kt: (w_hi, w_lo)[part][:, slot, kt * cols + lo:kt * cols + lo + width]

            def ch(hi, lo, t0=0):
                return lambda part, kt: (hi, lo)[part][:, t0 + kt, :]

            def tok(hi, lo, tt, t0=0):
                return lambda part, kt: (hi, lo)[part][:, t0 + kt, tt * P:(tt + 1) * P]

            def chunk_in(c):
                pe.wait_ge(lo_done, c + 1)

            def bank_in(u):
                if not isinstance(u, int) or u >= 2:
                    pe.wait_ge(bank_free, u - 1)

            def enter(name):
                if use0[name]:
                    pe.wait_ge(bank_free, use0[name])

            def half(c, slot, out, j, x, cols=256):
                return split_mm(out[:, j * T:(j + 1) * T], wt(slot, cols, j * P, P), x, range(KD), True)

            def norm_sums(name):
                t, gw, w, slots = NORMS[name]
                p0, g0 = NORM_AT[name]
                for g in range(t // gw):
                    b = B[NORM_BANK[name][g // 2]]
                    out = b[:, (g % 2) * T:(g % 2 + 1) * T]
                    for k in range(gw):
                        tile = g * gw + k
                        if tile % w == 0:
                            pe.wait_ge(n_sq, p0 + tile // w + 1)
                        last = mm(out, A("ones"), sqb[name][:, tile % slots, :], start=k == 0, stop=k == gw - 1)
                    last.then_inc(n_sum, 1)

            pe.wait_ge(pa_in, 16)
            norm_sums("x")
            xh = ch(h_hi, h_lo)
            pe.wait_ge(n_lo, norm_end("x"))
            c = SEC["A"][0]
            chunk_in(c)
            split_mm(G[0][:, 0:T], wt(c % 2, 192, 64, P), xh, range(KD), True)
            for tt in range(TT):
                last = split_mm(G[0][:, T + 64 * tt:T + 64 * tt + 64], wt(c % 2, 192, 0, 64), tok(h_hi, h_lo, tt),
                                range(KD), False)
            last.then_inc(chunk_used, 1)
            c = SEC["QA"][0]
            chunk_in(c)
            half(c, c % 2, G[1], 0, xh)
            half(c, c % 2, G[1], 1, xh).then_inc(chunk_used, 1)

            def transposes(i):
                pe.wait_ge(xbc_ready, i + 1)
                if i >= 2:
                    pe.wait_ge(xdt_ready, i - 1)
                for j in range(2):
                    for tt in range(TT):
                        last = nc.tensor.transpose(B[2 + i % 2][:, tt * T + j * P:tt * T + (j + 1) * P],
                                                   xbcT[:, 2 * i + j, tt * P:(tt + 1) * P], A("ident"))
                last.then_inc(xs_tr, 1)

            enter("XBC")
            for i in range(12):
                c = SEC["XBC"][0] + i
                chunk_in(c)
                bank_in(use0["XBC"] + i)
                b = G[(use0["XBC"] + i) % 2]
                half(c, c % 2, b, 0, xh)
                half(c, c % 2, b, 1, xh).then_inc(chunk_used, 1)
                if i == 0:
                    norm_sums("qa")
                    norm_sums("kva")
                if i == 1:
                    pe.wait_ge(a_ready, 1)
                    keep = A("keep")
                    mm(B[4][:, 0:32], keep[:, 0:P], a_tok[:, 0, :], start=True, stop=True)
                    mm(B[4][:, 32:64], keep[:, P:T], a_tok[:, 0, :], start=True, stop=False)
                    mm(B[4][:, 32:64], keep[:, 0:P], a_tok[:, 1, :], start=False, stop=True)
                    mm(B[4][0:32, 128:384], a_tok[:, 0, :], keep[:, 0:T], start=True, stop=False)
                    mm(B[4][0:32, 256:384], a_tok[:, 1, :], keep[:, 0:P], start=False,
                       stop=True).then_inc(cum_ps, 1)
                if 2 <= i < 10:
                    transposes(i - 2)

            def scores(g):
                if g == 0:
                    pe.wait_ge(xbc_ready, 12)
                    pe.wait_ge(acumT_sb, 1)
                if g >= 2:
                    pe.wait_ge(score_sb, g - 1)
                b = B[4 + g % 2]
                mm(b[:, 0:T], xbcT[:, 16 + g, 0:P], xbcT[:, 20 + g, :], start=True, stop=True)
                mm(b[:, T:BW], xbcT[:, 16 + g, P:T], xbcT[:, 20 + g, P:T], start=True,
                   stop=True).then_inc(score_ps, 1)

            def y_heads(i):
                pe.wait_ge(m_ready, i + 1)
                if i == 0:
                    pe.wait_ge(score_sb, NG_SSD)
                    pe.wait_ge(xdt_ready, 8)
                if i >= 2:
                    pe.wait_ge(y_ready, i - 1)
                b = B[4 + i % 2]
                for h in range(4):
                    rows = slice((h % 2) * 64, (h % 2) * 64 + 64)
                    col = (4 * i + h) * HD_SSD
                    t0 = (h // 2) * T
                    mm(b[rows, t0:t0 + T], xdt[:, 0, col:col + 64], Mt[:, i % 2, h, 0:T], start=True, stop=False)
                    last = mm(b[rows, t0 + P:t0 + T], xdt[:, 1, col:col + 64], Mt[:, i % 2, h, T:BW], start=False,
                              stop=True)
                last.then_inc(y_ps, 1)

            enter("Z")
            for i in range(9):
                name, k = ("Z", i) if i < 8 else ("GATE_A", 0)
                c, u = SEC[name][0] + k, use0[name] + k
                if name == "GATE_A":
                    enter(name)
                chunk_in(c)
                bank_in(u)
                half(c, c % 2, G[u % 2], 0, xh)
                if i == 0:
                    for g in range(NG_SSD):
                        scores(g)
                half(c, c % 2, G[u % 2], 1, xh).then_inc(chunk_used, 1)
                if i >= 1:
                    y_heads(i - 1)

            enter("UQ")
            pe.wait_ge(n_lo, norm_end("kva"))
            u = use0["UQ"]
            for k in range(2):
                c = SEC["UQ"][0] + k
                chunk_in(c)
                for hf in range(2):
                    for tt in range(TT):
                        bank_in(u)
                        last = split_mm(G[u % 2][:, 0:384], wt(c % 2, 768, hf * 384, 384), tok(qn_hi, qn_lo, tt),
                                        range(2), False)
                        last.then_inc(u_ps, 1) if not (hf and tt) else last.then_inc(chunk_used, 1)
                        u += 1
            c = SEC["UKV"][0]
            chunk_in(c)
            for quarter in range(4):
                for tt in range(TT):
                    bank_in(u)
                    last = split_mm(G[u % 2][:, :], wt(c % 2, 2048, quarter * 512, 512), tok(qn_hi, qn_lo, tt, 2),
                                    range(1), False)
                    last.then_inc(u_ps, 1) if quarter + tt < 4 else last.then_inc(chunk_used, 1)
                    u += 1

            def head_step(s):
                h = s
                if h < H_MLA:
                    if h == 0:
                        pe.wait_ge(kq_ready, 1)
                        pe.wait_ge(n_var, norm_groups("y"))
                    if h >= 2:
                        pe.wait_ge(qkT_sb, h - 1)
                    b = B[h % 2]
                    for j, src in enumerate((q96, k96)):
                        for tt in range(TT):
                            last = nc.tensor.transpose(b[0:QK, j * T + tt * P:j * T + (tt + 1) * P],
                                                       src[:, tt, h, :], A("ident"))
                    last.then_inc(qkT_ps, 1)
                h = s - 1
                if 0 <= h < H_MLA:
                    pe.wait_ge(qkT_sb, h + 1)
                    if h >= 2:
                        pe.wait_ge(sm_ready, h - 1)
                    b, kq = B[2 + h % 2], qkT[0:QK, h % 2, :]
                    mm(b[:, 0:P], kq[:, 0:P], kq[:, T:T + P], start=True, stop=True)
                    mm(b[:, P:BW], kq[:, P:T], kq[:, T:2 * T], start=True, stop=True).then_inc(s_ps, 1)
                h = s - 2
                if 0 <= h < H_MLA:
                    pe.wait_ge(p_ready, h + 1)
                    if h == 0:
                        pe.wait_ge(y_ready, 8)
                    if h >= 1:
                        pe.wait_ge(pt_sb, h)
                    for n in range(3):
                        last = nc.tensor.transpose(B[4][:, n * P:(n + 1) * P], Sm[:, h % 2, n * P:(n + 1) * P],
                                                   A("ident"))
                    last.then_inc(pt_ps, 1)
                h = s - 3
                if 0 <= h < H_MLA:
                    pe.wait_ge(pt_sb, h + 1)
                    if h % 2 == 0 and h >= 2:
                        pe.wait_ge(o_lo, h // 2)
                    rows = slice((h % 2) * 64, (h % 2) * 64 + 64)
                    mm(B[5][rows, 0:T], vS[:, 0, h, :], PTs[:, h % 2, 0:T], start=True, stop=False)
                    mm(B[5][rows, P:T], vS[:, 1, h, :], PTs[:, h % 2, T:BW], start=False,
                       stop=True).then_inc(o_ps, 1)

            step = 0
            enter("GATE_B")
            for i in range(7):
                c, u = SEC["GATE_B"][0] + i, use0["GATE_B"] + i
                chunk_in(c)
                bank_in(u)
                half(c, c % 2, G[u % 2], 0, xh)
                if i:
                    head_step(step)
                    step += 1
                half(c, c % 2, G[u % 2], 1, xh).then_inc(chunk_used, 1)
                if i:
                    head_step(step)
                    step += 1
                else:
                    norm_sums("y")
            enter("SSDP")
            pe.wait_ge(n_lo, norm_end("y"))
            for i in range(8):
                c, u = SEC["SSDP"][0] + i, use0["SSDP"] + i
                chunk_in(c)
                bank_in(u)
                out, x = G[u % 2][:, 0:T], ch(y_hi, y_lo)
                split_mm(out, wt(c % 2, P, 0, P), x, range(8), True, stop=False)
                if step < H_MLA + 3:
                    head_step(step)
                    step += 1
                split_mm(out, wt(c % 2, P, 0, P), x, range(8, 16), True, start=False).then_inc(chunk_used, 1)
                if step < H_MLA + 3 and i >= 1:
                    head_step(step)
                    step += 1
            enter("MLAP")
            pe.wait_ge(o_lo, 8)
            for i in range(4):
                c, u = SEC["MLAP"][0] + i, use0["MLAP"] + i
                chunk_in(c)
                bank_in(u)
                half(c, c % 2, G[u % 2], 0, ch(ohi, olo))
                half(c, c % 2, G[u % 2], 1, ch(ohi, olo)).then_inc(chunk_used, 1)
            enter("WO")
            pe.wait_ge(mix_lo, 4)
            for i in range(4):
                c, u = SEC["WO"][0] + i, use0["WO"] + i
                chunk_in(c)
                bank_in(u)
                half(c, c % 2, G[u % 2], 0, xh)
                half(c, c % 2, G[u % 2], 1, xh).then_inc(chunk_used, 1)

            norm_sums("ffn")
            pe.wait_ge(n_lo, norm_end("ffn"))
            enter("UP")

            def channel_chunk(c, slot, u, bank):
                chunk_in(c)
                bank_in(u)
                half(c, slot, G[bank], 0, xh)
                half(c, slot, G[bank], 1, xh).then_inc(chunk_used, 1)

            def channel_section(name):
                c0, n, _ = SEC[name]
                u0 = use0[name]
                with pe.Fori(0, n // 4, 1) as i:
                    for j in range(4):
                        channel_chunk(i * 4 + (c0 + j), (c0 + j) % 2, i * 4 + (u0 + j), (u0 + j) % 2)
                for k in range(n // 4 * 4, n):
                    channel_chunk(c0 + k, (c0 + k) % 2, u0 + k, (u0 + k) % 2)

            channel_section("UP")
            enter("DOWN")
            pe.wait_ge(f_lo, 22)

            def down_section(name, kts, hi, lo):
                c0, n, _ = SEC[name]
                with pe.Fori(0, n // 4, 1) as i:
                    for j in range(4):
                        chunk_in(i * 4 + (c0 + j))
                        bank = (use0[name] + j // 2) % 2
                        if j % 2 == 0:
                            bank_in(i * 2 + (use0[name] + j // 2))
                        split_mm(G[bank][:, 0:T], wt((c0 + j) % 2, P, 0, P), ch(hi, lo, j % 2 * kts), range(kts), True,
                                 start=j % 2 == 0, stop=j % 2 == 1).then_inc(chunk_used, 1)

            down_section("DOWN", 11, g_hi, g_lo)

            norm_sums("x2")
            pe.wait_ge(n_lo, norm_end("x2"))
            enter("CKV")
            c, u = SEC["CKV"][0], use0["CKV"]
            channel_chunk(c, c % 2, u, u % 2)
            chunk_in(c + 1)
            bank_in(u + 1)
            half(c + 1, (c + 1) % 2, G[(u + 1) % 2], 0, xh, P).then_inc(chunk_used, 1)

            def token_half(c, u, tt, cols=256):
                if tt == 0:
                    chunk_in(c)
                    bank_in(u)
                last = split_mm(G[u % 2][:, tt * cols:(tt + 1) * cols], wt(c % 2, cols, 0, cols),
                                tok(h_hi, h_lo, tt), range(KD), False)
                if tt:
                    last.then_inc(chunk_used, 1)

            for name in ("TM_A", "TM_G"):
                enter(name)
                for i in range(SEC[name][1]):
                    for tt in range(TT):
                        token_half(SEC[name][0] + i, use0[name] + i, tt, 64 if name == "TM_G" else 256)
            enter("CW1")
            pe.wait_ge(b_lo, 1)
            for i in range(4):
                c, u = SEC["CW1"][0] + i, use0["CW1"] + i
                chunk_in(c)
                bank_in(u)
                split_mm(G[u % 2][:, 0:3 * CG], wt(c % 2, P, 0, P),
                         lambda part, kt: (bT_hi, bT_lo)[part][:, i // 2, kt].rearrange("p g n -> p (g n)"),
                         range(16), True).then_inc(chunk_used, 1)

            def second_layer():
                pe.wait_ge(ge_done, 1)
                for kv, name in enumerate(("w2_k", "w2_v")):
                    w2 = Bp(name).rearrange("p (m d) -> p m d", m=2)
                    for g in range(G_NSA):
                        for m in range(2):
                            last = mm(B[0][0:CG, (kv * 3 + g) * HD:(kv * 3 + g + 1) * HD],
                                      hid[:, 0, kv, m, g * CG:(g + 1) * CG], w2[:, m, :], start=m == 0, stop=m == 1)
                last.then_inc(c_ps, 1)

            def k_transposes():
                pe.wait_ge(k_ready, 1)
                for n in range(6):
                    for tt in range(TT):
                        last = nc.tensor.transpose(B[1 + n // 2][0:HD, (n % 2) * T + tt * P:(n % 2) * T + tt * P + P],
                                                   tm[:, tt, 768 + n * HD:768 + (n + 1) * HD], A("ident"))
                last.then_inc(kT_ps, 1)

            def kc_transposes():
                pe.wait_ge(cn_ready, 1)
                for g in range(G_NSA):
                    last = nc.tensor.transpose(B[0][0:HD, g * CG:(g + 1) * CG], cn[:, 0, g, :],
                                               A("ident")[0:CG, 0:CG])
                last.then_inc(cT_ps, 1)

            def nsa_step(s):
                h = s
                if s == 0:
                    pe.wait_ge(cT_sb, 1)
                    pe.wait_ge(kT_sb, 1)
                if h < H_NSA:
                    if h >= 1:
                        pe.wait_ge(nq_sb, h)
                    for tt in range(TT):
                        last = nc.tensor.transpose(B[0][0:HD, tt * P:(tt + 1) * P], tm[:, tt, h * HD:(h + 1) * HD],
                                                   A("ident"))
                elif h < H_NSA + 2:
                    pe.wait_ge(nq_sb, h)
                if 0 <= h - 2 < H_NSA:
                    pe.wait_ge(np_ready, h - 1)
                    for tt in range(TT):
                        last = nc.tensor.transpose(B[0][0:CG, T + tt * P:T + (tt + 1) * P],
                                                   S2[:, h % 2, 768 + tt * CG:768 + (tt + 1) * CG], A("ident"))
                if h < H_NSA + 2:
                    last.then_inc(nq_ps, 1)
                h = s - 1
                if 0 <= h < H_NSA:
                    pe.wait_ge(nq_sb, h + 1)
                    if h >= 1:
                        pe.wait_ge(nm_ready, h)
                    q, g = qkT2[:, h % 2, 0:T], h // HPG
                    for n, b in enumerate((B[1], B[2])):
                        kT = kswT[:, 3 * n + g, :]
                        mm(b[:, 0:P], q[:, 0:P], kT[:, 0:P], start=True, stop=True)
                        mm(b[:, P:BW], q[:, P:T], kT, start=True, stop=True)
                    for tt in range(TT):
                        last = mm(B[2][:, BW + tt * CG:BW + (tt + 1) * CG], q[:, tt * P:(tt + 1) * P], kcT[:, g, :],
                                  start=True, stop=True)
                    last.then_inc(ns_ps, 1)
                h = s - 2
                if 0 <= h < H_NSA:
                    if h >= 1:
                        pe.wait_ge(npt_sb, h)
                    for n in range(6):
                        last = nc.tensor.transpose(B[3 + n // 3][:, n % 3 * P:(n % 3 + 1) * P],
                                                   S2[:, h % 2, n * P:(n + 1) * P], A("ident"))
                    last.then_inc(npt_ps, 1)
                h = s - 3
                if 0 <= h < H_NSA:
                    pe.wait_ge(npt_sb, h + 1)
                    pe.wait_ge(nq_sb, h + 3)
                    if h % 2 == 0 and h >= 2:
                        pe.wait_ge(no_lo, h // 2)
                    g, out = h // HPG, B[5][(h % 2) * 64:(h % 2) * 64 + 64, :]
                    for n in range(2):
                        c0 = 1152 + 192 * n + g * HD
                        pt = PT2[:, 2 * (h % 2) + n, :]
                        mm(out[:, 0:T], tm[:, 0, c0:c0 + HD], pt[:, 0:T], start=n == 0, stop=False)
                        mm(out[:, P:T], tm[:, 1, c0:c0 + HD], pt[:, T:BW], start=False, stop=False)
                    mm(out[:, 0:T], vc[:, g, :], pcT[:, h % 2, :], start=False, stop=True).then_inc(no_ps, 1)

            def dil_step(s):
                u = s
                if u < H_DIL:
                    if u == 0:
                        pe.wait_ge(k_ready, 2)
                        pe.wait_ge(nq_sb, H_NSA + 2)
                    if u >= 1:
                        pe.wait_ge(dq_sb, u)
                    for j, c0 in enumerate((1536, 2304)):
                        col = c0 + (u % 3 * DH + u // 3) * HD
                        for tt in range(TT):
                            last = nc.tensor.transpose(B[0][0:HD, j * T + tt * P:j * T + (tt + 1) * P],
                                                       tm[:, tt, col:col + HD], A("ident"))
                    last.then_inc(dq_ps, 1)
                u = s - 1
                if 0 <= u < H_DIL:
                    pe.wait_ge(dq_sb, u + 1)
                    if u == 0:
                        pe.wait_ge(nm_ready, H_NSA)
                    if u >= 2:
                        pe.wait_ge(dm_part, u - 1)
                    b, q = B[1 + u % 2], qkT2[:, u % 2, :]
                    mm(b[:, 0:P], q[:, 0:P], q[:, T:T + P], start=True, stop=True)
                    mm(b[:, P:BW], q[:, P:T], q[:, T:2 * T], start=True, stop=True).then_inc(ds_ps, 1)
                u = s - 5
                if 0 <= u < H_DIL:
                    pe.wait_ge(dp_ready, u // 3 + 1)
                    if u == 0:
                        pe.wait_ge(npt_sb, H_NSA)
                    if u >= 2:
                        pe.wait_ge(dpt_sb, u - 1)
                    for n in range(3):
                        last = nc.tensor.transpose(B[3 + u % 2][:, n * P:(n + 1) * P],
                                                   S2[:, u // 3 % 2, u % 3 * BW + n * P:u % 3 * BW + (n + 1) * P],
                                                   A("ident"))
                    last.then_inc(dpt_ps, 1)
                u = s - 6
                if 0 <= u < H_DIL:
                    hh, g = u // 3, u % 3
                    pe.wait_ge(dpt_sb, u + 1)
                    if u == 0:
                        pe.wait_ge(no_lo, H_NSA // 2)
                    if hh == 2 and g == 0:
                        pe.wait_ge(do_lo, 1)
                    out, col = B[5][(hh % 2) * 64:(hh % 2) * 64 + 64, :], 3072 + (g * DH + hh) * HD
                    mm(out[:, 0:T], tm[:, 0, col:col + HD], PT2[:, u % 2, 0:T], start=g == 0, stop=False)
                    mm(out[:, P:T], tm[:, 1, col:col + HD], PT2[:, u % 2, T:BW], start=False,
                       stop=g == 2).then_inc(do_ps, 1)

            enter("TM_B")
            nsa = dil = 0
            for i in range(9):
                for tt in range(TT):
                    token_half(SEC["TM_B"][0] + i, use0["TM_B"] + i, tt)
                    if i == 0 and tt == 1:
                        k_transposes()
                        second_layer()
                    if i == 1 and tt == 1:
                        kc_transposes()
                    if i >= 3:
                        nsa_step(nsa)
                        nsa += 1
            enter("GATE2")
            for i in range(8):
                c, u = SEC["GATE2"][0] + i, use0["GATE2"] + i
                chunk_in(c)
                bank_in(u)
                for j in range(2):
                    last = half(c, c % 2, G[u % 2], j, xh)
                    if j:
                        last.then_inc(chunk_used, 1)
                    if nsa < H_NSA + 3:
                        nsa_step(nsa)
                        nsa += 1
                    else:
                        dil_step(dil)
                        dil += 1
            while dil < H_DIL + 6:
                dil_step(dil)
                dil += 1
            enter("OAB")
            pe.wait_ge(no_lo, 6)
            pe.wait_ge(do_lo, 2)
            u = use0["OAB"]
            for i in range(4):
                c = SEC["OAB"][0] + i
                chunk_in(c)
                for kts in (range(6), range(6, 8)):
                    bank_in(u)
                    for j in range(2):
                        last = split_mm(G[u % 2][:, j * T:(j + 1) * T], wt(c % 2, 256, j * P, P), ch(o2_hi, o2_lo),
                                        kts, True)
                    last.then_inc(chunk_used if kts[0] else oab_ps, 1)
                    u += 1
            enter("WOUT")
            pe.wait_ge(mix2_lo, 4)
            for i in range(4):
                c, u = SEC["WOUT"][0] + i, use0["WOUT"] + i
                channel_chunk(c, c % 2, u, u % 2)
            norm_sums("ffn2")
            pe.wait_ge(n_lo, norm_end("ffn2"))
            enter("UP2")
            channel_section("UP2")
            enter("DOWN2")
            pe.wait_ge(sq_lo, 16)
            down_section("DOWN2", 16, s_hi, s_lo)

        @block.scalar
        def _(act):
            fn = nc.scalar.activation
            own = Tally(act, act_own)

            def hi_of(c, it=None):
                used = next(u for c0, n, u in SEC.values() if c0 <= c < c0 + n)
                slot = c % RAW_SLOTS
                rounds = c // RAW_SLOTS + 1
                if it is None:
                    act.wait_ge(landed[slot], 16 * rounds)
                    if c >= SPLIT_SLOTS:
                        act.wait_ge(chunk_used, c - 1)
                else:
                    act.wait_ge(landed[slot], it * 16 + 16 * rounds)
                    act.wait_ge(chunk_used, it * 4 + (c - 1))
                fn(w_hi[:, c % 2, 0:used], raw[:, slot, 0:used], ACT.Copy).then_inc(hi_done, 1)

            LAST = NCHUNK - 1

            def ahead(c, it=None):
                if c + 1 <= LAST:
                    hi_of(c + 1, it)

            def norm_squares(name):
                t, gw, w, slots = NORMS[name]
                p0, g0 = NORM_AT[name]
                src, s0 = NORM_IO[name][:2]
                for p in range(t // w):
                    k = p * w
                    g = k // gw
                    if k >= slots:
                        act.wait_ge(n_sum, g0 + g)
                    fn(sqb[name][:, k % slots:k % slots + w, :], src[:, s0 + k:s0 + k + w, :],
                       ACT.Square).then_inc(n_sq, 1)

            def norm_root(name):
                t, gw, _, _ = NORMS[name]
                n = t // gw
                act.wait_ge(n_var, norm_groups(name))
                fn(rs[:, 0:n, :], rs[:, 0:n, :], ACT.Sqrt).then_inc(n_rs, 1)

            def norm_hi(name, pieces=None):
                t, gw, w, slots = NORMS[name]
                p0, _ = NORM_AT[name]
                _, s0, _, hi, _ = NORM_IO[name]
                for p in pieces or range(t // w):
                    act.wait_ge(n_f, p0 + p + 1)
                    k = p * w
                    fn(hi[:, s0 + k:s0 + k + w, :], hfb[name][:, k % slots:k % slots + w, :],
                       ACT.Copy).then_inc(n_hi, 1)

            act.dma_start(xT[:, :, :], x_t).then_inc(x_in, 16)
            act.dma_start(pa[:, :], params_a).then_inc(pa_in, 16)
            act.wait_ge(x_in, 16)
            norm_squares("x")
            hi_of(0)
            norm_root("x")
            norm_hi("x")
            hi_of(1)
            act.wait_ge(dtr_ready, 1)
            own.link(fn(dtw[:, 1, :], dtw[:, 0, :], ACT.Abs))
            fn(dtw[:, 2, :], dtw[:, 1, :], ACT.Exp, scale=-1.0).then_inc(sp_exp, 1)
            fn(expa[:, :], A("alog"), ACT.Exp).then_inc(sp_exp, 1)
            hi_of(2)
            act.wait_ge(sp_u, 1)
            fn(dtw[:, 4, :], dtw[:, 3, :], ACT.Ln).then_inc(sp_ln, 1)
            act.wait_ge(bank_free, 2)
            norm_squares("qa")
            act.wait_ge(n_sum, norm_groups("qa"))
            norm_squares("kva")
            x0 = SEC["XBC"][0]

            def conv_copy(i):
                act.wait_ge(chunk_used, x0 + i + 1)
                if i >= 2:
                    act.wait_ge(conv_acc, i - 1)
                fn(ub[:, i % 2], G[(use0["XBC"] + i) % 2][:, :].rearrange("p (j t) -> p j t", j=2),
                   ACT.Copy).then_inc(bank_free, 1)

            def conv_tanh(i):
                act.wait_ge(conv_acc, i + 1)
                if i >= 2:
                    act.wait_ge(xbc_ready, i - 1)
                fn(tb[:, i % 2], cacc[:, i % 2], ACT.Tanh).then_inc(conv_t, 1)

            def rows(i):
                if i >= 2:
                    act.wait_ge(seg_ready, i - 1)
                act.dma_start(Rb[:, i % 2], scr[4 * i:4 * i + 4, :].rearrange("(o h) t -> o h t", o=1)
                              .broadcast_to([P, 4, T])).then_inc(rows_in[i % 2], 16)

            for i in range(12):
                ahead(x0 + i)
                conv_copy(i)
                if i == 1:
                    norm_root("qa")
                    norm_hi("qa")
                    norm_root("kva")
                    norm_hi("kva")
                if i >= 1:
                    conv_tanh(i - 1)
                if i == 4:
                    act.wait_ge(acumT_sb, 1)
                    act.dma_start(scr, acumT[:, :]).then_inc(rows_out, 16)
                if i == 6:
                    act.wait_ge(rows_out, 16)
                    rows(0)
                    rows(1)
            conv_tanh(11)

            def gate_tanh(name, i, m):
                c, u = SEC[name][0] + i, use0[name] + i
                act.wait_ge(chunk_used, c + 1)
                for j in range(2):
                    ins = fn(gT[:, m + j, :], G[u % 2][:, j * T:(j + 1) * T], ACT.Tanh, scale=0.5,
                             bias=gbh[:, m + j:m + j + 1])
                ins.then_inc(bank_free, 1)

            for i in range(8):
                c = SEC["Z"][0] + i
                ahead(c)
                act.wait_ge(seg_ready, i + 1)
                if i >= 1:
                    act.wait_ge(m_ready, i)
                fn(seg[:, :, :], seg[:, :, :], ACT.Exp).then_inc(decay_ready, 1)
                if i + 2 < 8:
                    rows(i + 2)
                act.wait_ge(chunk_used, c + 1)
                if i >= 2:
                    act.wait_ge(bank_free, use0["Z"] + i - 1)
                fn(tb[:, i % 2], G[(use0["Z"] + i) % 2][:, :].rearrange("p (j t) -> p j t", j=2), ACT.Tanh,
                   scale=0.5).then_inc(z_t, 1)
            ahead(SEC["GATE_A"][0])
            gate_tanh("GATE_A", 0, 0)

            c_uq = SEC["UQ"][0]
            act.wait_ge(y_ready, 8)
            for n in range(16):
                if n in (0, 4, 8):
                    ahead(c_uq + n // 4)
                if n in (3, 7, 15):
                    act.wait_ge(chunk_used, c_uq + n // 4 + 1 if n < 8 else c_uq + 3)
                else:
                    act.wait_ge(u_ps, n + 1 - (n > 3) - (n > 7))
                bank = G[(use0["UQ"] + n) % 2]
                if n < 8:
                    fn(sqt[:, n % 2, 0:384], bank[:, 0:384], ACT.Square).then_inc(u_sq, 1)
                else:
                    fn(sqt[:, n % 2, 0:256].rearrange("p (h d) -> p h d", h=4),
                       bank[:, :].rearrange("p (h d) -> p h d", h=4)[:, :, 0:NOPE], ACT.Square).then_inc(u_sq, 1)
            act.wait_ge(kq_ss, 1)
            fn(rqk[:, :, :, :], rqk[:, :, :, :], ACT.Sqrt).then_inc(kq_rs, 1)

            def head_step(s):
                h = s
                if h < H_MLA:
                    act.wait_ge(qkT_ps, h + 1)
                    if h >= 2:
                        act.wait_ge(s_ps, h - 1)
                    fn(qkT[0:QK, h % 2, :], B[h % 2][0:QK, :], ACT.Copy).then_inc(qkT_sb, 1)
                h = s - 1
                if 0 <= h < H_MLA:
                    act.wait_ge(sm_ready, h + 1)
                    for tt, (a, b) in enumerate(((0, P), (P, BW))):
                        ins = fn(Sm[:, h % 2, a:b], Sm[:, h % 2, a:b], ACT.Exp, scale=qsc[:, 0, tt, h:h + 1],
                                 bias=mx[:, h % 2, 2 + tt:3 + tt], accum_out=mx[:, h % 2, 4 + tt:5 + tt])
                        ins.then_inc(p_exp, 1)
                h = s - 3
                if 0 <= h < H_MLA and h % 2:
                    act.wait_ge(o_ps, h + 1)
                    fn(ohi[:, h // 2, :], B[5][:, 0:T], ACT.Copy).then_inc(o_hi, 1)

            step = 0
            for i in range(7):
                ahead(SEC["GATE_B"][0] + i)
                if i == 0:
                    act.wait_ge(y_ready, 8)
                    norm_squares("y")
                    norm_root("y")
                    gate_tanh("GATE_B", i, 2)
                    norm_hi("y", range(0, 2))
                    continue
                head_step(step)
                gate_tanh("GATE_B", i, 2 + 2 * i)
                head_step(step + 1)
                step += 2
                if i < 4:
                    norm_hi("y", range(2 * i, 2 * i + 2))
            for i in range(8):
                ahead(SEC["SSDP"][0] + i)
                for _ in range(1 if i == 0 else 2):
                    if step < H_MLA + 3:
                        head_step(step)
                        step += 1
            for i in range(4):
                ahead(SEC["MLAP"][0] + i)
                if i == 0:
                    act.wait_ge(chunk_used, SEC["GATE_B"][0] + 7)
                act.wait_ge(mix_ready, i + 1)
                fn(h_hi[:, 2 * i:2 * i + 2, :], mixa[:, 2 * i:2 * i + 2, :], ACT.Copy).then_inc(mix_hi, 1)
            for i in range(4):
                ahead(SEC["WO"][0] + i)
                act.wait_ge(bank_free, use0["WO"] + i + 1)
                fn(sqb["ffn"][:, 2 * i:2 * i + 2, :], xT[:, 2 * i:2 * i + 2, :], ACT.Square).then_inc(n_sq, 1)
            norm_root("ffn")
            act.wait_ge(chunk_used, SEC["UP"][0])
            norm_hi("ffn")

            c0, u0 = SEC["UP"][0], use0["UP"]

            def ffn_copy(k, par, bank, it=None):
                kk = k if it is None else it * 4 + k
                act.wait_ge(chunk_used, kk + (c0 + 1))
                if k >= 2 or it is not None:
                    act.wait_ge(f_acc, kk - 1)
                fn(fub[:, par], G[bank][:, :].rearrange("p (j t) -> p j t", j=2), ACT.Copy).then_inc(bank_free, 1)

            def ffn_gate(k, par, it=None):
                kk = k if it is None else it * 4 + k
                act.wait_ge(f_acc, kk + 1)
                fn(ftg[:, par], facc[:, par, 0, :], ACT.Tanh).then_inc(f_t, 1)
                act.wait_ge(f_g, kk + 1)
                fn(g_hi[:, kk, :], fg[:, par], ACT.Copy).then_inc(f_hi, 1)

            ahead(c0)
            ffn_copy(0, 0, u0 % 2)
            ahead(c0 + 1)
            ffn_copy(1, 1, (u0 + 1) % 2)
            ffn_gate(0, 0)
            with act.Fori(0, 4, 1) as i:
                for j in range(4):
                    k = 2 + j
                    ahead(c0 + k, i)
                    ffn_copy(k, k % 2, (u0 + k) % 2, i)
                    ffn_gate(k - 1, (k - 1) % 2, i)
            for k in range(18, 22):
                ahead(c0 + k)
                ffn_copy(k, k % 2, (u0 + k) % 2)
                ffn_gate(k - 1, (k - 1) % 2)
            ffn_gate(21, 1)
            c0 = SEC["DOWN"][0]
            with act.Fori(0, 3, 1) as i:
                for j in range(4):
                    ahead(c0 + j, i)
            for k in range(12, 16):
                ahead(c0 + k)

            act.dma_start(pb[:, :], params_b).then_inc(pb_in, 16)
            act.wait_ge(bank_free, use0["CKV"])
            norm_squares("x2")
            norm_root("x2")
            norm_hi("x2")
            for i in range(2):
                c = SEC["CKV"][0] + i
                ahead(c)
                act.wait_ge(chunk_used, c + 1)
                w = 512 >> i
                fn(ckv[:, 2 * i:2 * i + 2 - i, :], G[(use0["CKV"] + i) % 2][:, 0:w]
                   .rearrange("p (j t) -> p j t", j=2 - i), ACT.Copy).then_inc(bank_free, 1)
            act.wait_ge(bank_free, use0["CKV"] + 2)
            for r in range(2):
                for sh in range(2):
                    act.dma_start(cblk[sh * 64:sh * 64 + 64, r:6:2, 0:T - sh],
                                  ckv[r * 64:r * 64 + 64, :, sh:T]).then_inc(cblk_in, 16)

            def token_squares(n, name, i, heads):
                c, u = SEC[name][0] + i, use0[name] + i
                act.wait_ge(chunk_used, c + 1)
                if n >= 2:
                    act.wait_ge(t_free, n - 1)
                src = G[u % 2][:, :].rearrange("p (t h d) -> p t h d", t=2, d=HD)[:, :, 0:heads, :]
                fn(sqt2[:, n % 2].rearrange("p (t h) d -> p t h d", t=2)[:, :, 0:heads, :], src,
                   ACT.Square).then_inc(t_sq, 1)

            for i in range(6):
                ahead(SEC["TM_A"][0] + i)
                if i < 5:
                    token_squares(i, "TM_A", i, 2 if i == 4 else 4)
                if i == 3:
                    act.wait_ge(b_ready, 1)
                    fn(bT_hi[:, :, :, :, :].rearrange("p a b g n -> p (a b g n)"),
                       bT[:, :, :, :, :].rearrange("p a b g n -> p (a b g n)"), ACT.Copy).then_inc(b_hi, 1)
            ahead(SEC["TM_G"][0])
            act.wait_ge(chunk_used, SEC["TM_G"][0] + 1)
            fn(gnsa[:, :, :], G[use0["TM_G"] % 2][:, 0:P].rearrange("p (t n) -> p t n", t=2)[:, :, 0:36], ACT.Tanh,
               scale=0.5).then_inc(bank_free, 1)
            for i in range(4):
                c = SEC["CW1"][0] + i
                ahead(c)
                act.wait_ge(chunk_used, c + 1)
                if i == 0:
                    act.wait_ge(b_lo, 1)
                ins = fn(hid[:, 0, i // 2, i % 2, :], G[(use0["CW1"] + i) % 2][:, 0:3 * CG], ACT.Copy)
                ins.then_inc(bank_free, 1)
            act.wait_ge(ge_in, 1)
            fn(hid[:, 1], hid[:, 1], ACT.Tanh, scale=(2.0 / np.pi) ** 0.5).then_inc(ge_t, 1)
            act.wait_ge(ss_ready, 1)
            fn(r2[:, :, 0:18], ss2[:, :, 0:18], ACT.Sqrt).then_inc(rs_ready, 1)

            def nsa_step(s):
                h = s
                if h < H_NSA + 2:
                    act.wait_ge(nq_ps, h + 1)
                    if h < H_NSA:
                        if h >= 2:
                            act.wait_ge(ns_ps, h - 1)
                        ins = fn(qkT2[:, h % 2, 0:T], B[0][0:HD, 0:T], ACT.Copy)
                    if h >= 2:
                        if h < H_NSA:
                            own.link(ins)
                        if h >= 4:
                            act.wait_ge(no_ps, h - 3)
                        ins = fn(pcT[:, h % 2, :], B[0][0:CG, T:2 * T], ACT.Copy)
                    ins.then_inc(nq_sb, 1)
                h = s - 1
                if 0 <= h < H_NSA:
                    act.wait_ge(nm_ready, h + 1)
                    m, sc = m2[:, h % 2], qs2[:, 0, :, h]
                    for b, c0, w0, w1 in ((1, 0, P, T), (2, BW, P, T), (0, 768, CG, CG)):
                        for tt in range(TT):
                            lo = c0 + tt * w0
                            x = S2[:, h % 2, lo:lo + (w1 if tt else w0)]
                            fn(x, x, ACT.Exp, scale=sc[:, tt:tt + 1], bias=m[:, 1, 2 * b + tt:2 * b + tt + 1],
                               accum_out=m[:, 2, 2 * b + tt:2 * b + tt + 1]).then_inc(n_exp, 1)
                h = s - 3
                if 0 <= h < H_NSA and h % 2:
                    act.wait_ge(no_ps, h + 1)
                    fn(o2_hi[:, h // 2, :], B[5][:, 0:T], ACT.Copy).then_inc(no_hi, 1)

            def dil_step(s):
                u = s
                if u < H_DIL:
                    act.wait_ge(dq_ps, u + 1)
                    if u >= 2:
                        act.wait_ge(ds_ps, u - 1)
                    elif u == 0:
                        act.wait_ge(ns_ps, H_NSA)
                    fn(qkT2[:, u % 2, :], B[0][0:HD, :], ACT.Copy).then_inc(dq_sb, 1)
                u = s - 1
                if 0 <= u < H_DIL and u % 3 == 2:
                    hh = u // 3
                    act.wait_ge(dm_ready, hh + 1)
                    for g in range(DG):
                        for tt, (a, b) in enumerate(((0, P), (P, BW))):
                            x = S2[:, hh % 2, g * BW + a:g * BW + b]
                            head = 18 + g * DH + hh
                            fn(x, x, ACT.Exp, scale=qs2[:, 0, tt, head:head + 1], bias=md[:, 0, tt:tt + 1],
                               accum_out=m2[:, hh % 2, 2, 2 * g + tt:2 * g + tt + 1]).then_inc(d_exp, 1)
                u = s - 6
                if 0 <= u < H_DIL and u % 6 == 5:
                    act.wait_ge(do_ps, u + 1)
                    fn(o2_hi[:, 6 + u // 6, :], B[5][:, 0:T], ACT.Copy).then_inc(do_hi, 1)

            nsa = dil = 0
            for i in range(9):
                ahead(SEC["TM_B"][0] + i)
                if i < 6:
                    token_squares(5 + i, "TM_B", i, 4)
                if i == 0:
                    act.wait_ge(kT_ps, 1)
                    for n in range(3):
                        ins = fn(kswT[:, 2 * n:2 * n + 2, :], B[1 + n][0:HD, :].rearrange("p (j t) -> p j t", j=2),
                                 ACT.Copy)
                    ins.then_inc(kT_sb, 1)
                    act.wait_ge(c_ss, 1)
                    fn(ssc[:, 1, :], ssc[:, 0, :], ACT.Sqrt).then_inc(c_rs, 1)
                if i == 1:
                    act.wait_ge(cT_ps, 1)
                    fn(kcT[:, :, :], B[0][0:HD, 0:3 * CG].rearrange("p (g n) -> p g n", g=3),
                       ACT.Copy).then_inc(cT_sb, 1)
                if i >= 3:
                    nsa_step(nsa)
                    nsa_step(nsa + 1)
                    nsa += 2
            for i in range(8):
                c, u = SEC["GATE2"][0] + i, use0["GATE2"] + i
                ahead(c)
                for j in range(2):
                    if j == 1:
                        if i == 0:
                            act.wait_ge(ss_ready, 2)
                            fn(r2[:, :, 18:42], ss2[:, :, 18:42], ACT.Sqrt).then_inc(rs_ready, 1)
                        act.wait_ge(chunk_used, c + 1)
                        fn(gT2[:, 2 * i:2 * i + 2, :], G[u % 2][:, :].rearrange("p (j t) -> p j t", j=2), ACT.Tanh,
                           scale=0.5).then_inc(bank_free, 1)
                    if nsa < H_NSA + 3:
                        nsa_step(nsa)
                        nsa += 1
                    else:
                        dil_step(dil)
                        dil += 1
            while dil < H_DIL + 6:
                dil_step(dil)
                dil += 1
            for i in range(4):
                ahead(SEC["OAB"][0] + i)
                if i == 0:
                    act.wait_ge(chunk_used, SEC["OAB"][0])
                act.wait_ge(mix2_ready, i + 1)
                fn(h_hi[:, 2 * i:2 * i + 2, :], mix2[:, 2 * i:2 * i + 2, :], ACT.Copy).then_inc(mix2_hi, 1)
            for i in range(4):
                ahead(SEC["WOUT"][0] + i)
                act.wait_ge(bank_free, use0["WOUT"] + i + 1)
                fn(sqb["ffn2"][:, 2 * i:2 * i + 2, :], xT[:, 2 * i:2 * i + 2, :], ACT.Square).then_inc(n_sq, 1)
            norm_root("ffn2")
            act.wait_ge(chunk_used, SEC["UP2"][0])
            norm_hi("ffn2")
            c0, u0 = SEC["UP2"][0], use0["UP2"]

            def relu(k, par, bank, it=None):
                kk = k if it is None else it * 4 + k
                act.wait_ge(chunk_used, kk + (c0 + 1))
                if k >= 2 or it is not None:
                    act.wait_ge(sq_f, kk - 1)
                fn(srl[:, par], G[bank][:, :].rearrange("p (j t) -> p j t", j=2), ACT.Relu).then_inc(bank_free, 1)

            def square_hi(k, par, it=None):
                kk = k if it is None else it * 4 + k
                act.wait_ge(sq_f, kk + 1)
                fn(s_hi[:, bass.ds(kk * 2, 2), :], ssqr[:, par], ACT.Copy).then_inc(sq_hi, 1)

            for k in range(2):
                ahead(c0 + k)
                relu(k, k % 2, (u0 + k) % 2)
            square_hi(0, 0)
            with act.Fori(0, 3, 1) as i:
                for j in range(4):
                    k = 2 + j
                    ahead(c0 + k, i)
                    relu(k, k % 2, (u0 + k) % 2, i)
                    square_hi(k - 1, (k - 1) % 2, i)
            for k in range(14, 16):
                ahead(c0 + k)
                relu(k, k % 2, (u0 + k) % 2)
                square_hi(k - 1, (k - 1) % 2)
            square_hi(15, 1)
            c0 = SEC["DOWN2"][0]
            with act.Fori(0, 3, 1) as i:
                for j in range(4):
                    ahead(c0 + j, i)
            for k in range(12, 15):
                ahead(c0 + k)

        @block.vector
        def _(dve):
            v = nc.vector
            own = Tally(dve, dve_own)
            link = own.link

            def half_of(dst, src):
                return v.tensor_scalar(dst, src, 0.5, None, ALU.mult)

            def norm_vars(name):
                t, gw, _, _ = NORMS[name]
                g0 = NORM_AT[name][1]
                for g in range(t // gw):
                    if g % 2 == 0:
                        dve.wait_ge(n_sum, g0 + min(g + 2, t // gw))
                    b = B[NORM_BANK[name][g // 2]][:, (g % 2) * T:(g % 2 + 1) * T]
                    eps = EPS * (4.0 if name == "y" else 1.0)
                    link(v.tensor_scalar(rs[:, g, :], b, 1.0 / (gw * P), eps, ALU.mult, ALU.add))
                    v.reciprocal(rs[:, g, :], rs[:, g, :]).then_inc(n_var, 1)

            def norm_scale(name, pieces=None):
                t, gw, w, slots = NORMS[name]
                p0, _ = NORM_AT[name]
                src, s0, gain, hi, lo = NORM_IO[name]
                for p in pieces or range(t // w):
                    if p * w >= slots:
                        dve.wait_ge(n_hi, p0 + p - slots // w + 1)
                    for k in range(p * w, p * w + w):
                        ins = v.scalar_tensor_tensor(out=hfb[name][:, k % slots, :], in0=src[:, s0 + k, :],
                                                     scalar=A(gain)[:, k:k + 1], in1=rs[:, k // gw, :], op0=ALU.mult,
                                                     op1=ALU.mult)
                        if k < p * w + w - 1:
                            link(ins)
                    ins.then_inc(n_f, 1)
                    dve.wait_ge(n_hi, p0 + p + 1)
                    k = p * w
                    v.tensor_tensor(lo[:, s0 + k:s0 + k + w, :], hfb[name][:, k % slots:k % slots + w, :],
                                    hi[:, s0 + k:s0 + k + w, :], ALU.subtract).then_inc(n_lo, 1)
                    dve.wait_ge(n_lo, p0 + p + 1)

            dve.wait_ge(pa_in, 16)
            dve.wait_ge(x_in, 16)
            norm_vars("x")
            dve.wait_ge(n_rs, 1)
            norm_scale("x")
            link(half_of(cwh[:, :, 0:4], A("cw").rearrange("p (m j) -> p m j", j=4)))
            link(half_of(cwh[:, :, 4:5], A("cb").rearrange("p (m j) -> p m j", j=1)))
            link(half_of(gbh[:, :], A("gate_b")))
            fw4, fb4 = A("fw").rearrange("p (m j) -> p m j", j=3), A("fb").rearrange("p (m j) -> p m j", j=1)
            link(v.tensor_copy(fwh[:, :, 0:3], fw4))
            link(v.tensor_copy(fwh[:, :, 3:4], fb4))
            link(half_of(fwh[:, 0:44:2, 0:4], fwh[:, 0:44:2, 0:4]))

            dve.wait_ge(chunk_used, 1)
            link(v.tensor_copy(qaT[:, 2, :], G[0][:, 0:T]))
            tokm = G[0][:, T:T + 2 * 64].rearrange("p (t n) -> p t n", t=2)
            dt2 = dtw[:, 0, :].rearrange("p (t n) -> p t n", t=2)
            v.tensor_tensor(dt2, tokm[:, :, 0:32], A("dtb").unsqueeze(1).broadcast_to([P, TT, 32]),
                            ALU.add).then_inc(dtr_ready, 1)
            v.tensor_copy(kr[:, :, :], tokm[:, :, 32:64]).then_inc(bank_free, 1)
            dve.wait_ge(bank_free, 1)
            dve.wait_ge(chunk_used, 2)
            v.tensor_copy(qaT[:, 0:2, :], G[1][:, :].rearrange("p (j t) -> p j t", j=2)).then_inc(bank_free, 1)
            dve.wait_ge(bank_free, 2)
            dve.wait_ge(sp_exp, 2)
            v.tensor_scalar(dtw[:, 3, :], dtw[:, 2, :], 1.0, None, ALU.add).then_inc(sp_u, 1)
            dve.wait_ge(sp_u, 1)
            link(v.tensor_scalar(dtw[:, 5, :], dtw[:, 3, :], -1.0, None, ALU.add))
            link(v.tensor_tensor(dtw[:, 6, :], dtw[:, 2, :], dtw[:, 5, :], ALU.subtract))
            link(v.reciprocal(dtw[:, 7, :], dtw[:, 3, :]))
            link(v.tensor_tensor(dtw[:, 6, :], dtw[:, 6, :], dtw[:, 7, :], ALU.mult))
            dve.wait_ge(sp_ln, 1)
            link(v.tensor_tensor(dtw[:, 6, :], dtw[:, 6, :], dtw[:, 4, :], ALU.add))
            link(v.scalar_tensor_tensor(out=dtw[:, 0, :], in0=dtw[:, 0, :], scalar=0.0, in1=dtw[:, 6, :], op0=ALU.max,
                                        op1=ALU.add))
            link(v.scalar_tensor_tensor(out=a_tok[:, 0, :], in0=dt2[:, 0, :], scalar=-1.0, in1=expa[:, :],
                                        op0=ALU.mult, op1=ALU.mult))
            v.scalar_tensor_tensor(out=a_tok[:, 1, :], in0=dt2[:, 1, :], scalar=-1.0, in1=expa[:, :],
                                   op0=ALU.mult, op1=ALU.mult).then_inc(a_ready, 1)
            for tt in range(TT):
                link(v.tensor_tensor_reduce(out=krt[:, 0:2, tt, :].rearrange("p a b -> p a b"), in0=kr[:, tt, :]
                                            .rearrange("p (a b) -> p a b", a=2), in1=kr[:, tt, :]
                                            .rearrange("p (a b) -> p a b", a=2), scale=1.0, scalar=0.0,
                                            op0=ALU.mult, op1=ALU.add, accum_out=sskr[:, tt:tt + 1]))
            link(v.tensor_tensor(krg[:, :, :], kr[:, :, :], A("g_k")[:, NOPE:QK].unsqueeze(1)
                                 .broadcast_to([P, TT, ROPE]), ALU.mult))
            cos, sin = (A(n).rearrange("p (t n) -> p t n", t=2) for n in ("cos16", "sin16"))
            HR = ROPE // 2
            link(v.tensor_tensor(krt[:, 0], krg[:, :, 0:HR], cos, ALU.mult))
            link(v.tensor_tensor(krt[:, 1], krg[:, :, HR:ROPE], sin, ALU.mult))
            link(v.tensor_tensor(krt[:, 2], krg[:, :, 0:HR], sin, ALU.mult))
            link(v.tensor_tensor(krt[:, 3], krg[:, :, HR:ROPE], cos, ALU.mult))
            link(v.tensor_tensor(krr[:, :, 0:HR], krt[:, 0], krt[:, 1], ALU.subtract))
            link(v.tensor_tensor(krr[:, :, HR:ROPE], krt[:, 2], krt[:, 3], ALU.add))

            def conv(i):
                dve.wait_ge(bank_free, use0["XBC"] + i + 1)
                if i >= 2:
                    dve.wait_ge(xbc_ready, i - 1)
                for j in range(2):
                    m, u, c = 2 * i + j, ub[:, i % 2, j], cacc[:, i % 2, j]
                    link(v.tensor_scalar(c, u, cwh[:, m, 3:4], cwh[:, m, 4:5], ALU.mult, ALU.add))
                    for d in (1, 2, 3):
                        ins = v.scalar_tensor_tensor(out=c[:, d:T], in0=u[:, 0:T - d], scalar=cwh[:, m, 3 - d:4 - d],
                                                     in1=c[:, d:T], op0=ALU.mult, op1=ALU.add)
                        if j == 0 or d < 3:
                            link(ins)
                ins.then_inc(conv_acc, 1)

            def conv_silu(i):
                dve.wait_ge(conv_t, i + 1)
                v.scalar_tensor_tensor(out=xbcT[:, 2 * i:2 * i + 2, :], in0=tb[:, i % 2], scalar=1.0,
                                       in1=cacc[:, i % 2], op0=ALU.add, op1=ALU.mult).then_inc(xbc_ready, 1)

            def scale_by_dt(i):
                dve.wait_ge(xs_tr, i + 1)
                v.tensor_tensor(xdt[:, :, 256 * i:256 * i + 256].rearrange("p t (h d) -> p t h d", d=HD_SSD),
                                B[2 + i % 2][:, :].rearrange("p (t h d) -> p t h d", t=2, d=HD_SSD),
                                dt2[:, :, 4 * i:4 * i + 4].unsqueeze(3).broadcast_to([P, TT, 4, HD_SSD]),
                                ALU.mult).then_inc(xdt_ready, 1)

            for i in range(12):
                conv(i)
                if i >= 1:
                    conv_silu(i - 1)
                if i == 0:
                    norm_vars("qa")
                    dve.wait_ge(n_rs, 2)
                    norm_scale("qa")
                    norm_vars("kva")
                    dve.wait_ge(n_rs, 3)
                    norm_scale("kva")
                if i == 2:
                    dve.wait_ge(cum_ps, 1)
                    link(v.tensor_copy(acum[:, :, :], B[4][:, 0:64].rearrange("p (t n) -> p t n", t=2)))
                    v.tensor_copy(acumT[:, :], B[4][0:32, 128:384]).then_inc(acumT_sb, 1)
                if 3 <= i < 11:
                    scale_by_dt(i - 3)
            conv_silu(11)

            keep = A("keep")

            def seg_step(i):
                dve.wait_ge(rows_in[i % 2], 16 * (i // 2 + 1))
                if i >= 1:
                    dve.wait_ge(m_ready, i)
                for h in range(4):
                    for tt, (a, b, lo) in enumerate(((0, T, 0), (T, BW, P))):
                        ins = v.tensor_scalar(seg[:, h, a:b], Rb[:, i % 2, h, lo:T],
                                              acum[:, tt, 4 * i + h:4 * i + h + 1], 0.0, ALU.subtract, ALU.min)
                ins.then_inc(seg_ready, 1)

            def m_step(i):
                dve.wait_ge(decay_ready, i + 1)
                if i >= 2:
                    dve.wait_ge(y_ps, i - 1)
                v.tensor_tensor(Mt[:, i % 2], seg[:, :, :], scM[:, i // 2].unsqueeze(1).broadcast_to([P, 4, BW]),
                                ALU.mult).then_inc(m_ready, 1)

            def y_step(i):
                dve.wait_ge(y_ps, i + 1)
                dve.wait_ge(bank_free, use0["Z"] + i + 1)
                for j in range(2):
                    m = 2 * i + j
                    link(v.scalar_tensor_tensor(out=xbcT[:, m, :], in0=xbcT[:, m, :], scalar=A("dskip")[:, m:m + 1],
                                                in1=B[4 + i % 2][:, j * T:(j + 1) * T], op0=ALU.mult, op1=ALU.add))
                v.tensor_tensor(xbcT[:, 2 * i:2 * i + 2, :], xbcT[:, 2 * i:2 * i + 2, :], zs[:, i % 2],
                                ALU.mult).then_inc(y_ready, 1)

            def z_step(i):
                dve.wait_ge(z_t, i + 1)
                if i >= 2:
                    dve.wait_ge(y_ready, i - 1)
                v.scalar_tensor_tensor(out=zs[:, i % 2], in0=tb[:, i % 2], scalar=1.0,
                                       in1=G[(use0["Z"] + i) % 2][:, :].rearrange("p (j t) -> p j t", j=2),
                                       op0=ALU.add, op1=ALU.mult).then_inc(bank_free, 1)

            for i in range(8):
                seg_step(i)
                if i == 0:
                    for g in range(NG_SSD):
                        dve.wait_ge(score_ps, g + 1)
                        v.tensor_tensor(scM[:, g], B[4 + g % 2][:, 0:BW], keep, ALU.mult).then_inc(score_sb, 1)
                    dve.wait_ge(score_sb, NG_SSD)
                m_step(i)
                if i >= 1:
                    y_step(i - 1)
                z_step(i)
            y_step(7)

            c_uq = SEC["UQ"][0]
            hd = lambda t: t.rearrange("p (h d) -> p h d", h=4)
            for n in range(16):
                dve.wait_ge(u_sq, n + 1)
                tt, h0 = n % 2, 4 * (n // 2 % 4)
                bank = G[(use0["UQ"] + n) % 2]
                hs = slice(h0, h0 + 4)
                if n < 8:
                    link(v.tensor_reduce(ssq[:, 0, tt, hs], hd(sqt[:, n % 2, 0:384]), AX_X, ALU.add))
                    v.tensor_tensor(q96[:, tt, hs, :], hd(bank[:, 0:384]),
                                    A("g_q").unsqueeze(1).broadcast_to([P, 4, QK]), ALU.mult).then_inc(bank_free, 1)
                else:
                    link(v.tensor_reduce(ssq[:, 1, tt, hs], hd(sqt[:, n % 2, 0:256]), AX_X, ALU.add))
                    link(v.tensor_tensor(k96[:, tt, hs, 0:NOPE], hd(bank[:, :])[:, :, 0:NOPE],
                                         A("g_k")[:, 0:NOPE].unsqueeze(1).broadcast_to([P, 4, NOPE]), ALU.mult))
                    v.tensor_copy(vS[:, tt, hs, :], hd(bank[:, :])[:, :, NOPE:]).then_inc(bank_free, 1)
            dve.wait_ge(bank_free, use0["GATE_B"])
            link(v.tensor_tensor(ssq[:, 1], ssq[:, 1], sskr[:, :].unsqueeze(2).broadcast_to([P, TT, H_MLA]), ALU.add))
            link(v.tensor_scalar(rqk[:, :, :, :], ssq[:, :, :, :], 1.0 / QK, EPS, ALU.mult, ALU.add))
            v.reciprocal(rqk[:, :, :, :], rqk[:, :, :, :]).then_inc(kq_ss, 1)
            cosb, sinb = (t.unsqueeze(2).broadcast_to([P, TT, H_MLA, HR]) for t in (cos, sin))
            x1, x2 = q96[:, :, :, NOPE:NOPE + HR], q96[:, :, :, NOPE + HR:QK]
            link(v.tensor_tensor(rot[:, 0], x1, sinb, ALU.mult))
            link(v.tensor_tensor(rot[:, 1], x2, sinb, ALU.mult))
            link(v.tensor_tensor(x1, x1, cosb, ALU.mult))
            link(v.tensor_tensor(x2, x2, cosb, ALU.mult))
            link(v.tensor_tensor(x1, x1, rot[:, 1], ALU.subtract))
            link(v.tensor_tensor(x2, x2, rot[:, 0], ALU.add))
            dve.wait_ge(kq_rs, 1)
            link(v.tensor_scalar(qsc[:, 0], rqk[:, 0], QK ** -0.5, None, ALU.mult))
            link(v.tensor_scalar(qsc[:, 1], rqk[:, 0], -QK ** -0.5, None, ALU.mult))
            for tt in range(TT):
                rk = rqk[:, 1, tt, :].unsqueeze(2)
                link(v.tensor_tensor(k96[:, tt, :, 0:NOPE], k96[:, tt, :, 0:NOPE], rk.broadcast_to([P, H_MLA, NOPE]),
                                     ALU.mult))
                ins = v.tensor_tensor(k96[:, tt, :, NOPE:QK], krr[:, tt, :].unsqueeze(1).broadcast_to([P, H_MLA, ROPE]),
                                      rk.broadcast_to([P, H_MLA, ROPE]), ALU.mult)
                if tt == 0:
                    link(ins)
            ins.then_inc(kq_ready, 1)
            dve.wait_ge(kq_ready, 1)

            causal = A("causal")

            def head_step(s):
                h = s - 1
                if 0 <= h < H_MLA:
                    dve.wait_ge(s_ps, h + 1)
                    if h >= 2:
                        dve.wait_ge(pt_ps, h - 1)
                    m, b = mx[:, h % 2, :], B[2 + h % 2]
                    for tt, (lo, hi) in enumerate(((0, P), (P, BW))):
                        link(v.tensor_tensor_reduce(out=Sm[:, h % 2, lo:hi], in0=b[:, lo:hi], in1=causal[:, lo:hi],
                                                    scale=1.0, scalar=NEG, op0=ALU.add, op1=ALU.max,
                                                    accum_out=m[:, tt:tt + 1]))
                    v.tensor_tensor(m[:, 2:4], m[:, 0:2], qsc[:, 1, :, h], ALU.mult).then_inc(sm_ready, 1)
                h = s - 2
                if 0 <= h < H_MLA:
                    dve.wait_ge(pt_ps, h + 1)
                    if h >= 2:
                        dve.wait_ge(o_ps, h - 1)
                    v.tensor_copy(PTs[:, h % 2, :], B[4][:, 0:BW]).then_inc(pt_sb, 1)
                h = s - 1
                if 0 <= h < H_MLA:
                    dve.wait_ge(p_exp, 2 * h + 2)
                    m = mx[:, h % 2, :]
                    link(v.reciprocal(m[:, 6:8], m[:, 4:6]))
                    link(v.tensor_scalar(Sm[:, h % 2, 0:P], Sm[:, h % 2, 0:P], m[:, 6:7], None, ALU.mult))
                    v.tensor_scalar(Sm[:, h % 2, P:BW], Sm[:, h % 2, P:BW], m[:, 7:8], None,
                                    ALU.mult).then_inc(p_ready, 1)
                h = s - 3
                if 0 <= h < H_MLA and h % 2:
                    dve.wait_ge(o_hi, h // 2 + 1)
                    v.tensor_tensor(olo[:, h // 2, :], B[5][:, 0:T], ohi[:, h // 2, :],
                                    ALU.subtract).then_inc(o_lo, 1)

            step = 0
            for i in range(7):
                if i == 0:
                    norm_vars("y")
                    dve.wait_ge(n_rs, 4)
                    norm_scale("y", range(0, 2))
                    continue
                head_step(step)
                head_step(step + 1)
                step += 2
                if i < 4:
                    norm_scale("y", range(2 * i, 2 * i + 2))
            dve.wait_ge(bank_free, use0["SSDP"])
            for i in range(8):
                for _ in range(1 if i == 0 else 2):
                    if step < H_MLA + 3:
                        head_step(step)
                        step += 1
                dve.wait_ge(chunk_used, SEC["SSDP"][0] + i + 1)
                v.scalar_tensor_tensor(out=gT[:, i, :], in0=gT[:, i, :], scalar=1.0,
                                       in1=G[(use0["SSDP"] + i) % 2][:, 0:T], op0=ALU.add,
                                       op1=ALU.mult).then_inc(bank_free, 1)
            two = lambda t: t.rearrange("p (j t) -> p j t", j=2)
            for i in range(4):
                dve.wait_ge(chunk_used, SEC["MLAP"][0] + i + 1)
                gm, ma = gT[:, 8 + 2 * i:10 + 2 * i, :], mixa[:, 2 * i:2 * i + 2, :]
                v.scalar_tensor_tensor(out=gm, in0=gm, scalar=1.0, in1=two(G[(use0["MLAP"] + i) % 2][:, :]),
                                       op0=ALU.add, op1=ALU.mult).then_inc(bank_free, 1)
                dve.wait_ge(bank_free, use0["MLAP"] + i + 1)
                if i == 0:
                    dve.wait_ge(qkT_sb, H_MLA)
                v.tensor_tensor(ma, gT[:, 2 * i:2 * i + 2, :], gm, ALU.add).then_inc(mix_ready, 1)
                dve.wait_ge(mix_hi, i + 1)
                v.tensor_tensor(h_lo[:, 2 * i:2 * i + 2, :], ma, h_hi[:, 2 * i:2 * i + 2, :],
                                ALU.subtract).then_inc(mix_lo, 1)
            for i in range(4):
                dve.wait_ge(chunk_used, SEC["WO"][0] + i + 1)
                x = xT[:, 2 * i:2 * i + 2, :]
                v.scalar_tensor_tensor(out=x, in0=two(G[(use0["WO"] + i) % 2][:, :]), scalar=0.5, in1=x, op0=ALU.mult,
                                       op1=ALU.add).then_inc(bank_free, 1)
            norm_vars("ffn")
            dve.wait_ge(n_rs, 5)
            norm_scale("ffn")

            u0 = use0["UP"]

            def ffn_conv(k, par, it=None):
                kk = k if it is None else it * 4 + k
                dve.wait_ge(bank_free, kk + (u0 + 1))
                if k >= 2 or it is not None:
                    dve.wait_ge(f_g, kk - 1)
                for j in range(2):
                    w = fwh[:, bass.ds(kk * 2 + j, 1), :].rearrange("p a b -> p (a b)")
                    u, c = fub[:, par, j], facc[:, par, j]
                    link(v.tensor_scalar(c, u, w[:, 2:3], w[:, 3:4], ALU.mult, ALU.add))
                    for d in (1, 2):
                        ins = v.scalar_tensor_tensor(out=c[:, d:T], in0=u[:, 0:T - d], scalar=w[:, 2 - d:3 - d],
                                                     in1=c[:, d:T], op0=ALU.mult, op1=ALU.add)
                        if j == 0 or d == 1:
                            link(ins)
                ins.then_inc(f_acc, 1)

            def ffn_product(k, par, it=None):
                kk = k if it is None else it * 4 + k
                dve.wait_ge(f_t, kk + 1)
                link(v.scalar_tensor_tensor(out=ftg[:, par], in0=ftg[:, par], scalar=1.0, in1=facc[:, par, 0],
                                            op0=ALU.add, op1=ALU.mult))
                if k >= 2 or it is not None:
                    dve.wait_ge(f_lo, kk - 1)
                v.tensor_tensor(fg[:, par], ftg[:, par], facc[:, par, 1], ALU.mult).then_inc(f_g, 1)
                dve.wait_ge(f_hi, kk + 1)
                v.tensor_tensor(g_lo[:, kk, :], fg[:, par], g_hi[:, kk, :], ALU.subtract).then_inc(f_lo, 1)

            ffn_conv(0, 0)
            ffn_conv(1, 1)
            ffn_product(0, 0)
            base = own.n
            with dve.Fori(0, 4, 1) as i:
                own.n = i * (4 * FFN_LINKS) + base
                for j in range(4):
                    k = 2 + j
                    ffn_conv(k, k % 2, i)
                    ffn_product(k - 1, (k - 1) % 2, i)
            own.n = base + 16 * FFN_LINKS
            for k in range(18, 22):
                ffn_conv(k, k % 2)
                ffn_product(k - 1, (k - 1) % 2)
            ffn_product(21, 1)
            u0, c0 = use0["DOWN"], SEC["DOWN"][0]
            with dve.Fori(0, 4, 1) as i:
                for j in range(2):
                    dve.wait_ge(chunk_used, i * 4 + (c0 + 2 * j + 2))
                    x = xT[:, i * 2 + j, :]
                    v.tensor_tensor(x, G[(u0 + j) % 2][:, 0:T], x, ALU.add).then_inc(bank_free, 1)

            dve.wait_ge(pb_in, 16)
            dve.wait_ge(bank_free, use0["CKV"])
            norm_vars("x2")
            dve.wait_ge(n_rs, 6)
            norm_scale("x2")
            dve.wait_ge(n_hi, norm_end("x2"))
            link(v.memset(bT[:, :, :, :, :], 0.0))
            dve.wait_ge(cblk_in, 64)
            for kv, name in enumerate(("pos_k", "pos_v")):
                tokens = cblk[:, 3 * kv:3 * kv + 3, :].rearrange("p g (n b two) -> p g n b two", b=8, two=2)
                for half_block in range(2):
                    ins = v.tensor_tensor(
                        bT[:, kv, 8 * half_block:8 * half_block + 8, :, 0:NC].rearrange("p b g n -> p g n b"),
                        tokens[:, :, half_block:half_block + NC, :, 0],
                        Bp(name)[:, 8 * half_block:8 * half_block + 8].unsqueeze(1).unsqueeze(1)
                        .broadcast_to([P, 3, NC, 8]), ALU.add)
                    if kv + half_block < 2:
                        link(ins)
            ins.then_inc(b_ready, 1)

            cos32, sin32 = (Bp(n).rearrange("p (t n) -> p t n", t=2) for n in ("cos32", "sin32"))
            HH = HD // 2

            def rotate(x, n, cosb, sinb, t0, t1):
                x1, x2 = x[..., 0:HH], x[..., HH:HD]
                link(v.tensor_tensor(t0, x1, sinb, ALU.mult))
                link(v.tensor_tensor(t1, x2, sinb, ALU.mult))
                link(v.tensor_tensor(x1, x1, cosb, ALU.mult))
                link(v.tensor_tensor(x2, x2, cosb, ALU.mult))
                link(v.tensor_tensor(x1, x1, t1, ALU.subtract))
                link(v.tensor_tensor(x2, x2, t0, ALU.add))

            def token_heads(n, name, i, heads, head0, gain):
                u = use0[name] + i
                dve.wait_ge(t_sq, n + 1)
                src = G[u % 2][:, :].rearrange("p (t h d) -> p t h d", t=2, d=HD)
                c0 = i * 256 if name == "TM_A" else 1536 + i * 256
                dst = tm[:, :, c0:c0 + 256].rearrange("p t (h d) -> p t h d", d=HD)
                v.tensor_reduce(ss2[:, :, head0:head0 + heads], sqt2[:, n % 2].rearrange("p (t h) d -> p t h d", t=2)
                                [:, :, 0:heads, :], AX_X, ALU.add).then_inc(t_free, 1)
                if heads < 4:
                    link(v.tensor_copy(dst[:, :, heads:4, :], src[:, :, heads:4, :]))
                v.tensor_tensor(dst[:, :, 0:heads, :], src[:, :, 0:heads, :], gain, ALU.mult).then_inc(bank_free, 1)
                dve.wait_ge(bank_free, u + 1)
                bc = lambda t: t.unsqueeze(2).broadcast_to([P, TT, heads, HH])
                rotate(dst[:, :, 0:heads, :], heads, bc(cos32), bc(sin32), rt[:, 0, :, 0:heads], rt[:, 1, :, 0:heads])

            def same_gain(name):
                return Bp(name).unsqueeze(1).unsqueeze(1).broadcast_to([P, TT, 4, HD])

            def k_gain(h0, n):
                return (Bp("g_k")[:, h0 * HD:(h0 + n) * HD].rearrange("p (h d) -> p h d", d=HD).unsqueeze(1)
                        .broadcast_to([P, TT, n, HD]))

            for i in range(6):
                if i < 3:
                    token_heads(i, "TM_A", i, 4, 4 * i, same_gain("g_qa2"))
                elif i < 5:
                    token_heads(i, "TM_A", i, 4 if i == 3 else 2, 4 * i, k_gain(4 * (i - 3), 4 if i == 3 else 2))
                else:
                    u = use0["TM_A"] + i
                    dve.wait_ge(chunk_used, SEC["TM_A"][0] + i + 1)
                    v.tensor_copy(tm[:, :, 1280:1536], G[u % 2][:, :].rearrange("p (t n) -> p t n", t=2)
                                  ).then_inc(bank_free, 1)
                if i == 3:
                    dve.wait_ge(b_hi, 1)
                    flat = lambda t: t[:, :, :, :, :].rearrange("p a b g n -> p (a b g n)")
                    v.tensor_tensor(flat(bT_lo), flat(bT), flat(bT_hi), ALU.subtract).then_inc(b_lo, 1)

            def roots(lo, hi, n, k_lo, k_cols):
                link(v.tensor_scalar(ss2[:, :, lo:hi], ss2[:, :, lo:hi], 1.0 / HD, EPS, ALU.mult, ALU.add))
                v.reciprocal(ss2[:, :, lo:hi], ss2[:, :, lo:hi]).then_inc(ss_ready, 1)
                dve.wait_ge(rs_ready, n)
                link(v.tensor_scalar(qs2[:, 0, :, lo:hi], r2[:, :, lo:hi], HD ** -0.5, None, ALU.mult))
                link(v.tensor_scalar(qs2[:, 1, :, lo:hi], r2[:, :, lo:hi], -HD ** -0.5, None, ALU.mult))
                k = tm[:, :, k_cols:k_cols + (hi - k_lo) * HD].rearrange("p t (h d) -> p t h d", d=HD)
                v.tensor_tensor(k, k, r2[:, :, k_lo:hi].unsqueeze(3).broadcast_to([P, TT, hi - k_lo, HD]),
                                ALU.mult).then_inc(k_ready, 1)

            dve.wait_ge(bank_free, use0["TM_G"] + 1)
            link(v.tensor_scalar(gnsa[:, :, :], gnsa[:, :, :], 0.5, 0.5, ALU.mult, ALU.add))
            dve.wait_ge(bank_free, use0["CW1"] + 4)
            link(v.tensor_tensor(hid[:, 1], hid[:, 0], hid[:, 0], ALU.mult))
            link(v.tensor_scalar(hid[:, 1], hid[:, 1], 0.044715, 1.0, ALU.mult, ALU.add))
            v.tensor_tensor(hid[:, 1], hid[:, 1], hid[:, 0], ALU.mult).then_inc(ge_in, 1)
            dve.wait_ge(ge_t, 1)
            link(v.tensor_scalar(hid[:, 1], hid[:, 1], 0.5, 0.5, ALU.mult, ALU.add))
            v.tensor_tensor(hid[:, 0], hid[:, 0], hid[:, 1], ALU.mult).then_inc(ge_done, 1)
            roots(0, 18, 1, 12, 768)

            def compressed_keys():
                dve.wait_ge(c_ps, 1)
                ps = B[0][0:CG, 0:6 * HD].rearrange("p (k g d) -> p k g d", k=2, g=3)
                link(v.tensor_copy(vc[:, :, :], ps[:, 1]))
                link(v.tensor_copy(cn[:, 0], ps[:, 0]))
                link(v.tensor_tensor(cn[:, 1], cn[:, 0], cn[:, 0], ALU.mult))
                link(v.tensor_reduce(ssc[:, 0, :], cn[:, 1], AX_X, ALU.add))
                link(v.tensor_scalar(ssc[:, 0, :], ssc[:, 0, :], 1.0 / HD, EPS, ALU.mult, ALU.add))
                v.reciprocal(ssc[:, 0, :], ssc[:, 0, :]).then_inc(c_ss, 1)
                dve.wait_ge(c_rs, 1)
                link(v.tensor_tensor(cn[:, 0], cn[:, 0], ssc[:, 1, :].unsqueeze(2).broadcast_to([CG, 3, HD]),
                                     ALU.mult))
                link(v.tensor_tensor(cn[:, 0], cn[:, 0], Bp("g_kc")[0:CG].unsqueeze(1).broadcast_to([CG, 3, HD]),
                                     ALU.mult))
                bc = lambda name: Bp(name)[0:CG].unsqueeze(1).broadcast_to([CG, 3, HH])
                rotate(cn[:, 0], 3, bc("cosc"), bc("sinc"), cn[:, 1, :, 0:HH], cn[:, 2, :, 0:HH])

            any_key, no_key, cmp_add = Bp("cmp_any"), Bp("cmp_none"), Bp("cmp_add")

            def nsa_step(s):
                h = s - 1
                if 0 <= h < H_NSA:
                    dve.wait_ge(ns_ps, h + 1)
                    if h >= 2:
                        dve.wait_ge(npt_ps, h - 1)
                        dve.wait_ge(nq_ps, h + 1)
                    m = m2[:, h % 2]
                    for b, src, s0, c0, w0, w1, mask in ((1, B[1], 0, 0, P, T, causal), (2, B[2], 0, BW, P, T, causal),
                                                         (0, B[2], BW, 768, CG, CG, cmp_add)):
                        for tt in range(TT):
                            w, o = (w1 if tt else w0), tt * w0
                            link(v.tensor_tensor_reduce(
                                out=S2[:, h % 2, c0 + o:c0 + o + w], in0=src[:, s0 + o:s0 + o + w],
                                in1=mask[:, o:o + w], scale=1.0, scalar=NEG, op0=ALU.add, op1=ALU.max,
                                accum_out=m[:, 0, 2 * b + tt:2 * b + tt + 1]))
                    link(v.tensor_tensor(m[:, 0, 0:2], m[:, 0, 0:2], any_key, ALU.mult))
                    v.tensor_tensor(m[:, 1].rearrange("p (b t) -> p b t", t=2),
                                    m[:, 0].rearrange("p (b t) -> p b t", t=2),
                                    qs2[:, 1, :, h].unsqueeze(1).broadcast_to([P, 3, TT]),
                                    ALU.mult).then_inc(nm_ready, 1)
                h = s - 2
                if 0 <= h < H_NSA:
                    dve.wait_ge(npt_ps, h + 1)
                    if h >= 2:
                        dve.wait_ge(no_ps, h - 1)
                    link(v.tensor_copy(PT2[:, 2 * (h % 2), :], B[3][:, 0:BW]))
                    v.tensor_copy(PT2[:, 2 * (h % 2) + 1, :], B[4][:, 0:BW]).then_inc(npt_sb, 1)
                h = s - 1
                if 0 <= h < H_NSA:
                    dve.wait_ge(n_exp, 6 * h + 6)
                    m = m2[:, h % 2]
                    link(v.tensor_tensor(m[:, 2, 0:2], m[:, 2, 0:2], no_key, ALU.add))
                    link(v.reciprocal(m[:, 3], m[:, 2]))
                    link(v.tensor_tensor(m[:, 3].rearrange("p (b t) -> p t b", t=2),
                                         m[:, 3].rearrange("p (b t) -> p t b", t=2),
                                         gnsa[:, :, 3 * h:3 * h + 3], ALU.mult))
                    for b, c0, w0, w1 in ((1, 0, P, T), (2, BW, P, T), (0, 768, CG, CG)):
                        for tt in range(TT):
                            w, o = (w1 if tt else w0), c0 + tt * w0
                            x = S2[:, h % 2, o:o + w]
                            ins = v.tensor_scalar(x, x, m[:, 3, 2 * b + tt:2 * b + tt + 1], None, ALU.mult)
                    ins.then_inc(np_ready, 1)
                h = s - 3
                if 0 <= h < H_NSA and h % 2:
                    dve.wait_ge(no_hi, h // 2 + 1)
                    v.tensor_tensor(o2_lo[:, h // 2, :], B[5][:, 0:T], o2_hi[:, h // 2, :],
                                    ALU.subtract).then_inc(no_lo, 1)

            dil_mask = Bp("dil")

            def dil_step(s):
                u = s - 1
                if 0 <= u < H_DIL:
                    hh, g = u // 3, u % 3
                    dve.wait_ge(ds_ps, u + 1)
                    if g == 0 and hh >= 2:
                        dve.wait_ge(dpt_ps, 3 * hh - 3)
                    if u == 0:
                        dve.wait_ge(npt_ps, H_NSA)
                        dve.wait_ge(nq_ps, H_NSA + 2)
                    m = m2[:, hh % 2]
                    for tt, (a, b) in enumerate(((0, P), (P, BW))):
                        link(v.tensor_tensor_reduce(
                            out=S2[:, hh % 2, g * BW + a:g * BW + b], in0=B[1 + u % 2][:, a:b],
                            in1=dil_mask[:, g * BW + a:g * BW + b], scale=1.0, scalar=NEG, op0=ALU.add, op1=ALU.max,
                            accum_out=m[:, 0, 2 * g + tt:2 * g + tt + 1]))
                    v.tensor_tensor(m[:, 1, 2 * g:2 * g + 2], m[:, 0, 2 * g:2 * g + 2],
                                    qs2[:, 1, :, 18 + g * DH + hh], ALU.mult).then_inc(dm_part, 1)
                    if g == 2:
                        dve.wait_ge(dm_part, u + 1)
                        v.tensor_reduce(md[:, 0, :], m[:, 1].rearrange("p (b t) -> p t b", t=2), AX_X,
                                        ALU.min).then_inc(dm_ready, 1)
                u = s - 5
                if 0 <= u < H_DIL:
                    dve.wait_ge(dpt_ps, u + 1)
                    if u >= 2:
                        dve.wait_ge(do_ps, u - 1)
                    if u == 0:
                        dve.wait_ge(no_ps, H_NSA)
                    v.tensor_copy(PT2[:, u % 2, :], B[3 + u % 2][:, 0:BW]).then_inc(dpt_sb, 1)
                u = s - 1
                if 0 <= u < H_DIL and u % 3 == 2:
                    hh = u // 3
                    dve.wait_ge(d_exp, 6 * hh + 6)
                    m = m2[:, hh % 2]
                    link(v.tensor_reduce(md[:, 1, :], m[:, 2].rearrange("p (b t) -> p t b", t=2), AX_X, ALU.add))
                    link(v.reciprocal(md[:, 1, :], md[:, 1, :]))
                    x = S2[:, hh % 2, :].rearrange("p (g n) -> p g n", g=3)
                    link(v.tensor_scalar(x[:, :, 0:P], x[:, :, 0:P], md[:, 1, 0:1], None, ALU.mult))
                    v.tensor_scalar(x[:, :, P:BW], x[:, :, P:BW], md[:, 1, 1:2], None,
                                    ALU.mult).then_inc(dp_ready, 1)
                u = s - 6
                if 0 <= u < H_DIL and u % 6 == 5:
                    dve.wait_ge(do_hi, u // 6 + 1)
                    v.tensor_tensor(o2_lo[:, 6 + u // 6, :], B[5][:, 0:T], o2_hi[:, 6 + u // 6, :],
                                    ALU.subtract).then_inc(do_lo, 1)

            nsa = dil = 0
            for i in range(9):
                if i < 6:
                    token_heads(5 + i, "TM_B", i, 4, 18 + 4 * i, same_gain("g_qb" if i < 3 else "g_kb"))
                else:
                    u = use0["TM_B"] + i
                    dve.wait_ge(chunk_used, SEC["TM_B"][0] + i + 1)
                    v.tensor_copy(tm[:, :, 1536 + 256 * i:1792 + 256 * i], G[u % 2][:, :]
                                  .rearrange("p (t n) -> p t n", t=2)).then_inc(bank_free, 1)
                if i == 0:
                    compressed_keys()
                    dve.wait_ge(dve_own, own.n)
                    v.memset(cn[:, 3], 0.0).then_inc(cn_ready, 1)
                if i >= 3:
                    nsa_step(nsa)
                    nsa_step(nsa + 1)
                    nsa += 2
            for i in range(8):
                for j in range(2):
                    if i == 0 and j == 1:
                        roots(18, 42, 2, 30, 2304)
                    if nsa < H_NSA + 3:
                        nsa_step(nsa)
                        nsa += 1
                    else:
                        dil_step(dil)
                        dil += 1
            while dil < H_DIL + 6:
                dil_step(dil)
                dil += 1
            dve.wait_ge(bank_free, use0["OAB"])
            for i in range(4):
                for half_gates in range(2):
                    u = use0["OAB"] + 2 * i + half_gates
                    if half_gates:
                        dve.wait_ge(chunk_used, SEC["OAB"][0] + i + 1)
                    else:
                        dve.wait_ge(oab_ps, i + 1)
                    g = gT2[:, 8 * half_gates + 2 * i:8 * half_gates + 2 * i + 2, :]
                    v.scalar_tensor_tensor(out=g, in0=g, scalar=1.0, in1=two(G[u % 2][:, :]), op0=ALU.add,
                                           op1=ALU.mult).then_inc(bank_free, 1)
                dve.wait_ge(bank_free, u + 1)
                ma = mix2[:, 2 * i:2 * i + 2, :]
                v.tensor_tensor(ma, gT2[:, 2 * i:2 * i + 2, :], gT2[:, 8 + 2 * i:10 + 2 * i, :],
                                ALU.add).then_inc(mix2_ready, 1)
                dve.wait_ge(mix2_hi, i + 1)
                v.tensor_tensor(h_lo[:, 2 * i:2 * i + 2, :], ma, h_hi[:, 2 * i:2 * i + 2, :],
                                ALU.subtract).then_inc(mix2_lo, 1)
            for i in range(4):
                dve.wait_ge(chunk_used, SEC["WOUT"][0] + i + 1)
                x = xT[:, 2 * i:2 * i + 2, :]
                v.scalar_tensor_tensor(out=x, in0=two(G[(use0["WOUT"] + i) % 2][:, :]), scalar=0.5, in1=x,
                                       op0=ALU.mult, op1=ALU.add).then_inc(bank_free, 1)
            norm_vars("ffn2")
            dve.wait_ge(n_rs, 7)
            norm_scale("ffn2")
            u0 = use0["UP2"]

            def square(k, par, it=None):
                kk = k if it is None else it * 4 + k
                dve.wait_ge(bank_free, kk + (u0 + 1))
                if k >= 2 or it is not None:
                    dve.wait_ge(sq_lo, kk - 1)
                v.tensor_tensor(ssqr[:, par], srl[:, par], srl[:, par], ALU.mult).then_inc(sq_f, 1)
                dve.wait_ge(sq_hi, kk + 1)
                v.tensor_tensor(s_lo[:, bass.ds(kk * 2, 2), :], ssqr[:, par], s_hi[:, bass.ds(kk * 2, 2), :],
                                ALU.subtract).then_inc(sq_lo, 1)

            for k in range(2):
                square(k, k % 2)
            with dve.Fori(0, 3, 1) as i:
                for j in range(4):
                    square(2 + j, j % 2, i)
            for k in range(14, 16):
                square(k, k % 2)
            u0, c0 = use0["DOWN2"], SEC["DOWN2"][0]
            with dve.Fori(0, 4, 1) as i:
                for j in range(2):
                    dve.wait_ge(chunk_used, i * 4 + (c0 + 2 * j + 2))
                    x = xT[:, i * 2 + j, :]
                    v.tensor_tensor(x, G[(u0 + j) % 2][:, 0:T], x, ALU.add).then_inc(bank_free, 1)


def kernel(**inputs):
    import concourse.bacc as bacc
    from concourse.bass_utils import run_bass_kernel_spmd

    a = {n: np.asarray(v) for n, v in inputs.items()}
    x = a["x"].reshape(T, D)
    pa, pb = pack_params(a)
    arrays = {"wstream": pack_stream(a), "x_t": np.ascontiguousarray(_rows(x.T, KD)), "params_a": pa, "params_b": pb}
    nc = bacc.Bacc("TRN2", target_bir_lowering=False, num_devices=1)
    args = [nc.dram_tensor(n, v.shape, F32, kind="ExternalInput").ap() for n, v in arrays.items()]
    out = nc.dram_tensor("out_t", (P, KD, T), F32, kind="ExternalOutput").ap()
    blocks_kernel(nc, *args, out)
    r = run_bass_kernel_spmd(nc, [arrays], core_ids=[0])
    y = r.results[0]["out_t"]
    return np.ascontiguousarray(y.transpose(2, 1, 0).reshape(1, T, D))
```

```python
from contextlib import ExitStack

import concourse.bass as bass
import numpy as np
from concourse import mybir

F32 = mybir.dt.float32
F32R = mybir.dt.float32r
ALU = mybir.AluOpType
ACT = mybir.ActivationFunctionType
AX_X = mybir.AxisListType.X

P = 128
T = 256
TT = T // P
D = 1024
KD = D // P
EPS = 1e-6
NEG = -1e30

DI, NH_SSD, HD_SSD, NG_SSD, NS = 2048, 32, 64, 4, 128
XBC = DI + 2 * NG_SSD * NS
QL, KVL, H_MLA, NOPE, ROPE, VD = 256, 128, 16, 64, 32, 64
QK = NOPE + ROPE
FF = 2816
OFF_XBC, OFF_DT = DI, DI + XBC
OFF_QA = OFF_DT + NH_SSD
OFF_KVA = OFF_QA + QL
OFF_KR = OFF_KVA + KVL
OFF_G = OFF_KR + ROPE

H_NSA, G_NSA, HPG, HD = 12, 3, 4, 64
NC = 15
CG = 16
H_DIL, DG, DH = 12, 3, 4
FF2 = 4096
DIL = ((128, 1), (512, 4), (2048, 16))

SLOT = 2048
SLOTS, AHEAD = 4, 2
BW = 384

_SIZES = [("A", 1, 1536), ("QA", 1, 2048), ("XBC", 12, 2048), ("Z", 8, 2048), ("GATE_A", 1, 2048),
          ("UQ", 2, 1536), ("UKV", 1, 2048), ("GATE_B", 7, 2048), ("SSDP", 8, 2048), ("MLAP", 4, 2048), ("WO", 4, 2048), ("UP", 22, 2048),
          ("DOWN", 16, 1408), ("CKV", 2, 2048), ("TM_A", 6, 2048), ("TM_G", 1, 512), ("CW1", 4, 2048),
          ("TM_B", 9, 2048), ("GATE2", 8, 2048),
          ("OAB", 4, 2048), ("WOUT", 4, 2048), ("UP2", 16, 2048), ("DOWN2", 16, 2048)]
SEC = {}
_c = 0
for _name, _n, _used in _SIZES:
    SEC[_name] = (_c, _n, _used)
    _c += _n
NCHUNK = _c


def _rows(w, kt):
    return w.reshape(kt, P, -1).transpose(1, 0, 2)


def _chunks(w, kt, cols):
    r = _rows(w, kt)
    n = r.shape[2] // cols
    return r.reshape(P, kt, n, cols).transpose(2, 0, 1, 3).reshape(n, P, kt * cols)


def pack_stream(a):
    w1, w2 = a["w_in"][0], a["w_in_2"][0]
    out = np.zeros((NCHUNK, P, SLOT), np.float32)

    def put(sec, part, at=0):
        c0 = SEC[sec][0] + at
        out[c0:c0 + part.shape[0], :, :part.shape[2]] = part

    first = np.concatenate([w1[:, OFF_DT:OFF_QA], w1[:, OFF_KR:OFF_G], w1[:, OFF_KVA:OFF_KR]], axis=1)
    put("A", _chunks(first, KD, 192))
    put("QA", _chunks(w1[:, OFF_QA:OFF_KVA], KD, 256))
    put("XBC", _chunks(w1[:, OFF_XBC:OFF_DT], KD, 256))
    put("Z", _chunks(w1[:, :DI], KD, 256))
    put("UQ", _chunks(a["w_uq"][0], 2, 768))
    put("UKV", _chunks(a["w_ukv"][0], 1, 2048))
    gates = _chunks(w1[:, OFF_G:], KD, 256)
    put("GATE_A", gates[:1])
    put("GATE_B", gates[1:])
    put("SSDP", _chunks(a["w_ssd_proj"][0], 16, 128))
    put("MLAP", _chunks(a["w_mla_proj"][0], KD, 256))
    put("WO", _chunks(a["w_o"][0], KD, 256))
    up = a["w_up"][0].reshape(D, 2, FF // P, P).transpose(0, 2, 1, 3).reshape(D, 2 * FF)
    put("UP", _chunks(up, KD, 256))
    dn = _rows(a["w_down"][0], 22).reshape(P, 2, 11, KD, P).transpose(3, 1, 0, 2, 4).reshape(16, P, 11 * P)
    put("DOWN", dn)
    put("CKV", _chunks(w2[:, 768:1024], KD, 256))
    put("CKV", _chunks(w2[:, 1024:1152], KD, 128), 1)
    for n, w in enumerate((a["cmp_k_w1_2"][0], a["cmp_v_w1_2"][0])):
        put("CW1", _chunks(w[:1024], KD, 256), 2 * n)
        put("CW1", _chunks(w[1024:], KD, 256), 2 * n + 1)
    tm = np.concatenate([w2[:, 0:768], w2[:, 1152:1344], w2[:, 1536:1728], w2[:, 1344:1536], w2[:, 1728:1920],
                         w2[:, 1956:4260]], axis=1)
    tm = _chunks(tm, KD, 256)
    put("TM_A", tm[:6])
    put("TM_B", tm[6:])
    g = np.zeros((D, 64), np.float32)
    g[:, :36] = w2[:, 1920:1956]
    put("TM_G", _chunks(g, KD, 64))
    put("GATE2", _chunks(w2[:, 4260:], KD, 256))
    put("OAB", _chunks(np.concatenate([a["w_o_a_2"][0], a["w_o_b_2"][0]], axis=0), KD, 256))
    put("WOUT", _chunks(a["w_out_2"][0], KD, 256))
    put("UP2", _chunks(a["w_up_2"][0], KD, 256))
    dn = _rows(a["w_down_2"][0], 32).reshape(P, 2, 16, KD, P).transpose(3, 1, 0, 2, 4).reshape(16, P, 16 * P)
    put("DOWN2", dn)
    return out


def _col(v, tiles):
    return v.reshape(tiles, P).T


def _bc(v):
    return np.broadcast_to(v.reshape(1, -1), (P, v.size))


def _tables(dim, pos, power=False):
    inv = np.float32(1.0) / (np.float32(10000.0) ** (np.arange(0, dim, 2, dtype=np.float32) / np.float32(dim)))
    if power:
        inv = np.power(np.float32(10000.0), -np.arange(dim // 2, dtype=np.float32) / np.float32(dim // 2))
    ang = np.asarray(pos, np.float32)[:, None] * inv[None, :].astype(np.float32)
    return np.cos(ang).astype(np.float32), np.sin(ang).astype(np.float32)


def _tok(t):
    return t.reshape(TT, P, -1).transpose(1, 0, 2).reshape(P, -1)


def _blocks(m):
    return np.concatenate([m[:P, :P], m[P:, :]], axis=1)


PA, PB = {}, {}


def pack_params(a):
    q, k = np.arange(T)[:, None], np.arange(T)[None, :]
    tri = (np.arange(P)[:, None] <= np.arange(P)[None, :]).astype(np.float32)
    one = np.ones((P, P), np.float32)
    c16, s16 = _tables(ROPE, np.arange(T))
    add = lambda ok: np.where(ok, 0.0, NEG).astype(np.float32)
    cw = a["conv_ssd_w"][0].reshape(4, 24, P).transpose(2, 1, 0).reshape(P, -1)
    fw = a["conv_ffn_w"][0].reshape(3, 2, 22, P).transpose(3, 2, 1, 0).reshape(P, -1)
    fb = a["conv_ffn_b"][0].reshape(2, 22, P).transpose(2, 1, 0).reshape(P, -1)
    ds = np.repeat(a["d_skip"][0], HD_SSD)
    early = [
        ("eps", _bc(np.array([EPS, 4 * EPS], np.float32))), ("g_mix", _col(a["norm_mix_g"][0], KD)), ("ones", one), ("ident", np.eye(P, dtype=np.float32)),
        ("cw", cw), ("cb", _col(a["conv_ssd_b"][0], 24)), ("g_qa", _col(a["q_a_norm_g"][0], 2)),
        ("g_kva", _col(a["kv_a_norm_g"][0], 1)), ("dtb", _bc(a["dt_bias"][0])), ("alog", _bc(a["a_log"][0])),
        ("keep", np.concatenate([tri, one, tri], axis=1)), ("dskip", _col(ds, 16)),
        ("g_ssd", _col(a["ssd_norm_g"][0], 16)), ("gate_b", _col(a["gate_b"][0], 16)),
        ("g_q", _bc(a["q_norm_g"][0])), ("g_k", _bc(a["k_norm_g"][0])), ("cos16", _tok(c16)), ("sin16", _tok(s16)),
        ("causal", _blocks(add(k <= q))), ("g_ffn", _col(a["norm_ffn_g"][0], KD)), ("fw", fw), ("fb", fb),
        ("g1", _col(a["norm1_g_2"][0], KD)), ("g2", _col(a["norm2_g_2"][0], KD)),
    ]
    cend = np.arange(CG) * 16 + 31
    ok = (cend[None, :] <= np.arange(T)[:, None]) & (np.arange(CG)[None, :] < NC)
    c32, s32 = _tables(HD, np.arange(T), True)
    cc, sc = _tables(HD, cend, True)
    pad = lambda t: np.concatenate([t, np.zeros((P - CG, t.shape[1]), np.float32)], axis=0)
    pos = lambda v: v.reshape(16, 2 * HD).T
    late = [
        ("pos_k", pos(a["cmp_k_pos_2"][0])), ("pos_v", pos(a["cmp_v_pos_2"][0])),
        ("w2_k", _rows(a["cmp_k_w2_2"][0], 2).reshape(P, -1)), ("w2_v", _rows(a["cmp_v_w2_2"][0], 2).reshape(P, -1)),
        ("g_kc", _bc(a["k_norm_cmp_2"][0])), ("g_qa2", _bc(a["q_norm_a_2"][0])), ("g_k", _bc(np.concatenate(
            [np.tile(a["k_norm_slc_2"][0], 3), np.tile(a["k_norm_win_2"][0], 3)]))), ("g_qb", _bc(a["q_norm_b_2"][0])), ("g_kb", _bc(a["k_norm_b_2"][0])),
        ("cos32", _tok(c32)), ("sin32", _tok(s32)), ("cosc", pad(cc)), ("sinc", pad(sc)),
        ("cmp_add", _tok(add(ok))), ("cmp_any", _tok(ok.any(1, keepdims=True).astype(np.float32))),
        ("cmp_none", _tok((~ok.any(1, keepdims=True)).astype(np.float32))),
        ("dil", np.concatenate([_blocks(add((k <= q) & (q - k <= w) & ((q - k) % d == 0))) for w, d in DIL], axis=1)),
    ]
    packed = []
    for parts, where in ((early, PA), (late, PB)):
        at = 0
        for name, p in parts:
            where[name] = (at, p.shape[1])
            at += p.shape[1]
        packed.append(np.ascontiguousarray(np.concatenate([p for _, p in parts], axis=1), dtype=np.float32))
    return packed


NORMS = {"x": (8, 8, 2, 8), "qa": (2, 2, 2, 4), "kva": (1, 1, 1, 4), "y": (16, 4, 2, 4), "ffn": (8, 8, 2, 8),
         "x2": (8, 8, 2, 8), "ffn2": (8, 8, 2, 8)}
NORM_AT = {}
_p = _g = 0
for _name, (_t, _gw, _w, _s) in NORMS.items():
    NORM_AT[_name] = (_p, _g)
    _p += _t // _w
    _g += _t // _gw


RS_AT = {"kva": 1}
NORM_ORDER = list(NORMS)


def norm_groups(name):
    t, gw, _, _ = NORMS[name]
    return NORM_AT[name][1] + t // gw


def norm_end(name):
    t, _, w, _ = NORMS[name]
    return NORM_AT[name][0] + t // w


class Tally:

    def __init__(self, eng, sem):
        self.eng, self.sem, self.n = eng, sem, 0

    def sig(self, ins):
        ins.then_inc(self.sem, 1)
        self.n = self.n + 1

    def wait(self):
        self.eng.wait_ge(self.sem, self.n)

    def behind(self, k):
        self.eng.wait_ge(self.sem, self.n - k)

    def link(self, ins):
        self.sig(ins)
        self.wait()


FFN_LINKS = 3


def rotation(own, eng, x1, x2, cosb, sinb, t0, t1, done=None):
    own.sig(eng.tensor_tensor(t0, x1, sinb, ALU.mult))
    own.sig(eng.tensor_tensor(t1, x2, sinb, ALU.mult))
    own.behind(1)
    own.sig(eng.tensor_tensor(x1, x1, cosb, ALU.mult))
    own.behind(1)
    own.sig(eng.tensor_tensor(x2, x2, cosb, ALU.mult))
    own.behind(1)
    own.sig(eng.tensor_tensor(x1, x1, t1, ALU.subtract))
    own.behind(1)
    last = eng.tensor_tensor(x2, x2, t0, ALU.add)
    if done is None:
        own.sig(last)
    else:
        last.then_inc(done, 1)


def blocks_kernel(nc, wstream, x_t, params_a, params_b, out_t):
    with ExitStack() as ctx:
        def sem(name):
            return ctx.enter_context(nc.semaphore(name))

        cursor = [(nc.sbuf_base + 63) // 64 * 64]

        def fixed(name, shape, dt=F32):
            t = nc.alloc_sbuf_tensor_at(name, shape, dt, offset=cursor[0])
            cursor[0] += (int(np.prod(shape[1:])) * 4 + 31) // 32 * 32
            return t

        ring = cursor[0]
        raw = fixed("raw", [P, SLOTS, SLOT])
        w_hi = fixed("w_hi", [P, SLOTS, SLOT], F32R)
        w_lo = nc.alloc_sbuf_tensor_at("w_lo", [P, SLOTS, SLOT], F32R, offset=ring)
        xT = fixed("xT", [P, KD, T])
        h_hi = fixed("h_hi", [P, KD, T], F32R)
        h_lo = fixed("h_lo", [P, KD, T], F32R)
        pa = fixed("pa", [P, params_a.shape[1]])
        rs = fixed("rs", [P, TT, 4])
        ry = fixed("ry", [P, 4, T])
        small = cursor[0]
        expa = fixed("expa", [P, NH_SSD])
        a_tok = fixed("a_tok", [P, TT, NH_SSD])
        acum = fixed("acum", [P, TT, NH_SSD])
        krr = fixed("krr", [P, TT, ROPE])
        sskr = fixed("sskr", [P, TT])
        ssq = fixed("ssq", [P, 2, TT, H_MLA])
        rqk = fixed("rqk", [P, 2, TT, H_MLA])
        qsc = fixed("qsc", [P, 2, TT, H_MLA])
        mx = fixed("mx", [P, 3, 8])
        cwh = fixed("cwh", [P, 24, 5])
        fwh = fixed("fwh", [P, 44, 4])
        gbh = fixed("gbh", [P, 16])
        end_first, cursor[0] = cursor[0], small
        ss2 = fixed("ss2", [P, TT, 42])
        r2 = fixed("r2", [P, TT, 42])
        qs2 = fixed("qs2", [P, 2, TT, 42])
        m2 = fixed("m2", [P, 3, 4, 6])
        md = fixed("md", [P, 2, 2])
        ssc = fixed("ssc", [CG, 2, 3])
        vc = fixed("vc", [CG, 3, HD])
        kcT = fixed("kcT", [HD, 3, CG])
        cursor[0] = max(cursor[0], end_first)
        ARENA, LIMIT = cursor[0], nc.sbuf_usable_end

        def at(name, kib, shape, dt=F32):
            off = ARENA + int(kib * 1024)
            assert off + int(np.prod(shape[1:])) * 4 <= LIMIT, (name, off, LIMIT)
            return nc.alloc_sbuf_tensor_at(name, shape, dt, offset=off)

        def A(name):
            o, n = PA[name]
            return pa[:, o:o + n]

        xbcT = at("xbcT", 0, [P, 24, T])
        xdt = at("xdt", 24, [P, TT, DI])
        scM = at("scM", 40, [P, NG_SSD, BW])
        Rb = at("Rb", 46, [P, 2, 4, T])
        seg = at("seg", 54, [P, 4, BW])
        Mt = at("Mt", 60, [P, 2, 4, BW])
        zs = at("zs", 78, [P, 2, 2, T])
        cacc = at("cacc", 98, [P, 2, 2, T])
        qn_hi = at("qn_hi", 84, [P, 3, T], F32R)
        qn_lo = at("qn_lo", 87, [P, 3, T], F32R)
        qaT = at("qaT", 90, [P, 3, T])
        tb = at("tb", 93, [P, 2, 2, T])
        dtw = at("dtw", 76, [P, 8, 2 * NH_SSD])
        acumT = at("acumT", 97, [NH_SSD, T])
        kr = at("kr", 82, [P, TT, ROPE])
        krg = at("krg", 82.25, [P, TT, ROPE])
        krt = at("krt", 82.5, [P, 4, TT, ROPE // 2])
        ohi = at("ohi", 0, [P, 8, T], F32R)
        olo = at("olo", 8, [P, 8, T], F32R)
        vS = at("vS", 16, [P, TT, H_MLA, VD])
        y_hi = at("y_hi", 24, [P, 16, T], F32R)
        y_lo = at("y_lo", 40, [P, 16, T], F32R)
        k96 = at("k96", 56, [P, TT, H_MLA, QK])
        q96 = at("q96", 68, [P, TT, H_MLA, QK])
        sqt = at("sqt", 80, [P, 2, 384])
        qkT = at("qkT", 80, [P, 2, 2 * T])
        rot = at("rot", 84, [P, 2, TT, H_MLA, ROPE // 2])
        Sm = at("Sm", 84, [P, 3, BW])
        PTs = at("PTs", 88.5, [P, BW])
        gT = at("gT", 90, [P, 16, T])
        mixa = at("mixa", 56, [P, KD, T])
        g_hi = at("g_hi", 0, [P, 22, T], F32R)
        g_lo = at("g_lo", 22, [P, 22, T], F32R)
        facc = at("facc", 84, [P, 2, 2, T])
        ftg = at("ftg", 88, [P, 2, T])
        fg = at("fg", 90, [P, 2, T])
        tm = at("tm", 0, [P, TT, 3840])
        gnsa = at("gnsa", 30, [P, TT, 3 * H_NSA])
        gT2 = at("gT2", 31, [P, 16, T])
        o2_hi = at("o2_hi", 47, [P, 8, T], F32R)
        o2_lo = at("o2_lo", 55, [P, 8, T], F32R)
        ckv = at("ckv", 63, [P, 3, T])
        cblk = at("cblk", 66, [P, 6, T])
        bT_hi = at("bT_hi", 72, [P, 2, 16, 3, CG], F32R)
        bT_lo = at("bT_lo", 78, [P, 2, 16, 3, CG], F32R)
        bT = at("bT", 84, [P, 2, 16, 3, CG])
        hid = at("hid", 84, [3 * CG, 2, 2, 256])
        hidT = at("hidT", 69, [P, 2, 2, 3 * CG])
        cn = at("cn", 88, [CG, 3, 3, HD])
        kswT = at("kswT", 63, [HD, 6, T])
        SN = at("SN", 69, [P, 3, 768 + 2 * CG])
        SD = at("SD", 69, [P, 2, 1152])
        PT2 = at("PT2", 78.375, [P, 4, BW])
        qkT2 = at("qkT2", 84.375, [HD, 2, 2 * T])
        pcT = at("pcT", 88.375, [CG, 2, T])
        rt = at("rt", 90.375, [P, 2, TT, 4, HD // 2])
        sqt2 = at("sqt2", 92.375, [P, 2, TT * 4, HD])
        pb = at("pb", 96.5, [P, params_b.shape[1]])
        mix2 = at("mix2", 0, [P, KD, T])
        s_hi = at("s_hi", 0, [P, 32, T], F32R)
        s_lo = at("s_lo", 32, [P, 32, T], F32R)
        srl = at("srl", 80, [P, 2, 2, T])
        ssqr = at("ssqr", 84, [P, 2, 2, T])

        def Bp(name):
            o, n = PB[name]
            return pb[:, o:o + n]

        sqb = {"x": at("sq_x", 0, [P, 8, T]), "qa": at("sq_qa", 24, [P, 4, T]), "y": at("sq_y", 98, [P, 4, T]),
               "ffn": at("sq_ffn", 64, [P, 8, T]), "x2": at("sq_x2", 47, [P, 8, T]),
               "ffn2": at("sq_ffn2", 64, [P, 8, T])}
        hfb = {"x": at("hf_x", 8, [P, 8, T]), "qa": at("hf_qa", 28, [P, 4, T]), "y": at("hf_y", 102, [P, 4, T]),
               "ffn": at("hf_ffn", 72, [P, 8, T]), "x2": at("hf_x2", 55, [P, 8, T]),
               "ffn2": at("hf_ffn2", 72, [P, 8, T])}
        sqb["kva"], hfb["kva"] = sqb["qa"], hfb["qa"]
        dgb = {"x": at("dg_x", 102, [P, 2, P]), "qa": at("dg_qa", 103, [P, 4, P]), "y": at("dg_y", 80, [P, 8, P]),
               "ffn": at("dg_ffn", 80, [P, 2, P]), "x2": at("dg_x2", 63, [P, 2, P]),
               "ffn2": at("dg_ffn2", 80, [P, 2, P])}
        dgb["kva"] = dgb["qa"]
        NORM_IO = {"x": (xT, 0, "g_mix", h_hi, h_lo), "qa": (qaT, 0, "g_qa", qn_hi, qn_lo),
                   "kva": (qaT, 2, "g_kva", qn_hi, qn_lo), "y": (xbcT, 0, "g_ssd", y_hi, y_lo),
                   "ffn": (xT, 0, "g_ffn", h_hi, h_lo), "x2": (xT, 0, "g1", h_hi, h_lo),
                   "ffn2": (xT, 0, "g2", h_hi, h_lo)}

        banks = [ctx.enter_context(nc.psum_tensor(f"bank{i}", [P, 512], F32)) for i in range(8)]
        G = banks[0:2]
        B = banks[2:8]


        scr = nc.dram_tensor("acum_rows", [NH_SSD, T], F32, kind="Internal").ap()

        landed = [sem(f"landed{r}") for r in range(SLOTS)]
        hi_done, lo_done, chunk_used, bank_free = sem("hi_done"), sem("lo_done"), sem("chunk_used"), sem("bank_free")
        x_in, pa_first, pa_in = sem("x_in"), sem("pa_first"), sem("pa_in")
        n_sq, n_sum, n_rs, n_dg, n_bc, n_f, n_hi, n_lo = (sem("norm_" + s) for s in
                                                     ("sq", "sum", "root", "diag", "bcast", "f", "hi", "lo"))
        act_own, dve_own, pool_own = sem("act_own"), sem("dve_own"), sem("pool_own")
        y_rs = sem("y_rs")
        dtr_ready, sp_exp, sp_u, sp_ln = sem("dtr_ready"), sem("sp_exp"), sem("sp_u"), sem("sp_ln")
        a_ready, cum_ps, acumT_sb, rows_out = sem("a_ready"), sem("cum_ps"), sem("acumT_sb"), sem("rows_out")
        conv_u, conv_acc, conv_t, xbc_ready = sem("conv_u"), sem("conv_acc"), sem("conv_t"), sem("xbc_ready")
        xs_tr, xdt_ready = sem("xs_tr"), sem("xdt_ready")
        score_ps, score_sb = sem("score_ps"), sem("score_sb")
        rows_in = [sem("rows_in0"), sem("rows_in1")]
        seg_ready, decay_ready, m_ready, y_ps, y_ready = (sem("seg_ready"), sem("decay_ready"), sem("m_ready"),
                                                          sem("y_ps"), sem("y_ready"))
        z_t = sem("z_t")
        u_sq, kq_ss, kq_rs, kq_ready = sem("u_sq"), sem("kq_ss"), sem("kq_rs"), sem("kq_ready")
        qkT_ps, qkT_sb, s_ps, sm_ready, p_exp, p_ready = (sem("qkT_ps"), sem("qkT_sb"), sem("s_ps"), sem("sm_ready"),
                                                          sem("p_exp"), sem("p_ready"))
        pt_ps, pt_sb, o_ps, o_hi, o_lo = sem("pt_ps"), sem("pt_sb"), sem("o_ps"), sem("o_hi"), sem("o_lo")
        gate_t, mix_ready, mix_hi, mix_lo, x1_ready = (sem("gate_t"), sem("mix_ready"), sem("mix_hi"), sem("mix_lo"),
                                                       sem("x1_ready"))
        f_u, f_acc, f_t, f_g, f_hi, f_lo = (sem("f_u"), sem("f_acc"), sem("f_t"), sem("f_g"), sem("f_hi"),
                                            sem("f_lo"))
        pb_in, ckv_sb, cblk_in, b_ready, b_hi, b_lo = (sem("pb_in"), sem("ckv_sb"), sem("cblk_in"), sem("b_ready"),
                                                       sem("b_hi"), sem("b_lo"))
        t_sq, t_free, tm_done = sem("t_sq"), sem("t_free"), sem("tm_done")
        ge_in, ge_t, ge_done, hT_ps, hT_sb, c_ps, c_ss, c_rs, cn_ready, cT_ps, cT_sb = (
            sem("ge_in"), sem("ge_t"), sem("ge_done"), sem("hT_ps"), sem("hT_sb"), sem("c_ps"), sem("c_ss"), sem("c_rs"), sem("cn_ready"),
            sem("cT_ps"), sem("cT_sb"))
        ss_ready, rs_ready, k_ready, kT_ps, kT_sb = (sem("ss_ready"), sem("rs_ready"), sem("k_ready"), sem("kT_ps"),
                                                     sem("kT_sb"))
        nq_ps, nq_sb, ns_ps, nm_ready, n_exp, np_ready, npt_ps, npt_sb, no_ps, no_hi, no_lo = (
            sem("nsa_" + s) for s in ("qT_ps", "qT_sb", "s_ps", "max_ready", "exp", "p_ready", "pT_ps", "pT_sb",
                                      "o_ps", "o_hi", "o_lo"))
        dq_ps, dq_sb, ds_ps, dm_part, dm_ready, d_exp, dp_ready, dpt_ps, dpt_sb, do_ps, do_hi, do_lo = (
            sem("dil_" + s) for s in ("qkT_ps", "qkT_sb", "s_ps", "max_part", "max_ready", "exp", "p_ready", "pT_ps",
                                      "pT_sb", "o_ps", "o_hi", "o_lo"))
        mix2_ready, mix2_hi, mix2_lo, sq_relu, sq_f, sq_hi, sq_lo = (
            sem(s) for s in ("mix2_ready", "mix2_hi", "mix2_lo", "sq_relu", "sq_f", "sq_hi", "sq_lo"))
        u_ps, oab_ps, out_done = sem("u_ps"), sem("oab_ps"), sem("out_done")

        USES = [("A", 1), ("QA", 1), ("XBC", 12), ("Z", 8), ("GATE_A", 1), ("UQ", 8), ("UKV", 8), ("GATE_B", 7),
                ("SSDP", 8), ("MLAP", 4), ("WO", 4), ("UP", 22), ("DOWN", 8), ("CKV", 2), ("TM_A", 6), ("TM_G", 1),
                ("CW1", 2), ("TM_B", 9), ("GATE2", 8), ("OAB", 8), ("WOUT", 4), ("UP2", 16), ("DOWN2", 8)]
        use0, at_use = {}, 0
        for s, n in USES:
            use0[s] = at_use
            at_use += n

        block = ctx.enter_context(nc.Block())

        @block.sync
        def _(sp):
            def load(c, slot, used):
                if not isinstance(c, int) or c >= SLOTS:
                    sp.wait_ge(chunk_used, c - SLOTS + 1)
                sp.dma_start(raw[:, slot, 0:used], wstream[c, :, 0:used]).then_inc(landed[slot], 16)

            sp.dma_start(xT[:, :, :], x_t).then_inc(x_in, 16)
            for name, (c0, n, used) in SEC.items():
                loops = n // 4 if n >= 8 and c0 >= SLOTS else 0
                if loops:
                    with sp.Fori(0, loops, 1) as i:
                        for j in range(4):
                            load(i * 4 + (c0 + j), (c0 + j) % SLOTS, used)
                for c in range(c0 + 4 * loops, c0 + n):
                    load(c, c % SLOTS, used)
            for k in range(0, KD, 2):
                sp.wait_ge(bank_free, use0["DOWN2"] + k + 2)
                sp.dma_start(out_t[:, k:k + 2, :], xT[:, k:k + 2, :]).then_inc(out_done, 16)
            sp.wait_ge(out_done, 16 * KD // 2)

        @block.gpsimd
        def _(pool):
            def split_lo(c, slot, used):
                pool.wait_ge(hi_done, c + 1)
                nc.gpsimd.tensor_tensor(w_lo[:, slot, 0:used], raw[:, slot, 0:used], w_hi[:, slot, 0:used],
                                        ALU.subtract).then_inc(lo_done, 1)

            own = Tally(pool, pool_own)

            def rotate_heads(i):
                pool.wait_ge(bank_free, use0["TM_B"] + i + 1)
                x = tm[:, :, 1536 + 256 * i:1792 + 256 * i].rearrange("p t (h d) -> p t h d", d=HD)
                if own.n:
                    own.wait()
                cosb, sinb = (Bp(t).rearrange("p (t n) -> p t n", t=2).unsqueeze(2).broadcast_to([P, TT, 4, HD // 2])
                              for t in ("cos32", "sin32"))
                rotation(own, nc.gpsimd, x[..., 0:HD // 2], x[..., HD // 2:HD], cosb, sinb, rt[:, 0], rt[:, 1])

            for name, (c0, n, used) in SEC.items():
                if name == "TM_B":
                    for i in range(n):
                        split_lo(c0 + i, (c0 + i) % SLOTS, used)
                        if 0 <= i - 2 < 6:
                            rotate_heads(i - 2)
                    continue
                loops = n // 4 if n >= 8 else 0
                if loops:
                    with pool.Fori(0, loops, 1) as i:
                        for j in range(4):
                            split_lo(i * 4 + (c0 + j), (c0 + j) % SLOTS, used)
                for c in range(c0 + 4 * loops, c0 + n):
                    split_lo(c, c % SLOTS, used)

        @block.tensor
        def _(pe):
            mm = nc.tensor.matmul

            def split_mm(out, w, x, kts, w_first, start=True, stop=True, arriving=None):
                last = None
                for n, (wp, xp) in enumerate(((0, 0), (1, 0), (0, 1))):
                    for kt in kts:
                        if arriving and not wp and kt % 2 == 0:
                            pe.wait_ge(arriving[xp], arriving[2] + kt // 2 + 1)
                        l, r = w(wp, kt), x(xp, kt)
                        if not w_first:
                            l, r = r, l
                        last = mm(out, l, r, start=start and n == 0 and kt == kts[0],
                                  stop=stop and n == 2 and kt == kts[-1])
                return last

            def wt(slot, cols, lo, width):
                return lambda part, kt: (w_hi, w_lo)[part][:, slot, kt * cols + lo:kt * cols + lo + width]

            def ch(hi, lo, t0=0):
                return lambda part, kt: (hi, lo)[part][:, t0 + kt, :]

            def tok(hi, lo, tt, t0=0):
                return lambda part, kt: (hi, lo)[part][:, t0 + kt, tt * P:(tt + 1) * P]

            def chunk_in(c):
                pe.wait_ge(lo_done, c + 1)

            def bank_in(u):
                if not isinstance(u, int) or u >= 2:
                    pe.wait_ge(bank_free, u - 1)

            def enter(name):
                pe.wait_ge(bank_free, use0[name])

            def normed(name):
                return n_hi, n_lo, NORM_AT[name][0]

            def half(c, slot, out, j, x, cols=256, arriving=None):
                return split_mm(out[:, j * T:(j + 1) * T], wt(slot, cols, j * P, P), x, range(KD), True,
                                arriving=arriving)

            def norm_sums(name, groups=None):
                t, gw, w, slots = NORMS[name]
                p0, g0 = NORM_AT[name]
                for g in groups or range(t // gw):
                    col = RS_AT.get(name, 0) + g
                    for k in range(gw):
                        tile = g * gw + k
                        if tile % w == 0:
                            pe.wait_ge(n_sq, p0 + tile // w + 1)
                        for tt in range(TT):
                            last = mm(B[tt][:, col:col + 1], sqb[name][:, tile % slots, tt * P:(tt + 1) * P],
                                      A("ones")[:, 0:1], start=k == 0, stop=k == gw - 1)
                    last.then_inc(n_sum, 1)

            def norm_broadcast(*names):
                pe.wait_ge(n_dg, NORM_ORDER.index(names[-1]) + 1)
                for name in names:
                    t, gw, _, _ = NORMS[name]
                    for g in range(t // gw):
                        col = RS_AT.get(name, 0) + g
                        for tt in range(TT):
                            c0 = (col % 2) * T + tt * P
                            last = mm(B[col // 2][:, c0:c0 + P], A("ones"), dgb[name][:, 2 * col + tt, :], start=True,
                                      stop=True)
                    last.then_inc(n_bc, 1)

            pe.wait_ge(pa_first, 16)
            norm_sums("x")
            norm_broadcast("x")
            xh = ch(h_hi, h_lo)
            c = SEC["A"][0]
            chunk_in(c)
            split_mm(G[0][:, 0:T], wt(c % SLOTS, 192, 64, P), xh, range(KD), True,
                     arriving=normed("x"))
            for tt in range(TT):
                last = split_mm(G[0][:, T + 64 * tt:T + 64 * tt + 64], wt(c % SLOTS, 192, 0, 64), tok(h_hi, h_lo, tt),
                                range(KD), False)
            last.then_inc(chunk_used, 1)
            c = SEC["QA"][0]
            chunk_in(c)
            half(c, c % SLOTS, G[1], 0, xh)
            half(c, c % SLOTS, G[1], 1, xh).then_inc(chunk_used, 1)

            def transposes(i):
                pe.wait_ge(xbc_ready, i + 1)
                if i >= 2:
                    pe.wait_ge(xdt_ready, i - 1)
                for j in range(2):
                    for tt in range(TT):
                        last = nc.tensor.transpose(B[2 + i % 2][:, tt * T + j * P:tt * T + (j + 1) * P],
                                                   xbcT[:, 2 * i + j, tt * P:(tt + 1) * P], A("ident"))
                last.then_inc(xs_tr, 1)

            for i in range(12):
                c = SEC["XBC"][0] + i
                chunk_in(c)
                bank_in(use0["XBC"] + i)
                b = G[(use0["XBC"] + i) % 2]
                half(c, c % SLOTS, b, 0, xh)
                if i == 0:
                    enter("XBC")
                half(c, c % SLOTS, b, 1, xh).then_inc(chunk_used, 1)
                if i == 0:
                    norm_sums("qa")
                    norm_sums("kva")
                if i == 4:
                    norm_broadcast("qa", "kva")
                if i == 1:
                    pe.wait_ge(a_ready, 1)
                    keep = A("keep")
                    mm(B[4][:, 0:32], keep[:, 0:P], a_tok[:, 0, :], start=True, stop=True)
                    mm(B[4][:, 32:64], keep[:, P:T], a_tok[:, 0, :], start=True, stop=False)
                    mm(B[4][:, 32:64], keep[:, 0:P], a_tok[:, 1, :], start=False, stop=True)
                    mm(B[4][0:32, 128:384], a_tok[:, 0, :], keep[:, 0:T], start=True, stop=False)
                    mm(B[4][0:32, 256:384], a_tok[:, 1, :], keep[:, 0:P], start=False,
                       stop=True).then_inc(cum_ps, 1)
                if 2 <= i < 10:
                    transposes(i - 2)

            def scores(g):
                if g == 0:
                    pe.wait_ge(xbc_ready, 12)
                    pe.wait_ge(acumT_sb, 1)
                if g >= 2:
                    pe.wait_ge(score_sb, g - 1)
                b = B[4 + g % 2]
                mm(b[:, 0:T], xbcT[:, 16 + g, 0:P], xbcT[:, 20 + g, :], start=True, stop=True)
                mm(b[:, T:BW], xbcT[:, 16 + g, P:T], xbcT[:, 20 + g, P:T], start=True,
                   stop=True).then_inc(score_ps, 1)

            def y_heads(i):
                pe.wait_ge(m_ready, i + 1)
                if i == 0:
                    pe.wait_ge(score_sb, NG_SSD)
                    pe.wait_ge(xdt_ready, 8)
                if i >= 2:
                    pe.wait_ge(y_ready, i - 1)
                b = B[4 + i % 2]
                for h in range(4):
                    rows = slice((h % 2) * 64, (h % 2) * 64 + 64)
                    col = (4 * i + h) * HD_SSD
                    t0 = (h // 2) * T
                    mm(b[rows, t0:t0 + T], xdt[:, 0, col:col + 64], Mt[:, i % 2, h, 0:T], start=True, stop=False)
                    last = mm(b[rows, t0 + P:t0 + T], xdt[:, 1, col:col + 64], Mt[:, i % 2, h, T:BW], start=False,
                              stop=True)
                last.then_inc(y_ps, 1)

            for i in range(9):
                name, k = ("Z", i) if i < 8 else ("GATE_A", 0)
                c, u = SEC[name][0] + k, use0[name] + k
                if i in (5, 7):
                    norm_sums("y", [i // 2 - 2])
                chunk_in(c)
                bank_in(u)
                half(c, c % SLOTS, G[u % 2], 0, xh)
                if i == 0:
                    for g in range(NG_SSD):
                        scores(g)
                if k == 0:
                    enter(name)
                half(c, c % SLOTS, G[u % 2], 1, xh).then_inc(chunk_used, 1)
                if i >= 1:
                    y_heads(i - 1)

            norm_sums("y", [2])
            enter("UQ")
            pe.wait_ge(n_lo, norm_end("kva"))
            u = use0["UQ"]
            for k in range(2):
                c = SEC["UQ"][0] + k
                chunk_in(c)
                for hf in range(2):
                    for tt in range(TT):
                        bank_in(u)
                        last = split_mm(G[u % 2][:, 0:384], wt(c % SLOTS, 768, hf * 384, 384), tok(qn_hi, qn_lo, tt),
                                        range(2), False)
                        last.then_inc(u_ps, 1) if not (hf and tt) else last.then_inc(chunk_used, 1)
                        u += 1
            c = SEC["UKV"][0]
            chunk_in(c)
            for quarter in range(4):
                for tt in range(TT):
                    bank_in(u)
                    last = split_mm(G[u % 2][:, :], wt(c % SLOTS, 2048, quarter * 512, 512), tok(qn_hi, qn_lo, tt, 2),
                                    range(1), False)
                    last.then_inc(u_ps, 1) if quarter + tt < 4 else last.then_inc(chunk_used, 1)
                    u += 1

            def head_step(s):
                h = s
                if h < H_MLA:
                    if h == 0:
                        pe.wait_ge(kq_ready, 1)
                        pe.wait_ge(y_rs, 1)
                    if h >= 2:
                        pe.wait_ge(qkT_sb, h - 1)
                    b = B[h % 2]
                    for j, src in enumerate((q96, k96)):
                        for tt in range(TT):
                            last = nc.tensor.transpose(b[0:QK, j * T + tt * P:j * T + (tt + 1) * P],
                                                       src[:, tt, h, :], A("ident"))
                    last.then_inc(qkT_ps, 1)
                h = s - 1
                if 0 <= h < H_MLA:
                    pe.wait_ge(qkT_sb, h + 1)
                    if h >= 2:
                        pe.wait_ge(sm_ready, h - 1)
                    b, kq = B[2 + h % 2], qkT[0:QK, h % 2, :]
                    mm(b[:, 0:P], kq[:, 0:P], kq[:, T:T + P], start=True, stop=True)
                    mm(b[:, P:BW], kq[:, P:T], kq[:, T:2 * T], start=True, stop=True).then_inc(s_ps, 1)
                h = s - 4
                if 0 <= h < H_MLA:
                    pe.wait_ge(pt_sb, h + 1)
                    if h % 2 == 0 and h >= 2:
                        pe.wait_ge(o_lo, h // 2)
                    rows = slice((h % 2) * 64, (h % 2) * 64 + 64)
                    mm(B[5][rows, 0:T], vS[:, 0, h, :], PTs[:, 0:T], start=True, stop=False)
                    mm(B[5][rows, P:T], vS[:, 1, h, :], PTs[:, T:BW], start=False, stop=True).then_inc(o_ps, 1)
                h = s - 3
                if 0 <= h < H_MLA:
                    pe.wait_ge(p_ready, h + 1)
                    if h == 0:
                        pe.wait_ge(y_ready, 8)
                    if h >= 1:
                        pe.wait_ge(pt_sb, h)
                    for n in range(3):
                        last = nc.tensor.transpose(B[4][:, n * P:(n + 1) * P], Sm[:, h % 3, n * P:(n + 1) * P],
                                                   A("ident"))
                    last.then_inc(pt_ps, 1)

            step = 0
            for i in range(7):
                c, u = SEC["GATE_B"][0] + i, use0["GATE_B"] + i
                chunk_in(c)
                bank_in(u)
                half(c, c % SLOTS, G[u % 2], 0, xh)
                if i == 0:
                    enter("GATE_B")
                if i == 1:
                    norm_broadcast("y")
                if i:
                    head_step(step)
                    step += 1
                half(c, c % SLOTS, G[u % 2], 1, xh).then_inc(chunk_used, 1)
                if i:
                    head_step(step)
                    step += 1
                else:
                    norm_sums("y", [3])
            pe.wait_ge(n_lo, norm_end("y"))
            for i in range(8):
                c, u = SEC["SSDP"][0] + i, use0["SSDP"] + i
                chunk_in(c)
                bank_in(u)
                out, x = G[u % 2][:, 0:T], ch(y_hi, y_lo)
                split_mm(out, wt(c % SLOTS, P, 0, P), x, range(8), True, stop=False)
                if i == 0:
                    enter("SSDP")
                if step < H_MLA + 4:
                    head_step(step)
                    step += 1
                split_mm(out, wt(c % SLOTS, P, 0, P), x, range(8, 16), True, start=False).then_inc(chunk_used, 1)
                if step < H_MLA + 4 and i >= 1:
                    head_step(step)
                    step += 1
            pe.wait_ge(o_lo, 8)
            for i in range(4):
                c, u = SEC["MLAP"][0] + i, use0["MLAP"] + i
                chunk_in(c)
                bank_in(u)
                half(c, c % SLOTS, G[u % 2], 0, ch(ohi, olo))
                half(c, c % SLOTS, G[u % 2], 1, ch(ohi, olo)).then_inc(chunk_used, 1)
            for i in range(4):
                c, u = SEC["WO"][0] + i, use0["WO"] + i
                chunk_in(c)
                bank_in(u)
                half(c, c % SLOTS, G[u % 2], 0, xh, arriving=None if i else (mix_hi, mix_lo, 0))
                half(c, c % SLOTS, G[u % 2], 1, xh).then_inc(chunk_used, 1)

            norm_sums("ffn")
            norm_broadcast("ffn")

            def channel_chunk(c, slot, u, bank, arriving=None, first_of=None):
                chunk_in(c)
                bank_in(u)
                half(c, slot, G[bank], 0, xh, arriving=arriving)
                if first_of:
                    enter(first_of)
                half(c, slot, G[bank], 1, xh).then_inc(chunk_used, 1)

            def channel_section(name, norm):
                c0, n, _ = SEC[name]
                u0 = use0[name]
                channel_chunk(c0, c0 % SLOTS, u0, u0 % 2, normed(norm), name)
                c0, u0, n = c0 + 1, u0 + 1, n - 1
                with pe.Fori(0, n // 4, 1) as i:
                    for j in range(4):
                        channel_chunk(i * 4 + (c0 + j), (c0 + j) % SLOTS, i * 4 + (u0 + j), (u0 + j) % 2)
                for k in range(n // 4 * 4, n):
                    channel_chunk(c0 + k, (c0 + k) % SLOTS, u0 + k, (u0 + k) % 2)

            channel_section("UP", "ffn")
            def down_section(name, kts, hi, lo, ready, total):
                c0, n, _ = SEC[name]
                u0 = use0[name]

                def tile(k, it=None):
                    for j in range(2):
                        c = c0 + 2 * k + j
                        chunk_in(c if it is None else it * 4 + c)
                        if j == 0:
                            bank_in(u0 + k if it is None else it * 2 + (u0 + k))
                        if k == 0:
                            pe.wait_ge(ready, total // (2 - j))
                            if j == 1:
                                enter(name)
                        split_mm(G[(u0 + k) % 2][:, 0:T], wt(c % SLOTS, P, 0, P), ch(hi, lo, j * kts), range(kts),
                                 True, start=j == 0, stop=j == 1).then_inc(chunk_used, 1)

                tile(0)
                with pe.Fori(0, (KD - 2) // 2, 1) as i:
                    tile(1, i)
                    tile(2, i)
                tile(KD - 1)

            down_section("DOWN", 11, g_hi, g_lo, f_lo, 22)

            norm_sums("x2")
            norm_broadcast("x2")
            c, u = SEC["CKV"][0], use0["CKV"]
            channel_chunk(c, c % SLOTS, u, u % 2, normed("x2"), "CKV")
            chunk_in(c + 1)
            bank_in(u + 1)
            half(c + 1, (c + 1) % SLOTS, G[(u + 1) % 2], 0, xh, P).then_inc(chunk_used, 1)

            def token_half(c, u, tt, cols=256):
                if tt == 0:
                    chunk_in(c)
                    bank_in(u)
                last = split_mm(G[u % 2][:, tt * cols:(tt + 1) * cols], wt(c % SLOTS, cols, 0, cols),
                                tok(h_hi, h_lo, tt), range(KD), False)
                if tt:
                    last.then_inc(chunk_used, 1)

            for name in ("TM_A", "TM_G"):
                for i in range(SEC[name][1]):
                    for tt in range(TT):
                        if i == 0 and tt:
                            enter(name)
                        token_half(SEC[name][0] + i, use0[name] + i, tt, 64 if name == "TM_G" else 256)
            pe.wait_ge(b_lo, 1)
            for i in range(4):
                kv, k_half = i // 2, i % 2
                c, u = SEC["CW1"][0] + i, use0["CW1"] + kv
                chunk_in(c)
                if k_half == 0:
                    bank_in(u)
                split_mm(G[u % 2][0:3 * CG, 0:256], wt(c % SLOTS, 256, 0, 256),
                         lambda part, kt: (bT_hi, bT_lo)[part][:, kv, 8 * k_half + kt].rearrange("p g n -> p (g n)"),
                         range(KD), False, start=k_half == 0, stop=k_half == 1).then_inc(chunk_used, 1)

            def hidden_transposes():
                pe.wait_ge(ge_done, 1)
                for kv in range(2):
                    for m in range(2):
                        last = nc.tensor.transpose(B[5][:, (2 * kv + m) * 3 * CG:(2 * kv + m + 1) * 3 * CG],
                                                   hid[:, 0, kv, m * P:(m + 1) * P], A("ident")[0:3 * CG, 0:3 * CG])
                last.then_inc(hT_ps, 1)

            def second_layer():
                pe.wait_ge(hT_sb, 1)
                for kv, name in enumerate(("w2_k", "w2_v")):
                    w2 = Bp(name).rearrange("p (m d) -> p m d", m=2)
                    for g in range(G_NSA):
                        for m in range(2):
                            last = mm(B[0][0:CG, (kv * 3 + g) * HD:(kv * 3 + g + 1) * HD],
                                      hidT[:, kv, m, g * CG:(g + 1) * CG], w2[:, m, :], start=m == 0, stop=m == 1)
                last.then_inc(c_ps, 1)

            def k_transposes():
                pe.wait_ge(k_ready, 1)
                for n in range(6):
                    for tt in range(TT):
                        last = nc.tensor.transpose(B[1 + n // 2][0:HD, (n % 2) * T + tt * P:(n % 2) * T + tt * P + P],
                                                   tm[:, tt, 768 + n * HD:768 + (n + 1) * HD], A("ident"))
                last.then_inc(kT_ps, 1)

            def kc_transposes():
                pe.wait_ge(cn_ready, 1)
                for g in range(G_NSA):
                    last = nc.tensor.transpose(B[5][0:HD, g * CG:(g + 1) * CG], cn[:, 0, g, :],
                                               A("ident")[0:CG, 0:CG])
                last.then_inc(cT_ps, 1)

            def nsa_step(s):
                h = s
                if s == 1:
                    pe.wait_ge(cT_sb, 1)
                    pe.wait_ge(kT_sb, 1)
                if h < H_NSA + 3 and h >= 1:
                    pe.wait_ge(nq_sb, h)
                if h < H_NSA:
                    for tt in range(TT):
                        last = nc.tensor.transpose(B[0][0:HD, tt * P:(tt + 1) * P], tm[:, tt, h * HD:(h + 1) * HD],
                                                   A("ident"))
                if 0 <= h - 3 < H_NSA:
                    pe.wait_ge(np_ready, h - 2)
                    for tt in range(TT):
                        last = nc.tensor.transpose(B[0][0:CG, T + tt * P:T + (tt + 1) * P],
                                                   SN[:, h % 3, 768 + tt * CG:768 + (tt + 1) * CG], A("ident"))
                if h < H_NSA + 3:
                    last.then_inc(nq_ps, 1)
                h = s - 1
                if 0 <= h < H_NSA:
                    pe.wait_ge(nq_sb, h + 1)
                    if h >= 1:
                        pe.wait_ge(nm_ready, h)
                    q, g = qkT2[:, h % 2, 0:T], h // HPG
                    for n, b in enumerate((B[1], B[2])):
                        kT = kswT[:, 3 * n + g, :]
                        mm(b[:, 0:P], q[:, 0:P], kT[:, 0:P], start=True, stop=True)
                        mm(b[:, P:BW], q[:, P:T], kT, start=True, stop=True)
                    for tt in range(TT):
                        last = mm(B[2][:, BW + tt * CG:BW + (tt + 1) * CG], q[:, tt * P:(tt + 1) * P], kcT[:, g, :],
                                  start=True, stop=True)
                    last.then_inc(ns_ps, 1)
                h = s - 3
                if 0 <= h < H_NSA:
                    if h >= 1:
                        pe.wait_ge(npt_sb, h)
                    for n in range(6):
                        last = nc.tensor.transpose(B[3 + n // 3][:, n % 3 * P:(n % 3 + 1) * P],
                                                   SN[:, h % 3, n * P:(n + 1) * P], A("ident"))
                    last.then_inc(npt_ps, 1)
                h = s - 4
                if 0 <= h < H_NSA:
                    pe.wait_ge(npt_sb, h + 1)
                    pe.wait_ge(nq_sb, h + 4)
                    if h % 2 == 0 and h >= 2:
                        pe.wait_ge(no_lo, h // 2)
                    g, out = h // HPG, B[5][(h % 2) * 64:(h % 2) * 64 + 64, :]
                    for n in range(2):
                        c0 = 1152 + 192 * n + g * HD
                        pt = PT2[:, 2 * (h % 2) + n, :]
                        mm(out[:, 0:T], tm[:, 0, c0:c0 + HD], pt[:, 0:T], start=n == 0, stop=False)
                        mm(out[:, P:T], tm[:, 1, c0:c0 + HD], pt[:, T:BW], start=False, stop=False)
                    mm(out[:, 0:T], vc[:, g, :], pcT[:, h % 2, :], start=False, stop=True).then_inc(no_ps, 1)

            def dil_step(s):
                u = s
                if u < H_DIL:
                    if u == 0:
                        pe.wait_ge(k_ready, 2)
                        pe.wait_ge(nq_sb, H_NSA + 3)
                    if u >= 1:
                        pe.wait_ge(dq_sb, u)
                    for j, c0 in enumerate((1536, 2304)):
                        col = c0 + (u % 3 * DH + u // 3) * HD
                        for tt in range(TT):
                            last = nc.tensor.transpose(B[0][0:HD, j * T + tt * P:j * T + (tt + 1) * P],
                                                       tm[:, tt, col:col + HD], A("ident"))
                    last.then_inc(dq_ps, 1)
                u = s - 1
                if 0 <= u < H_DIL:
                    pe.wait_ge(dq_sb, u + 1)
                    if u == 0:
                        pe.wait_ge(nm_ready, H_NSA)
                    if u >= 2:
                        pe.wait_ge(dm_part, u - 1)
                    b, q = B[1 + u % 2], qkT2[:, u % 2, :]
                    mm(b[:, 0:P], q[:, 0:P], q[:, T:T + P], start=True, stop=True)
                    mm(b[:, P:BW], q[:, P:T], q[:, T:2 * T], start=True, stop=True).then_inc(ds_ps, 1)
                u = s - 5
                if 0 <= u < H_DIL:
                    pe.wait_ge(dp_ready, u // 3 + 1)
                    if u == 0:
                        pe.wait_ge(npt_sb, H_NSA)
                    if u >= 2:
                        pe.wait_ge(dpt_sb, u - 1)
                    for n in range(3):
                        last = nc.tensor.transpose(B[3 + u % 2][:, n * P:(n + 1) * P],
                                                   SD[:, u // 3 % 2, u % 3 * BW + n * P:u % 3 * BW + (n + 1) * P],
                                                   A("ident"))
                    last.then_inc(dpt_ps, 1)
                u = s - 6
                if 0 <= u < H_DIL:
                    hh, g = u // 3, u % 3
                    pe.wait_ge(dpt_sb, u + 1)
                    if u == 0:
                        pe.wait_ge(no_lo, H_NSA // 2)
                    if hh == 2 and g == 0:
                        pe.wait_ge(do_lo, 1)
                    out, col = B[5][(hh % 2) * 64:(hh % 2) * 64 + 64, :], 3072 + (g * DH + hh) * HD
                    mm(out[:, 0:T], tm[:, 0, col:col + HD], PT2[:, u % 2, 0:T], start=g == 0, stop=False)
                    mm(out[:, P:T], tm[:, 1, col:col + HD], PT2[:, u % 2, T:BW], start=False,
                       stop=g == 2).then_inc(do_ps, 1)

            nsa = dil = 0
            for i in range(9):
                for tt in range(TT):
                    if i == 0 and tt:
                        enter("TM_B")
                    token_half(SEC["TM_B"][0] + i, use0["TM_B"] + i, tt)
                    if i == 0:
                        (k_transposes, hidden_transposes)[tt]()
                    if i == 1 and tt == 0:
                        second_layer()
                    if i == 2 and tt == 0:
                        kc_transposes()
                    if i >= 2:
                        nsa_step(nsa)
                        nsa += 1
            for i in range(8):
                c, u = SEC["GATE2"][0] + i, use0["GATE2"] + i
                chunk_in(c)
                bank_in(u)
                for j in range(2):
                    if i == 0 and j:
                        enter("GATE2")
                    last = half(c, c % SLOTS, G[u % 2], j, xh)
                    if j:
                        last.then_inc(chunk_used, 1)
                    if nsa < H_NSA + 4:
                        nsa_step(nsa)
                        nsa += 1
                    else:
                        dil_step(dil)
                        dil += 1
            while dil < H_DIL + 6:
                dil_step(dil)
                dil += 1
            pe.wait_ge(no_lo, 6)
            pe.wait_ge(do_lo, 2)
            u = use0["OAB"]
            for i in range(4):
                c = SEC["OAB"][0] + i
                chunk_in(c)
                for kts in (range(6), range(6, 8)):
                    bank_in(u)
                    for j in range(2):
                        if u == use0["OAB"] and j:
                            enter("OAB")
                        last = split_mm(G[u % 2][:, j * T:(j + 1) * T], wt(c % SLOTS, 256, j * P, P), ch(o2_hi, o2_lo),
                                        kts, True)
                    last.then_inc(chunk_used if kts[0] else oab_ps, 1)
                    u += 1
            for i in range(4):
                c, u = SEC["WOUT"][0] + i, use0["WOUT"] + i
                channel_chunk(c, c % SLOTS, u, u % 2, None if i else (mix2_hi, mix2_lo, 0))
            norm_sums("ffn2")
            norm_broadcast("ffn2")
            channel_section("UP2", "ffn2")
            down_section("DOWN2", 16, s_hi, s_lo, sq_lo, 16)

        @block.scalar
        def _(act):
            fn = nc.scalar.activation
            own = Tally(act, act_own)

            def hi_of(c, it=None):
                used = next(u for c0, n, u in SEC.values() if c0 <= c < c0 + n)
                slot = c % SLOTS
                rounds = c // SLOTS + 1
                if it is None:
                    act.wait_ge(landed[slot], 16 * rounds)
                    if c >= SLOTS:
                        act.wait_ge(chunk_used, c - SLOTS + 1)
                else:
                    act.wait_ge(landed[slot], it * 16 + 16 * rounds)
                    act.wait_ge(chunk_used, it * 4 + (c - SLOTS + 1))
                fn(w_hi[:, slot, 0:used], raw[:, slot, 0:used], ACT.Copy).then_inc(hi_done, 1)

            LAST = NCHUNK - 1

            def ahead(c, it=None):
                if c + AHEAD <= LAST:
                    hi_of(c + AHEAD, it)

            def norm_squares(name, pieces=None):
                t, gw, w, slots = NORMS[name]
                p0, g0 = NORM_AT[name]
                src, s0 = NORM_IO[name][:2]
                for p in pieces or range(t // w):
                    k = p * w
                    g = k // gw
                    if k >= slots:
                        act.wait_ge(n_sum, g0 + g)
                    fn(sqb[name][:, k % slots:k % slots + w, :], src[:, s0 + k:s0 + k + w, :],
                       ACT.Square).then_inc(n_sq, 1)

            def norm_root(name):
                t, gw, _, _ = NORMS[name]
                n, r0 = t // gw, RS_AT.get(name, 0)
                eps = A("eps")[:, 1:2] if name == "y" else A("eps")[:, 0:1]
                act.wait_ge(n_sum, norm_groups(name))
                for tt in range(TT):
                    ins = fn(rs[:, tt, r0:r0 + n], B[tt][:, r0:r0 + n], ACT.Sqrt, scale=1.0 / (gw * P), bias=eps)
                ins.then_inc(n_rs, 1)

            def norm_hi(name, pieces=None):
                t, gw, w, slots = NORMS[name]
                p0, _ = NORM_AT[name]
                _, s0, _, hi, _ = NORM_IO[name]
                for p in pieces or range(t // w):
                    act.wait_ge(n_f, p0 + p + 1)
                    k = p * w
                    fn(hi[:, s0 + k:s0 + k + w, :], hfb[name][:, k % slots:k % slots + w, :],
                       ACT.Copy).then_inc(n_hi, 1)

            first = PA["cw"][0]
            act.dma_start(pa[:, 0:first], params_a[:, 0:first]).then_inc(pa_first, 16)
            act.wait_ge(x_in, 16)
            norm_squares("x")
            act.dma_start(pa[:, first:], params_a[:, first:]).then_inc(pa_in, 16)
            hi_of(0)
            hi_of(1)
            act.wait_ge(pa_first, 16)
            norm_root("x")
            norm_hi("x")
            hi_of(2)
            hi_of(3)
            act.wait_ge(dtr_ready, 1)
            own.link(fn(dtw[:, 1, :], dtw[:, 0, :], ACT.Abs))
            fn(dtw[:, 2, :], dtw[:, 1, :], ACT.Exp, scale=-1.0).then_inc(sp_exp, 1)
            fn(expa[:, :], A("alog"), ACT.Exp).then_inc(sp_exp, 1)
            act.wait_ge(sp_u, 1)
            fn(dtw[:, 4, :], dtw[:, 3, :], ACT.Ln).then_inc(sp_ln, 1)
            act.wait_ge(bank_free, 2)
            norm_squares("qa")
            act.wait_ge(n_sum, norm_groups("qa"))
            norm_squares("kva")
            x0 = SEC["XBC"][0]

            def conv_tap(i):
                act.wait_ge(chunk_used, x0 + i + 1)
                if i >= 2:
                    act.wait_ge(xbc_ready, i - 1)
                for j in range(2):
                    m = 2 * i + j
                    ins = fn(cacc[:, i % 2, j], G[(use0["XBC"] + i) % 2][:, j * T:(j + 1) * T], ACT.Identity,
                             scale=cwh[:, m, 3:4], bias=cwh[:, m, 4:5])
                ins.then_inc(conv_u, 1)

            def conv_tanh(i):
                act.wait_ge(bank_free, use0["XBC"] + i + 1)
                if i >= 2:
                    act.wait_ge(xbc_ready, i - 1)
                fn(tb[:, i % 2], cacc[:, i % 2], ACT.Tanh).then_inc(conv_t, 1)

            def rows(i):
                if i >= 2:
                    act.wait_ge(seg_ready, i - 1)
                act.dma_start(Rb[:, i % 2], scr[4 * i:4 * i + 4, :].rearrange("(o h) t -> o h t", o=1)
                              .broadcast_to([P, 4, T])).then_inc(rows_in[i % 2], 16)

            for i in range(12):
                ahead(x0 + i)
                if i >= 1:
                    conv_tanh(i - 1)
                conv_tap(i)
                if i == 2:
                    norm_root("qa")
                    norm_root("kva")
                if i == 4:
                    norm_hi("qa")
                    norm_hi("kva")
                if i == 5:
                    act.wait_ge(acumT_sb, 1)
                    act.dma_start(scr, acumT[:, :]).then_inc(rows_out, 16)
                if i == 7:
                    act.wait_ge(rows_out, 16)
                    rows(0)
                    rows(1)
            conv_tanh(11)

            def gate_tanh(name, i, m):
                c, u = SEC[name][0] + i, use0[name] + i
                act.wait_ge(chunk_used, c + 1)
                for j in range(2):
                    ins = fn(gT[:, m + j, :], G[u % 2][:, j * T:(j + 1) * T], ACT.Tanh, scale=0.5,
                             bias=gbh[:, m + j:m + j + 1])
                ins.then_inc(bank_free, 1)

            for i in range(8):
                c = SEC["Z"][0] + i
                ahead(c)
                act.wait_ge(seg_ready, i + 1)
                if i >= 1:
                    act.wait_ge(m_ready, i)
                fn(seg[:, :, :], seg[:, :, :], ACT.Exp).then_inc(decay_ready, 1)
                if i + 2 < 8:
                    rows(i + 2)
                act.wait_ge(chunk_used, c + 1)
                if i >= 2:
                    act.wait_ge(bank_free, use0["Z"] + i - 1)
                fn(tb[:, i % 2], G[(use0["Z"] + i) % 2][:, :].rearrange("p (j t) -> p j t", j=2), ACT.Tanh,
                   scale=0.5).then_inc(z_t, 1)
                if i >= 3:
                    act.wait_ge(y_ready, i - 2)
                    norm_squares("y", [i - 3])
            ahead(SEC["GATE_A"][0])
            gate_tanh("GATE_A", 0, 0)
            act.wait_ge(y_ready, 6)
            norm_squares("y", [5])

            c_uq = SEC["UQ"][0]
            act.wait_ge(y_ready, 8)
            for n in range(16):
                if n in (0, 4, 8):
                    ahead(c_uq + n // 4)
                if n in (3, 7, 15):
                    act.wait_ge(chunk_used, c_uq + n // 4 + 1 if n < 8 else c_uq + 3)
                else:
                    act.wait_ge(u_ps, n + 1 - (n > 3) - (n > 7))
                bank = G[(use0["UQ"] + n) % 2]
                if n < 8:
                    fn(sqt[:, n % 2, 0:384], bank[:, 0:384], ACT.Square).then_inc(u_sq, 1)
                else:
                    kv = bank[:, :].rearrange("p (h d) -> p h d", h=4)
                    fn(sqt[:, n % 2, 0:256].rearrange("p (h d) -> p h d", h=4), kv[:, :, 0:NOPE], ACT.Square)
                    fn(vS[:, n % 2, 4 * (n // 2 % 4):4 * (n // 2 % 4) + 4, :], kv[:, :, NOPE:],
                       ACT.Copy).then_inc(u_sq, 1)
            norm_squares("y", [6, 7])
            act.wait_ge(kq_ss, 1)
            fn(rqk[:, :, :, :], rqk[:, :, :, :], ACT.Sqrt).then_inc(kq_rs, 1)

            def head_step(s):
                h = s
                if h < H_MLA:
                    act.wait_ge(qkT_ps, h + 1)
                    if h >= 2:
                        act.wait_ge(s_ps, h - 1)
                    fn(qkT[0:QK, h % 2, :], B[h % 2][0:QK, :], ACT.Copy).then_inc(qkT_sb, 1)
                h = s - 1
                if 0 <= h < H_MLA:
                    act.wait_ge(sm_ready, h + 1)
                    for tt, (a, b) in enumerate(((0, P), (P, BW))):
                        ins = fn(Sm[:, h % 3, a:b], Sm[:, h % 3, a:b], ACT.Exp, scale=qsc[:, 0, tt, h:h + 1],
                                 bias=mx[:, h % 3, 2 + tt:3 + tt], accum_out=mx[:, h % 3, 4 + tt:5 + tt])
                        ins.then_inc(p_exp, 1)
                h = s - 4
                if 0 <= h < H_MLA and h % 2:
                    act.wait_ge(o_ps, h + 1)
                    fn(ohi[:, h // 2, :], B[5][:, 0:T], ACT.Copy).then_inc(o_hi, 1)

            step = 0
            for i in range(7):
                ahead(SEC["GATE_B"][0] + i)
                if i == 0:
                    act.wait_ge(y_ready, 8)
                    norm_root("y")
                    gate_tanh("GATE_B", i, 2)
                    act.wait_ge(n_bc, NORM_ORDER.index("y") + 1)
                    for b in range(2):
                        ins = fn(ry[:, 2 * b:2 * b + 2, :], B[b][:, :].rearrange("p (g t) -> p g t", g=2), ACT.Copy)
                    ins.then_inc(y_rs, 1)
                    norm_hi("y", range(0, 2))
                    continue
                head_step(step)
                gate_tanh("GATE_B", i, 2 + 2 * i)
                head_step(step + 1)
                step += 2
                if i < 4:
                    norm_hi("y", range(2 * i, 2 * i + 2))
            for i in range(8):
                ahead(SEC["SSDP"][0] + i)
                for _ in range(1 if i == 0 else 2):
                    if step < H_MLA + 4:
                        head_step(step)
                        step += 1
            for i in range(4):
                ahead(SEC["MLAP"][0] + i)
                if i == 0:
                    act.wait_ge(chunk_used, SEC["GATE_B"][0] + 7)
                act.wait_ge(mix_ready, i + 1)
                fn(h_hi[:, 2 * i:2 * i + 2, :], mixa[:, 2 * i:2 * i + 2, :], ACT.Copy).then_inc(mix_hi, 1)
            for i in range(4):
                ahead(SEC["WO"][0] + i)
                act.wait_ge(bank_free, use0["WO"] + i + 1)
                fn(sqb["ffn"][:, 2 * i:2 * i + 2, :], xT[:, 2 * i:2 * i + 2, :], ACT.Square).then_inc(n_sq, 1)
            norm_root("ffn")
            act.wait_ge(chunk_used, SEC["UP"][0])
            norm_hi("ffn")

            c0, u0 = SEC["UP"][0], use0["UP"]

            def ffn_tap(k, par, bank, it=None):
                kk = k if it is None else it * 4 + k
                act.wait_ge(chunk_used, kk + (c0 + 1))
                if k >= 2 or it is not None:
                    act.wait_ge(f_g, kk - 1)
                for j in range(2):
                    w = fwh[:, bass.ds(kk * 2 + j, 1), :].rearrange("p a b -> p (a b)")
                    ins = fn(facc[:, par, j], G[bank][:, j * T:(j + 1) * T], ACT.Identity, scale=w[:, 2:3],
                             bias=w[:, 3:4])
                ins.then_inc(f_u, 1)

            def ffn_tanh(k, par, it=None):
                kk = k if it is None else it * 4 + k
                act.wait_ge(bank_free, kk + (u0 + 1))
                if k >= 2 or it is not None:
                    act.wait_ge(f_g, kk - 1)
                fn(ftg[:, par], facc[:, par, 0, :], ACT.Tanh).then_inc(f_t, 1)

            def ffn_hi(k, par, it=None):
                kk = k if it is None else it * 4 + k
                act.wait_ge(f_g, kk + 1)
                fn(g_hi[:, kk, :], fg[:, par], ACT.Copy).then_inc(f_hi, 1)

            ahead(c0)
            ffn_tap(0, 0, u0 % 2)
            ahead(c0 + 1)
            ffn_tanh(0, 0)
            ffn_tap(1, 1, (u0 + 1) % 2)
            with act.Fori(0, 4, 1) as i:
                for j in range(4):
                    k = 2 + j
                    ahead(c0 + k, i)
                    ffn_tanh(k - 1, (k - 1) % 2, i)
                    ffn_hi(k - 2, k % 2, i)
                    ffn_tap(k, k % 2, (u0 + k) % 2, i)
            for k in range(18, 22):
                ahead(c0 + k)
                ffn_tanh(k - 1, (k - 1) % 2)
                ffn_hi(k - 2, k % 2)
                ffn_tap(k, k % 2, (u0 + k) % 2)
            ffn_tanh(21, 1)
            ffn_hi(20, 0)
            ffn_hi(21, 1)
            c0 = SEC["DOWN"][0]
            with act.Fori(0, 3, 1) as i:
                for j in range(4):
                    ahead(c0 + j, i)
            for k in range(12, 16):
                ahead(c0 + k)

            act.dma_start(pb[:, :], params_b).then_inc(pb_in, 16)
            act.wait_ge(bank_free, use0["CKV"])
            norm_squares("x2")
            norm_root("x2")
            norm_hi("x2")
            for i in range(2):
                c = SEC["CKV"][0] + i
                ahead(c)
                act.wait_ge(chunk_used, c + 1)
                w = 512 >> i
                fn(ckv[:, 2 * i:2 * i + 2 - i, :], G[(use0["CKV"] + i) % 2][:, 0:w]
                   .rearrange("p (j t) -> p j t", j=2 - i), ACT.Copy).then_inc(bank_free, 1)
            act.wait_ge(bank_free, use0["CKV"] + 2)
            for r in range(2):
                for sh in range(2):
                    act.dma_start(cblk[sh * 64:sh * 64 + 64, r:6:2, 0:T - sh],
                                  ckv[r * 64:r * 64 + 64, :, sh:T]).then_inc(cblk_in, 16)

            def token_squares(n, name, i, heads):
                c, u = SEC[name][0] + i, use0[name] + i
                act.wait_ge(chunk_used, c + 1)
                if n >= 2:
                    act.wait_ge(t_free, n - 1)
                src = G[u % 2][:, :].rearrange("p (t h d) -> p t h d", t=2, d=HD)[:, :, 0:heads, :]
                fn(sqt2[:, n % 2].rearrange("p (t h) d -> p t h d", t=2)[:, :, 0:heads, :], src,
                   ACT.Square).then_inc(t_sq, 1)

            for i in range(6):
                ahead(SEC["TM_A"][0] + i)
                if i < 5:
                    token_squares(i, "TM_A", i, 2 if i == 4 else 4)
                if i == 3:
                    act.wait_ge(b_ready, 1)
                    fn(bT_hi[:, :, :, :, :].rearrange("p a b g n -> p (a b g n)"),
                       bT[:, :, :, :, :].rearrange("p a b g n -> p (a b g n)"), ACT.Copy).then_inc(b_hi, 1)
            ahead(SEC["TM_G"][0])
            act.wait_ge(chunk_used, SEC["TM_G"][0] + 1)
            fn(gnsa[:, :, :], G[use0["TM_G"] % 2][:, 0:P].rearrange("p (t n) -> p t n", t=2)[:, :, 0:36], ACT.Tanh,
               scale=0.5).then_inc(bank_free, 1)
            act.wait_ge(ss_ready, 1)
            fn(r2[:, :, 0:18], ss2[:, :, 0:18], ACT.Sqrt).then_inc(rs_ready, 1)
            for i in range(4):
                c = SEC["CW1"][0] + i
                ahead(c)
                if i % 2:
                    act.wait_ge(chunk_used, c + 1)
                    fn(hid[:, 0, i // 2, :], G[(use0["CW1"] + i // 2) % 2][0:3 * CG, 0:256],
                       ACT.Copy).then_inc(bank_free, 1)
            act.wait_ge(ge_in, 1)
            fn(hid[:, 1], hid[:, 1], ACT.Tanh, scale=(2.0 / np.pi) ** 0.5).then_inc(ge_t, 1)

            def nsa_step(s):
                h = s
                if h < H_NSA + 3:
                    act.wait_ge(nq_ps, h + 1)
                    if h < H_NSA:
                        if h >= 2:
                            act.wait_ge(ns_ps, h - 1)
                        ins = fn(qkT2[:, h % 2, 0:T], B[0][0:HD, 0:T], ACT.Copy)
                    if h >= 3:
                        if h < H_NSA:
                            own.sig(ins)
                        if h >= 5:
                            act.wait_ge(no_ps, h - 4)
                        ins = fn(pcT[:, (h - 3) % 2, :], B[0][0:CG, T:2 * T], ACT.Copy)
                    ins.then_inc(nq_sb, 1)
                h = s - 1
                if 0 <= h < H_NSA:
                    act.wait_ge(nm_ready, h + 1)
                    m, sc = m2[:, h % 3], qs2[:, 0, :, h]
                    for b, c0, w0, w1 in ((1, 0, P, T), (2, BW, P, T), (0, 768, CG, CG)):
                        for tt in range(TT):
                            lo = c0 + tt * w0
                            x = SN[:, h % 3, lo:lo + (w1 if tt else w0)]
                            fn(x, x, ACT.Exp, scale=sc[:, tt:tt + 1], bias=m[:, 1, 2 * b + tt:2 * b + tt + 1],
                               accum_out=m[:, 2, 2 * b + tt:2 * b + tt + 1]).then_inc(n_exp, 1)
                h = s - 4
                if 0 <= h < H_NSA and h % 2:
                    act.wait_ge(no_ps, h + 1)
                    fn(o2_hi[:, h // 2, :], B[5][:, 0:T], ACT.Copy).then_inc(no_hi, 1)

            def dil_step(s):
                u = s
                if u < H_DIL:
                    act.wait_ge(dq_ps, u + 1)
                    if u >= 2:
                        act.wait_ge(ds_ps, u - 1)
                    elif u == 0:
                        act.wait_ge(ns_ps, H_NSA)
                    fn(qkT2[:, u % 2, :], B[0][0:HD, :], ACT.Copy).then_inc(dq_sb, 1)
                u = s - 1
                if 0 <= u < H_DIL and u % 3 == 2:
                    hh = u // 3
                    act.wait_ge(dm_ready, hh + 1)
                    for g in range(DG):
                        for tt, (a, b) in enumerate(((0, P), (P, BW))):
                            x = SD[:, hh % 2, g * BW + a:g * BW + b]
                            head = 18 + g * DH + hh
                            fn(x, x, ACT.Exp, scale=qs2[:, 0, tt, head:head + 1], bias=md[:, 0, tt:tt + 1],
                               accum_out=m2[:, hh % 2, 2, 2 * g + tt:2 * g + tt + 1]).then_inc(d_exp, 1)
                u = s - 6
                if 0 <= u < H_DIL and u % 6 == 5:
                    act.wait_ge(do_ps, u + 1)
                    fn(o2_hi[:, 6 + u // 6, :], B[5][:, 0:T], ACT.Copy).then_inc(do_hi, 1)

            nsa = dil = 0
            for i in range(9):
                ahead(SEC["TM_B"][0] + i)
                if i == 1:
                    act.wait_ge(c_ss, 1)
                    fn(ssc[:, 1, :], ssc[:, 0, :], ACT.Sqrt).then_inc(c_rs, 1)
                if i == 2:
                    act.wait_ge(cT_ps, 1)
                    fn(kcT[:, :, :], B[5][0:HD, 0:3 * CG].rearrange("p (g n) -> p g n", g=3),
                       ACT.Copy).then_inc(cT_sb, 1)
                    nsa_step(nsa)
                if i > 2:
                    nsa_step(nsa)
                if i < 6:
                    token_squares(5 + i, "TM_B", i, 4)
                if i == 0:
                    act.wait_ge(kT_ps, 1)
                    for n in range(3):
                        ins = fn(kswT[:, 2 * n:2 * n + 2, :], B[1 + n][0:HD, :].rearrange("p (j t) -> p j t", j=2),
                                 ACT.Copy)
                    ins.then_inc(kT_sb, 1)
                    act.wait_ge(hT_ps, 1)
                    fn(hidT[:, :, :, :].rearrange("p a b n -> p (a b n)"), B[5][:, 0:12 * CG],
                       ACT.Copy).then_inc(hT_sb, 1)
                if i >= 2:
                    nsa_step(nsa + 1)
                    nsa += 2
            for i in range(8):
                c, u = SEC["GATE2"][0] + i, use0["GATE2"] + i
                ahead(c)
                for j in range(2):
                    if j == 1:
                        if i == 0:
                            act.wait_ge(ss_ready, 2)
                            fn(r2[:, :, 18:42], ss2[:, :, 18:42], ACT.Sqrt).then_inc(rs_ready, 1)
                        act.wait_ge(chunk_used, c + 1)
                        fn(gT2[:, 2 * i:2 * i + 2, :], G[u % 2][:, :].rearrange("p (j t) -> p j t", j=2), ACT.Tanh,
                           scale=0.5).then_inc(bank_free, 1)
                    if nsa < H_NSA + 4:
                        nsa_step(nsa)
                        nsa += 1
                    else:
                        dil_step(dil)
                        dil += 1
            while dil < H_DIL + 6:
                dil_step(dil)
                dil += 1
            for i in range(4):
                ahead(SEC["OAB"][0] + i)
                if i == 0:
                    act.wait_ge(chunk_used, SEC["OAB"][0])
                act.wait_ge(mix2_ready, i + 1)
                fn(h_hi[:, 2 * i:2 * i + 2, :], mix2[:, 2 * i:2 * i + 2, :], ACT.Copy).then_inc(mix2_hi, 1)
            for i in range(4):
                ahead(SEC["WOUT"][0] + i)
                act.wait_ge(bank_free, use0["WOUT"] + i + 1)
                fn(sqb["ffn2"][:, 2 * i:2 * i + 2, :], xT[:, 2 * i:2 * i + 2, :], ACT.Square).then_inc(n_sq, 1)
            norm_root("ffn2")
            act.wait_ge(chunk_used, SEC["UP2"][0])
            norm_hi("ffn2")
            c0, u0 = SEC["UP2"][0], use0["UP2"]

            def relu(k, par, bank, it=None):
                kk = k if it is None else it * 4 + k
                act.wait_ge(chunk_used, kk + (c0 + 1))
                if k >= 2 or it is not None:
                    act.wait_ge(sq_f, kk - 1)
                fn(srl[:, par], G[bank][:, :].rearrange("p (j t) -> p j t", j=2), ACT.Relu).then_inc(bank_free, 1)

            def square_hi(k, par, it=None):
                kk = k if it is None else it * 4 + k
                act.wait_ge(sq_f, kk + 1)
                fn(s_hi[:, bass.ds(kk * 2, 2), :], ssqr[:, par], ACT.Copy).then_inc(sq_hi, 1)

            for k in range(2):
                ahead(c0 + k)
                relu(k, k % 2, (u0 + k) % 2)
            square_hi(0, 0)
            with act.Fori(0, 3, 1) as i:
                for j in range(4):
                    k = 2 + j
                    ahead(c0 + k, i)
                    relu(k, k % 2, (u0 + k) % 2, i)
                    square_hi(k - 1, (k - 1) % 2, i)
            for k in range(14, 16):
                ahead(c0 + k)
                relu(k, k % 2, (u0 + k) % 2)
                square_hi(k - 1, (k - 1) % 2)
            square_hi(15, 1)
            c0 = SEC["DOWN2"][0]
            with act.Fori(0, 3, 1) as i:
                for j in range(4):
                    ahead(c0 + j, i)
            for k in range(12, 16):
                ahead(c0 + k)

        @block.vector
        def _(dve):
            v = nc.vector
            own = Tally(dve, dve_own)
            link = own.link

            def half_of(dst, src):
                return v.tensor_scalar(dst, src, 0.5, None, ALU.mult)

            def norm_inverse(name):
                t, gw, _, _ = NORMS[name]
                r0 = RS_AT.get(name, 0)
                dve.wait_ge(n_rs, NORM_ORDER.index(name) + 1)
                n = t // gw
                link(v.reciprocal(rs[:, :, r0:r0 + n], rs[:, :, r0:r0 + n]))
                for g in range(r0, r0 + n):
                    for tt in range(TT):
                        ins = v.tensor_scalar(dgb[name][:, 2 * g + tt, :], A("ident"), rs[:, tt, g:g + 1], None,
                                              ALU.mult)
                ins.then_inc(n_dg, 1)

            def norm_scale(name, pieces=None):
                t, gw, w, slots = NORMS[name]
                p0, _ = NORM_AT[name]
                src, s0, gain, hi, lo = NORM_IO[name]
                r0 = RS_AT.get(name, 0)
                if name == "y":
                    dve.wait_ge(y_rs, 1)
                    root = lambda g: ry[:, g, :]
                else:
                    dve.wait_ge(n_bc, NORM_ORDER.index("kva" if name == "qa" else name) + 1)
                    root = lambda g: B[0][:, (r0 + g) * T:(r0 + g + 1) * T]

                def scale(p):
                    if p * w >= slots:
                        dve.wait_ge(n_lo, p0 + p - slots // w + 1)
                    for k in range(p * w, p * w + w):
                        ins = v.scalar_tensor_tensor(out=hfb[name][:, k % slots, :], in0=src[:, s0 + k, :],
                                                     scalar=A(gain)[:, k:k + 1], in1=root(k // gw), op0=ALU.mult,
                                                     op1=ALU.mult)
                    ins.then_inc(n_f, 1)

                def low(p):
                    dve.wait_ge(n_hi, p0 + p + 1)
                    k = p * w
                    v.tensor_tensor(lo[:, s0 + k:s0 + k + w, :], hfb[name][:, k % slots:k % slots + w, :],
                                    hi[:, s0 + k:s0 + k + w, :], ALU.subtract).then_inc(n_lo, 1)

                pieces = list(pieces or range(t // w))
                lead = slots // w
                for n, p in enumerate(pieces):
                    if n >= lead:
                        low(pieces[n - lead])
                    scale(p)
                for p in pieces[-lead:]:
                    low(p)

            dve.wait_ge(pa_first, 16)
            dve.wait_ge(x_in, 16)
            norm_inverse("x")
            norm_scale("x")
            dve.wait_ge(pa_in, 16)
            link(half_of(cwh[:, :, 0:4], A("cw").rearrange("p (m j) -> p m j", j=4)))
            link(half_of(cwh[:, :, 4:5], A("cb").rearrange("p (m j) -> p m j", j=1)))
            link(half_of(gbh[:, :], A("gate_b")))
            fw4, fb4 = A("fw").rearrange("p (m j) -> p m j", j=3), A("fb").rearrange("p (m j) -> p m j", j=1)
            link(v.tensor_copy(fwh[:, :, 0:3], fw4))
            link(v.tensor_copy(fwh[:, :, 3:4], fb4))
            link(half_of(fwh[:, 0:44:2, 0:4], fwh[:, 0:44:2, 0:4]))

            dve.wait_ge(chunk_used, 1)
            link(v.tensor_copy(qaT[:, 2, :], G[0][:, 0:T]))
            tokm = G[0][:, T:T + 2 * 64].rearrange("p (t n) -> p t n", t=2)
            dt2 = dtw[:, 0, :].rearrange("p (t n) -> p t n", t=2)
            v.tensor_tensor(dt2, tokm[:, :, 0:32], A("dtb").unsqueeze(1).broadcast_to([P, TT, 32]),
                            ALU.add).then_inc(dtr_ready, 1)
            v.tensor_copy(kr[:, :, :], tokm[:, :, 32:64]).then_inc(bank_free, 1)
            dve.wait_ge(bank_free, 1)
            dve.wait_ge(chunk_used, 2)
            v.tensor_copy(qaT[:, 0:2, :], G[1][:, :].rearrange("p (j t) -> p j t", j=2)).then_inc(bank_free, 1)
            dve.wait_ge(bank_free, 2)
            dve.wait_ge(sp_exp, 2)
            v.tensor_scalar(dtw[:, 3, :], dtw[:, 2, :], 1.0, None, ALU.add).then_inc(sp_u, 1)
            dve.wait_ge(sp_u, 1)
            link(v.tensor_scalar(dtw[:, 5, :], dtw[:, 3, :], -1.0, None, ALU.add))
            link(v.tensor_tensor(dtw[:, 6, :], dtw[:, 2, :], dtw[:, 5, :], ALU.subtract))
            link(v.reciprocal(dtw[:, 7, :], dtw[:, 3, :]))
            link(v.tensor_tensor(dtw[:, 6, :], dtw[:, 6, :], dtw[:, 7, :], ALU.mult))
            dve.wait_ge(sp_ln, 1)
            link(v.tensor_tensor(dtw[:, 6, :], dtw[:, 6, :], dtw[:, 4, :], ALU.add))
            link(v.scalar_tensor_tensor(out=dtw[:, 0, :], in0=dtw[:, 0, :], scalar=0.0, in1=dtw[:, 6, :], op0=ALU.max,
                                        op1=ALU.add))
            link(v.scalar_tensor_tensor(out=a_tok[:, 0, :], in0=dt2[:, 0, :], scalar=-1.0, in1=expa[:, :],
                                        op0=ALU.mult, op1=ALU.mult))
            v.scalar_tensor_tensor(out=a_tok[:, 1, :], in0=dt2[:, 1, :], scalar=-1.0, in1=expa[:, :],
                                   op0=ALU.mult, op1=ALU.mult).then_inc(a_ready, 1)
            for tt in range(TT):
                link(v.tensor_tensor_reduce(out=krt[:, 0:2, tt, :].rearrange("p a b -> p a b"), in0=kr[:, tt, :]
                                            .rearrange("p (a b) -> p a b", a=2), in1=kr[:, tt, :]
                                            .rearrange("p (a b) -> p a b", a=2), scale=1.0, scalar=0.0,
                                            op0=ALU.mult, op1=ALU.add, accum_out=sskr[:, tt:tt + 1]))
            link(v.tensor_tensor(krg[:, :, :], kr[:, :, :], A("g_k")[:, NOPE:QK].unsqueeze(1)
                                 .broadcast_to([P, TT, ROPE]), ALU.mult))
            cos, sin = (A(n).rearrange("p (t n) -> p t n", t=2) for n in ("cos16", "sin16"))
            HR = ROPE // 2
            link(v.tensor_tensor(krt[:, 0], krg[:, :, 0:HR], cos, ALU.mult))
            link(v.tensor_tensor(krt[:, 1], krg[:, :, HR:ROPE], sin, ALU.mult))
            link(v.tensor_tensor(krt[:, 2], krg[:, :, 0:HR], sin, ALU.mult))
            link(v.tensor_tensor(krt[:, 3], krg[:, :, HR:ROPE], cos, ALU.mult))
            link(v.tensor_tensor(krr[:, :, 0:HR], krt[:, 0], krt[:, 1], ALU.subtract))
            link(v.tensor_tensor(krr[:, :, HR:ROPE], krt[:, 2], krt[:, 3], ALU.add))

            def conv(i):
                dve.wait_ge(conv_u, i + 1)
                bank = G[(use0["XBC"] + i) % 2]
                for d in (1, 2, 3):
                    for j in range(2):
                        m, c = 2 * i + j, cacc[:, i % 2, j]
                        if d > 1:
                            own.behind(1)
                        ins = v.scalar_tensor_tensor(out=c[:, d:T], in0=bank[:, j * T:(j + 1) * T - d],
                                                     scalar=cwh[:, m, 3 - d:4 - d], in1=c[:, d:T], op0=ALU.mult,
                                                     op1=ALU.add)
                        if d < 3 or j == 0:
                            own.sig(ins)
                ins.then_inc(bank_free, 1)

            def conv_silu(i):
                dve.wait_ge(conv_t, i + 1)
                v.scalar_tensor_tensor(out=xbcT[:, 2 * i:2 * i + 2, :], in0=tb[:, i % 2], scalar=1.0,
                                       in1=cacc[:, i % 2], op0=ALU.add, op1=ALU.mult).then_inc(xbc_ready, 1)

            def scale_by_dt(i):
                dve.wait_ge(xs_tr, i + 1)
                v.tensor_tensor(xdt[:, :, 256 * i:256 * i + 256].rearrange("p t (h d) -> p t h d", d=HD_SSD),
                                B[2 + i % 2][:, :].rearrange("p (t h d) -> p t h d", t=2, d=HD_SSD),
                                dt2[:, :, 4 * i:4 * i + 4].unsqueeze(3).broadcast_to([P, TT, 4, HD_SSD]),
                                ALU.mult).then_inc(xdt_ready, 1)

            for i in range(12):
                conv(i)
                if i >= 1:
                    conv_silu(i - 1)
                if i == 2:
                    norm_inverse("qa")
                    norm_inverse("kva")
                if i == 4:
                    norm_scale("qa")
                    dve.wait_ge(n_lo, norm_end("qa"))
                    norm_scale("kva")
                if i == 2:
                    dve.wait_ge(cum_ps, 1)
                    link(v.tensor_copy(acum[:, :, :], B[4][:, 0:64].rearrange("p (t n) -> p t n", t=2)))
                    v.tensor_copy(acumT[:, :], B[4][0:32, 128:384]).then_inc(acumT_sb, 1)
                if 3 <= i < 11:
                    scale_by_dt(i - 3)
            conv_silu(11)

            keep = A("keep")

            def seg_step(i):
                dve.wait_ge(rows_in[i % 2], 16 * (i // 2 + 1))
                if i >= 1:
                    dve.wait_ge(m_ready, i)
                for h in range(4):
                    for tt, (a, b, lo) in enumerate(((0, T, 0), (T, BW, P))):
                        ins = v.tensor_scalar(seg[:, h, a:b], Rb[:, i % 2, h, lo:T],
                                              acum[:, tt, 4 * i + h:4 * i + h + 1], 0.0, ALU.subtract, ALU.min)
                ins.then_inc(seg_ready, 1)

            def m_step(i):
                dve.wait_ge(decay_ready, i + 1)
                if i >= 2:
                    dve.wait_ge(y_ps, i - 1)
                v.tensor_tensor(Mt[:, i % 2], seg[:, :, :], scM[:, i // 2].unsqueeze(1).broadcast_to([P, 4, BW]),
                                ALU.mult).then_inc(m_ready, 1)

            def y_step(i):
                dve.wait_ge(y_ps, i + 1)
                dve.wait_ge(bank_free, use0["Z"] + i + 1)
                for j in range(2):
                    m = 2 * i + j
                    link(v.scalar_tensor_tensor(out=xbcT[:, m, :], in0=xbcT[:, m, :], scalar=A("dskip")[:, m:m + 1],
                                                in1=B[4 + i % 2][:, j * T:(j + 1) * T], op0=ALU.mult, op1=ALU.add))
                v.tensor_tensor(xbcT[:, 2 * i:2 * i + 2, :], xbcT[:, 2 * i:2 * i + 2, :], zs[:, i % 2],
                                ALU.mult).then_inc(y_ready, 1)

            def z_step(i):
                dve.wait_ge(z_t, i + 1)
                if i >= 2:
                    dve.wait_ge(y_ready, i - 1)
                v.scalar_tensor_tensor(out=zs[:, i % 2], in0=tb[:, i % 2], scalar=1.0,
                                       in1=G[(use0["Z"] + i) % 2][:, :].rearrange("p (j t) -> p j t", j=2),
                                       op0=ALU.add, op1=ALU.mult).then_inc(bank_free, 1)

            for i in range(8):
                seg_step(i)
                if i == 0:
                    for g in range(NG_SSD):
                        dve.wait_ge(score_ps, g + 1)
                        v.tensor_tensor(scM[:, g], B[4 + g % 2][:, 0:BW], keep, ALU.mult).then_inc(score_sb, 1)
                    dve.wait_ge(score_sb, NG_SSD)
                m_step(i)
                if i >= 1:
                    y_step(i - 1)
                z_step(i)
            y_step(7)

            c_uq = SEC["UQ"][0]
            hd = lambda t: t.rearrange("p (h d) -> p h d", h=4)
            for n in range(16):
                dve.wait_ge(u_sq, n + 1)
                tt, h0 = n % 2, 4 * (n // 2 % 4)
                bank = G[(use0["UQ"] + n) % 2]
                hs = slice(h0, h0 + 4)
                if n < 8:
                    own.sig(v.tensor_reduce(ssq[:, 0, tt, hs], hd(sqt[:, n % 2, 0:384]), AX_X, ALU.add))
                    v.tensor_tensor(q96[:, tt, hs, :], hd(bank[:, 0:384]),
                                    A("g_q").unsqueeze(1).broadcast_to([P, 4, QK]), ALU.mult).then_inc(bank_free, 1)
                else:
                    own.sig(v.tensor_reduce(ssq[:, 1, tt, hs], hd(sqt[:, n % 2, 0:256]), AX_X, ALU.add))
                    v.tensor_tensor(k96[:, tt, hs, 0:NOPE], hd(bank[:, :])[:, :, 0:NOPE],
                                    A("g_k")[:, 0:NOPE].unsqueeze(1).broadcast_to([P, 4, NOPE]),
                                    ALU.mult).then_inc(bank_free, 1)
            dve.wait_ge(bank_free, use0["GATE_B"])
            link(v.tensor_tensor(ssq[:, 1], ssq[:, 1], sskr[:, :].unsqueeze(2).broadcast_to([P, TT, H_MLA]), ALU.add))
            link(v.tensor_scalar(rqk[:, :, :, :], ssq[:, :, :, :], 1.0 / QK, EPS, ALU.mult, ALU.add))
            v.reciprocal(rqk[:, :, :, :], rqk[:, :, :, :]).then_inc(kq_ss, 1)
            cosb, sinb = (t.unsqueeze(2).broadcast_to([P, TT, H_MLA, HR]) for t in (cos, sin))
            x1, x2 = q96[:, :, :, NOPE:NOPE + HR], q96[:, :, :, NOPE + HR:QK]
            rotation(own, v, x1, x2, cosb, sinb, rot[:, 0], rot[:, 1])
            own.wait()
            dve.wait_ge(kq_rs, 1)
            link(v.tensor_scalar(qsc[:, 0], rqk[:, 0], QK ** -0.5, None, ALU.mult))
            link(v.tensor_scalar(qsc[:, 1], rqk[:, 0], -QK ** -0.5, None, ALU.mult))
            for tt in range(TT):
                rk = rqk[:, 1, tt, :].unsqueeze(2)
                link(v.tensor_tensor(k96[:, tt, :, 0:NOPE], k96[:, tt, :, 0:NOPE], rk.broadcast_to([P, H_MLA, NOPE]),
                                     ALU.mult))
                ins = v.tensor_tensor(k96[:, tt, :, NOPE:QK], krr[:, tt, :].unsqueeze(1).broadcast_to([P, H_MLA, ROPE]),
                                      rk.broadcast_to([P, H_MLA, ROPE]), ALU.mult)
                if tt == 0:
                    link(ins)
            ins.then_inc(kq_ready, 1)
            dve.wait_ge(kq_ready, 1)

            causal = A("causal")

            def head_step(s):
                h = s - 2
                if 0 <= h < H_MLA:
                    dve.wait_ge(p_exp, 2 * h + 2)
                    m = mx[:, h % 3, :]
                    link(v.reciprocal(m[:, 6:8], m[:, 4:6]))
                    v.tensor_scalar(Sm[:, h % 3, 0:P], Sm[:, h % 3, 0:P], m[:, 6:7], None, ALU.mult)
                    v.tensor_scalar(Sm[:, h % 3, P:BW], Sm[:, h % 3, P:BW], m[:, 7:8], None,
                                    ALU.mult).then_inc(p_ready, 1)
                h = s - 1
                if 0 <= h < H_MLA:
                    dve.wait_ge(s_ps, h + 1)
                    if h >= 3:
                        dve.wait_ge(pt_ps, h - 2)
                    m, b = mx[:, h % 3, :], B[2 + h % 2]
                    for tt, (lo, hi) in enumerate(((0, P), (P, BW))):
                        own.sig(v.tensor_tensor_reduce(out=Sm[:, h % 3, lo:hi], in0=b[:, lo:hi], in1=causal[:, lo:hi],
                                                       scale=1.0, scalar=NEG, op0=ALU.add, op1=ALU.max,
                                                       accum_out=m[:, tt:tt + 1]))
                    own.wait()
                    v.tensor_tensor(m[:, 2:4], m[:, 0:2], qsc[:, 1, :, h], ALU.mult).then_inc(sm_ready, 1)
                h = s - 3
                if 0 <= h < H_MLA:
                    dve.wait_ge(pt_ps, h + 1)
                    if h >= 1:
                        dve.wait_ge(o_ps, h)
                    v.tensor_copy(PTs[:, :], B[4][:, 0:BW]).then_inc(pt_sb, 1)
                h = s - 4
                if 0 <= h < H_MLA and h % 2:
                    dve.wait_ge(o_hi, h // 2 + 1)
                    v.tensor_tensor(olo[:, h // 2, :], B[5][:, 0:T], ohi[:, h // 2, :],
                                    ALU.subtract).then_inc(o_lo, 1)

            step = 0
            for i in range(7):
                if i == 0:
                    norm_inverse("y")
                    norm_scale("y", range(0, 2))
                    continue
                head_step(step)
                head_step(step + 1)
                step += 2
                if i < 4:
                    norm_scale("y", range(2 * i, 2 * i + 2))
            dve.wait_ge(bank_free, use0["SSDP"])
            for i in range(8):
                if step < H_MLA + 4:
                    head_step(step)
                    step += 1
                dve.wait_ge(chunk_used, SEC["SSDP"][0] + i + 1)
                v.scalar_tensor_tensor(out=gT[:, i, :], in0=gT[:, i, :], scalar=1.0,
                                       in1=G[(use0["SSDP"] + i) % 2][:, 0:T], op0=ALU.add,
                                       op1=ALU.mult).then_inc(bank_free, 1)
                if step < H_MLA + 4 and i >= 1:
                    head_step(step)
                    step += 1
            two = lambda t: t.rearrange("p (j t) -> p j t", j=2)
            for i in range(4):
                dve.wait_ge(chunk_used, SEC["MLAP"][0] + i + 1)
                gm, ma = gT[:, 8 + 2 * i:10 + 2 * i, :], mixa[:, 2 * i:2 * i + 2, :]
                v.scalar_tensor_tensor(out=gm, in0=gm, scalar=1.0, in1=two(G[(use0["MLAP"] + i) % 2][:, :]),
                                       op0=ALU.add, op1=ALU.mult).then_inc(bank_free, 1)
                dve.wait_ge(bank_free, use0["MLAP"] + i + 1)
                if i == 0:
                    dve.wait_ge(qkT_sb, H_MLA)
                v.tensor_tensor(ma, gT[:, 2 * i:2 * i + 2, :], gm, ALU.add).then_inc(mix_ready, 1)
                dve.wait_ge(mix_hi, i + 1)
                v.tensor_tensor(h_lo[:, 2 * i:2 * i + 2, :], ma, h_hi[:, 2 * i:2 * i + 2, :],
                                ALU.subtract).then_inc(mix_lo, 1)
            for i in range(4):
                dve.wait_ge(chunk_used, SEC["WO"][0] + i + 1)
                x = xT[:, 2 * i:2 * i + 2, :]
                v.scalar_tensor_tensor(out=x, in0=two(G[(use0["WO"] + i) % 2][:, :]), scalar=0.5, in1=x, op0=ALU.mult,
                                       op1=ALU.add).then_inc(bank_free, 1)
            norm_inverse("ffn")
            norm_scale("ffn")

            u0 = use0["UP"]

            def ffn_conv(k, par, bank, it=None):
                kk = k if it is None else it * 4 + k
                dve.wait_ge(f_u, kk + 1)
                for d in (1, 2):
                    for j in range(2):
                        w = fwh[:, bass.ds(kk * 2 + j, 1), :].rearrange("p a b -> p (a b)")
                        c = facc[:, par, j]
                        ins = v.scalar_tensor_tensor(out=c[:, d:T], in0=G[bank][:, j * T:(j + 1) * T - d],
                                                     scalar=w[:, 2 - d:3 - d], in1=c[:, d:T], op0=ALU.mult,
                                                     op1=ALU.add)
                        if d == 1:
                            own.sig(ins)
                            if j == 1:
                                own.wait()
                ins.then_inc(bank_free, 1)

            def ffn_product(k, par, it=None):
                kk = k if it is None else it * 4 + k
                dve.wait_ge(f_t, kk + 1)
                if k >= 2 or it is not None:
                    dve.wait_ge(f_lo, kk - 1)
                link(v.scalar_tensor_tensor(out=ftg[:, par], in0=ftg[:, par], scalar=1.0, in1=facc[:, par, 0],
                                            op0=ALU.add, op1=ALU.mult))
                v.tensor_tensor(fg[:, par], ftg[:, par], facc[:, par, 1], ALU.mult).then_inc(f_g, 1)

            def ffn_lo(k, par, it=None):
                kk = k if it is None else it * 4 + k
                dve.wait_ge(f_hi, kk + 1)
                v.tensor_tensor(g_lo[:, kk, :], fg[:, par], g_hi[:, kk, :], ALU.subtract).then_inc(f_lo, 1)

            ffn_conv(0, 0, u0 % 2)
            ffn_conv(1, 1, (u0 + 1) % 2)
            ffn_product(0, 0)
            base = own.n
            with dve.Fori(0, 4, 1) as i:
                own.n = i * (4 * FFN_LINKS) + base
                for j in range(4):
                    k = 2 + j
                    ffn_conv(k, k % 2, (u0 + k) % 2, i)
                    ffn_lo(k - 2, k % 2, i)
                    ffn_product(k - 1, (k - 1) % 2, i)
            own.n = base + 16 * FFN_LINKS
            for k in range(18, 22):
                ffn_conv(k, k % 2, (u0 + k) % 2)
                ffn_lo(k - 2, k % 2)
                ffn_product(k - 1, (k - 1) % 2)
            ffn_lo(20, 0)
            ffn_product(21, 1)
            ffn_lo(21, 1)
            u0, c0 = use0["DOWN"], SEC["DOWN"][0]
            with dve.Fori(0, 4, 1) as i:
                for j in range(2):
                    dve.wait_ge(chunk_used, i * 4 + (c0 + 2 * j + 2))
                    x = xT[:, i * 2 + j, :]
                    v.tensor_tensor(x, G[(u0 + j) % 2][:, 0:T], x, ALU.add).then_inc(bank_free, 1)

            dve.wait_ge(pb_in, 16)
            dve.wait_ge(bank_free, use0["CKV"])
            norm_inverse("x2")
            norm_scale("x2")
            dve.wait_ge(n_hi, norm_end("x2"))
            link(v.memset(bT[:, :, :, :, :], 0.0))
            dve.wait_ge(cblk_in, 64)
            for kv, name in enumerate(("pos_k", "pos_v")):
                tokens = cblk[:, 3 * kv:3 * kv + 3, :].rearrange("p g (n b two) -> p g n b two", b=8, two=2)
                for half_block in range(2):
                    ins = v.tensor_tensor(
                        bT[:, kv, 8 * half_block:8 * half_block + 8, :, 0:NC].rearrange("p b g n -> p g n b"),
                        tokens[:, :, half_block:half_block + NC, :, 0],
                        Bp(name)[:, 8 * half_block:8 * half_block + 8].unsqueeze(1).unsqueeze(1)
                        .broadcast_to([P, 3, NC, 8]), ALU.add)
                    if kv + half_block < 2:
                        link(ins)
            ins.then_inc(b_ready, 1)

            cos32, sin32 = (Bp(n).rearrange("p (t n) -> p t n", t=2) for n in ("cos32", "sin32"))
            HH = HD // 2

            def rotate(x, n, cosb, sinb, t0, t1):
                x1, x2 = x[..., 0:HH], x[..., HH:HD]
                rotation(own, v, x1, x2, cosb, sinb, t0, t1)
                own.wait()

            def token_heads(n, name, i, heads, head0, gain):
                u = use0[name] + i
                dve.wait_ge(t_sq, n + 1)
                src = G[u % 2][:, :].rearrange("p (t h d) -> p t h d", t=2, d=HD)
                c0 = i * 256 if name == "TM_A" else 1536 + i * 256
                dst = tm[:, :, c0:c0 + 256].rearrange("p t (h d) -> p t h d", d=HD)
                v.tensor_reduce(ss2[:, :, head0:head0 + heads], sqt2[:, n % 2].rearrange("p (t h) d -> p t h d", t=2)
                                [:, :, 0:heads, :], AX_X, ALU.add).then_inc(t_free, 1)
                if heads < 4:
                    link(v.tensor_copy(dst[:, :, heads:4, :], src[:, :, heads:4, :]))
                v.tensor_tensor(dst[:, :, 0:heads, :], src[:, :, 0:heads, :], gain, ALU.mult).then_inc(bank_free, 1)
                dve.wait_ge(bank_free, u + 1)
                bc = lambda t: t.unsqueeze(2).broadcast_to([P, TT, heads, HH])
                if name == "TM_A":
                    rotate(dst[:, :, 0:heads, :], heads, bc(cos32), bc(sin32), rt[:, 0, :, 0:heads],
                           rt[:, 1, :, 0:heads])

            def same_gain(name):
                return Bp(name).unsqueeze(1).unsqueeze(1).broadcast_to([P, TT, 4, HD])

            def k_gain(h0, n):
                return (Bp("g_k")[:, h0 * HD:(h0 + n) * HD].rearrange("p (h d) -> p h d", d=HD).unsqueeze(1)
                        .broadcast_to([P, TT, n, HD]))

            for i in range(6):
                if i < 3:
                    token_heads(i, "TM_A", i, 4, 4 * i, same_gain("g_qa2"))
                elif i < 5:
                    token_heads(i, "TM_A", i, 4 if i == 3 else 2, 4 * i, k_gain(4 * (i - 3), 4 if i == 3 else 2))
                else:
                    u = use0["TM_A"] + i
                    dve.wait_ge(chunk_used, SEC["TM_A"][0] + i + 1)
                    v.tensor_copy(tm[:, :, 1280:1536], G[u % 2][:, :].rearrange("p (t n) -> p t n", t=2)
                                  ).then_inc(bank_free, 1)
                if i == 3:
                    dve.wait_ge(b_hi, 1)
                    flat = lambda t: t[:, :, :, :, :].rearrange("p a b g n -> p (a b g n)")
                    v.tensor_tensor(flat(bT_lo), flat(bT), flat(bT_hi), ALU.subtract).then_inc(b_lo, 1)

            def roots(lo, hi, n, k_lo, k_cols):
                link(v.tensor_scalar(ss2[:, :, lo:hi], ss2[:, :, lo:hi], 1.0 / HD, EPS, ALU.mult, ALU.add))
                v.reciprocal(ss2[:, :, lo:hi], ss2[:, :, lo:hi]).then_inc(ss_ready, 1)
                dve.wait_ge(rs_ready, n)
                link(v.tensor_scalar(qs2[:, 0, :, lo:hi], r2[:, :, lo:hi], HD ** -0.5, None, ALU.mult))
                link(v.tensor_scalar(qs2[:, 1, :, lo:hi], r2[:, :, lo:hi], -HD ** -0.5, None, ALU.mult))
                k = tm[:, :, k_cols:k_cols + (hi - k_lo) * HD].rearrange("p t (h d) -> p t h d", d=HD)
                v.tensor_tensor(k, k, r2[:, :, k_lo:hi].unsqueeze(3).broadcast_to([P, TT, hi - k_lo, HD]),
                                ALU.mult).then_inc(k_ready, 1)

            roots(0, 18, 1, 12, 768)
            dve.wait_ge(bank_free, use0["TM_G"] + 1)
            link(v.tensor_scalar(gnsa[:, :, :], gnsa[:, :, :], 0.5, 0.5, ALU.mult, ALU.add))
            dve.wait_ge(bank_free, use0["CW1"] + 2)
            link(v.tensor_tensor(hid[:, 1], hid[:, 0], hid[:, 0], ALU.mult))
            link(v.tensor_scalar(hid[:, 1], hid[:, 1], 0.044715, 1.0, ALU.mult, ALU.add))
            v.tensor_tensor(hid[:, 1], hid[:, 1], hid[:, 0], ALU.mult).then_inc(ge_in, 1)
            dve.wait_ge(ge_t, 1)
            link(v.tensor_scalar(hid[:, 1], hid[:, 1], 0.5, 0.5, ALU.mult, ALU.add))
            v.tensor_tensor(hid[:, 0], hid[:, 0], hid[:, 1], ALU.mult).then_inc(ge_done, 1)

            def compressed_keys():
                dve.wait_ge(c_ps, 1)
                ps = B[0][0:CG, 0:6 * HD].rearrange("p (k g d) -> p k g d", k=2, g=3)
                link(v.tensor_copy(vc[:, :, :], ps[:, 1]))
                link(v.tensor_copy(cn[:, 0], ps[:, 0]))
                link(v.tensor_tensor(cn[:, 1], cn[:, 0], cn[:, 0], ALU.mult))
                link(v.tensor_reduce(ssc[:, 0, :], cn[:, 1], AX_X, ALU.add))
                link(v.tensor_scalar(ssc[:, 0, :], ssc[:, 0, :], 1.0 / HD, EPS, ALU.mult, ALU.add))
                v.reciprocal(ssc[:, 0, :], ssc[:, 0, :]).then_inc(c_ss, 1)
                dve.wait_ge(c_rs, 1)
                link(v.tensor_tensor(cn[:, 0], cn[:, 0], ssc[:, 1, :].unsqueeze(2).broadcast_to([CG, 3, HD]),
                                     ALU.mult))
                link(v.tensor_tensor(cn[:, 0], cn[:, 0], Bp("g_kc")[0:CG].unsqueeze(1).broadcast_to([CG, 3, HD]),
                                     ALU.mult))
                bc = lambda name: Bp(name)[0:CG].unsqueeze(1).broadcast_to([CG, 3, HH])
                rotation(own, v, cn[:, 0, :, 0:HH], cn[:, 0, :, HH:HD], bc("cosc"), bc("sinc"), cn[:, 1, :, 0:HH],
                         cn[:, 2, :, 0:HH], cn_ready)

            any_key, no_key, cmp_add = Bp("cmp_any"), Bp("cmp_none"), Bp("cmp_add")

            def nsa_step(s):
                h = s - 2
                if 0 <= h < H_NSA:
                    dve.wait_ge(n_exp, 6 * h + 6)
                    m = m2[:, h % 3]
                    link(v.tensor_tensor(m[:, 2, 0:2], m[:, 2, 0:2], no_key, ALU.add))
                    link(v.reciprocal(m[:, 3], m[:, 2]))
                    link(v.tensor_tensor(m[:, 3].rearrange("p (b t) -> p t b", t=2),
                                         m[:, 3].rearrange("p (b t) -> p t b", t=2),
                                         gnsa[:, :, 3 * h:3 * h + 3], ALU.mult))
                    for b, c0, w0, w1 in ((1, 0, P, T), (2, BW, P, T), (0, 768, CG, CG)):
                        for tt in range(TT):
                            w, o = (w1 if tt else w0), c0 + tt * w0
                            x = SN[:, h % 3, o:o + w]
                            ins = v.tensor_scalar(x, x, m[:, 3, 2 * b + tt:2 * b + tt + 1], None, ALU.mult)
                    ins.then_inc(np_ready, 1)
                h = s - 1
                if 0 <= h < H_NSA:
                    dve.wait_ge(ns_ps, h + 1)
                    if h >= 3:
                        dve.wait_ge(npt_ps, h - 2)
                        dve.wait_ge(nq_ps, h + 1)
                    m = m2[:, h % 3]
                    for b, src, s0, c0, w0, w1, mask in ((0, B[2], BW, 768, CG, CG, cmp_add),
                                                         (1, B[1], 0, 0, P, T, causal), (2, B[2], 0, BW, P, T, causal)):
                        for tt in range(TT):
                            w, o = (w1 if tt else w0), tt * w0
                            own.sig(v.tensor_tensor_reduce(
                                out=SN[:, h % 3, c0 + o:c0 + o + w], in0=src[:, s0 + o:s0 + o + w],
                                in1=mask[:, o:o + w], scale=1.0, scalar=NEG, op0=ALU.add, op1=ALU.max,
                                accum_out=m[:, 0, 2 * b + tt:2 * b + tt + 1]))
                    own.wait()
                    link(v.tensor_tensor(m[:, 0, 0:2], m[:, 0, 0:2], any_key, ALU.mult))
                    v.tensor_tensor(m[:, 1].rearrange("p (b t) -> p b t", t=2),
                                    m[:, 0].rearrange("p (b t) -> p b t", t=2),
                                    qs2[:, 1, :, h].unsqueeze(1).broadcast_to([P, 3, TT]),
                                    ALU.mult).then_inc(nm_ready, 1)
                h = s - 3
                if 0 <= h < H_NSA:
                    dve.wait_ge(npt_ps, h + 1)
                    if h >= 2:
                        dve.wait_ge(no_ps, h - 1)
                    own.sig(v.tensor_copy(PT2[:, 2 * (h % 2), :], B[3][:, 0:BW]))
                    v.tensor_copy(PT2[:, 2 * (h % 2) + 1, :], B[4][:, 0:BW]).then_inc(npt_sb, 1)
                h = s - 4
                if 0 <= h < H_NSA and h % 2:
                    dve.wait_ge(no_hi, h // 2 + 1)
                    v.tensor_tensor(o2_lo[:, h // 2, :], B[5][:, 0:T], o2_hi[:, h // 2, :],
                                    ALU.subtract).then_inc(no_lo, 1)

            dil_mask = Bp("dil")

            def dil_step(s):
                u = s - 1
                if 0 <= u < H_DIL:
                    hh, g = u // 3, u % 3
                    dve.wait_ge(ds_ps, u + 1)
                    if g == 0 and hh >= 2:
                        dve.wait_ge(dpt_ps, 3 * hh - 3)
                    if u == 0:
                        dve.wait_ge(npt_ps, H_NSA)
                        dve.wait_ge(nq_ps, H_NSA + 3)
                    m = m2[:, hh % 2]
                    for tt, (a, b) in enumerate(((0, P), (P, BW))):
                        link(v.tensor_tensor_reduce(
                            out=SD[:, hh % 2, g * BW + a:g * BW + b], in0=B[1 + u % 2][:, a:b],
                            in1=dil_mask[:, g * BW + a:g * BW + b], scale=1.0, scalar=NEG, op0=ALU.add, op1=ALU.max,
                            accum_out=m[:, 0, 2 * g + tt:2 * g + tt + 1]))
                    v.tensor_tensor(m[:, 1, 2 * g:2 * g + 2], m[:, 0, 2 * g:2 * g + 2],
                                    qs2[:, 1, :, 18 + g * DH + hh], ALU.mult).then_inc(dm_part, 1)
                    if g == 2:
                        dve.wait_ge(dm_part, u + 1)
                        v.tensor_reduce(md[:, 0, :], m[:, 1].rearrange("p (b t) -> p t b", t=2), AX_X,
                                        ALU.min).then_inc(dm_ready, 1)
                u = s - 5
                if 0 <= u < H_DIL:
                    dve.wait_ge(dpt_ps, u + 1)
                    if u >= 2:
                        dve.wait_ge(do_ps, u - 1)
                    if u == 0:
                        dve.wait_ge(no_ps, H_NSA)
                    v.tensor_copy(PT2[:, u % 2, :], B[3 + u % 2][:, 0:BW]).then_inc(dpt_sb, 1)
                u = s - 1
                if 0 <= u < H_DIL and u % 3 == 2:
                    hh = u // 3
                    dve.wait_ge(d_exp, 6 * hh + 6)
                    m = m2[:, hh % 2]
                    link(v.tensor_reduce(md[:, 1, :], m[:, 2].rearrange("p (b t) -> p t b", t=2), AX_X, ALU.add))
                    link(v.reciprocal(md[:, 1, :], md[:, 1, :]))
                    x = SD[:, hh % 2, :].rearrange("p (g n) -> p g n", g=3)
                    link(v.tensor_scalar(x[:, :, 0:P], x[:, :, 0:P], md[:, 1, 0:1], None, ALU.mult))
                    v.tensor_scalar(x[:, :, P:BW], x[:, :, P:BW], md[:, 1, 1:2], None,
                                    ALU.mult).then_inc(dp_ready, 1)
                u = s - 6
                if 0 <= u < H_DIL and u % 6 == 5:
                    dve.wait_ge(do_hi, u // 6 + 1)
                    v.tensor_tensor(o2_lo[:, 6 + u // 6, :], B[5][:, 0:T], o2_hi[:, 6 + u // 6, :],
                                    ALU.subtract).then_inc(do_lo, 1)

            nsa = dil = 0
            for i in range(9):
                if i == 1:
                    compressed_keys()
                if i >= 2:
                    nsa_step(nsa)
                if i < 6:
                    token_heads(5 + i, "TM_B", i, 4, 18 + 4 * i, same_gain("g_qb" if i < 3 else "g_kb"))
                else:
                    u = use0["TM_B"] + i
                    dve.wait_ge(chunk_used, SEC["TM_B"][0] + i + 1)
                    v.tensor_copy(tm[:, :, 1536 + 256 * i:1792 + 256 * i], G[u % 2][:, :]
                                  .rearrange("p (t n) -> p t n", t=2)).then_inc(bank_free, 1)
                if i >= 2:
                    nsa_step(nsa + 1)
                    nsa += 2
            for i in range(8):
                for j in range(2):
                    if i == 0 and j == 1:
                        dve.wait_ge(pool_own, 36)
                        roots(18, 42, 2, 30, 2304)
                    if nsa < H_NSA + 4:
                        nsa_step(nsa)
                        nsa += 1
                    else:
                        dil_step(dil)
                        dil += 1
            while dil < H_DIL + 6:
                dil_step(dil)
                dil += 1
            dve.wait_ge(bank_free, use0["OAB"])
            for i in range(4):
                for half_gates in range(2):
                    u = use0["OAB"] + 2 * i + half_gates
                    if half_gates:
                        dve.wait_ge(chunk_used, SEC["OAB"][0] + i + 1)
                    else:
                        dve.wait_ge(oab_ps, i + 1)
                    g = gT2[:, 8 * half_gates + 2 * i:8 * half_gates + 2 * i + 2, :]
                    v.scalar_tensor_tensor(out=g, in0=g, scalar=1.0, in1=two(G[u % 2][:, :]), op0=ALU.add,
                                           op1=ALU.mult).then_inc(bank_free, 1)
                dve.wait_ge(bank_free, u + 1)
                ma = mix2[:, 2 * i:2 * i + 2, :]
                v.tensor_tensor(ma, gT2[:, 2 * i:2 * i + 2, :], gT2[:, 8 + 2 * i:10 + 2 * i, :],
                                ALU.add).then_inc(mix2_ready, 1)
                dve.wait_ge(mix2_hi, i + 1)
                v.tensor_tensor(h_lo[:, 2 * i:2 * i + 2, :], ma, h_hi[:, 2 * i:2 * i + 2, :],
                                ALU.subtract).then_inc(mix2_lo, 1)
            for i in range(4):
                dve.wait_ge(chunk_used, SEC["WOUT"][0] + i + 1)
                x = xT[:, 2 * i:2 * i + 2, :]
                v.scalar_tensor_tensor(out=x, in0=two(G[(use0["WOUT"] + i) % 2][:, :]), scalar=0.5, in1=x,
                                       op0=ALU.mult, op1=ALU.add).then_inc(bank_free, 1)
            norm_inverse("ffn2")
            norm_scale("ffn2")
            u0 = use0["UP2"]

            def square(k, par, it=None):
                kk = k if it is None else it * 4 + k
                dve.wait_ge(bank_free, kk + (u0 + 1))
                if k >= 2 or it is not None:
                    dve.wait_ge(sq_lo, kk - 1)
                v.tensor_tensor(ssqr[:, par], srl[:, par], srl[:, par], ALU.mult).then_inc(sq_f, 1)
                dve.wait_ge(sq_hi, kk + 1)
                v.tensor_tensor(s_lo[:, bass.ds(kk * 2, 2), :], ssqr[:, par], s_hi[:, bass.ds(kk * 2, 2), :],
                                ALU.subtract).then_inc(sq_lo, 1)

            for k in range(2):
                square(k, k % 2)
            with dve.Fori(0, 3, 1) as i:
                for j in range(4):
                    square(2 + j, j % 2, i)
            for k in range(14, 16):
                square(k, k % 2)
            u0, c0 = use0["DOWN2"], SEC["DOWN2"][0]
            with dve.Fori(0, 4, 1) as i:
                for j in range(2):
                    dve.wait_ge(chunk_used, i * 4 + (c0 + 2 * j + 2))
                    x = xT[:, i * 2 + j, :]
                    v.tensor_tensor(x, G[(u0 + j) % 2][:, 0:T], x, ALU.add).then_inc(bank_free, 1)


def kernel(**inputs):
    import concourse.bacc as bacc
    from concourse.bass_utils import run_bass_kernel_spmd

    a = {n: np.asarray(v) for n, v in inputs.items()}
    x = a["x"].reshape(T, D)
    pa, pb = pack_params(a)
    arrays = {"wstream": pack_stream(a), "x_t": np.ascontiguousarray(_rows(x.T, KD)), "params_a": pa, "params_b": pb}
    nc = bacc.Bacc("TRN2", target_bir_lowering=False, num_devices=1)
    args = [nc.dram_tensor(n, v.shape, F32, kind="ExternalInput").ap() for n, v in arrays.items()]
    out = nc.dram_tensor("out_t", (P, KD, T), F32, kind="ExternalOutput").ap()
    blocks_kernel(nc, *args, out)
    r = run_bass_kernel_spmd(nc, [arrays], core_ids=[0])
    y = r.results[0]["out_t"]
    return np.ascontiguousarray(y.transpose(2, 1, 0).reshape(1, T, D))
```

```python
from contextlib import ExitStack

import concourse.bass as bass
import numpy as np
from concourse import mybir

F32 = mybir.dt.float32
F32R = mybir.dt.float32r
ALU = mybir.AluOpType
ACT = mybir.ActivationFunctionType
AX_X = mybir.AxisListType.X

P = 128
T = 256
TT = T // P
D = 1024
KD = D // P
EPS = 1e-6
NEG = -1e30

DI, NH_SSD, HD_SSD, NG_SSD, NS = 2048, 32, 64, 4, 128
XBC = DI + 2 * NG_SSD * NS
QL, KVL, H_MLA, NOPE, ROPE, VD = 256, 128, 16, 64, 32, 64
QK = NOPE + ROPE
FF = 2816
OFF_XBC, OFF_DT = DI, DI + XBC
OFF_QA = OFF_DT + NH_SSD
OFF_KVA = OFF_QA + QL
OFF_KR = OFF_KVA + KVL
OFF_G = OFF_KR + ROPE

H_NSA, G_NSA, HPG, HD = 12, 3, 4, 64
NC = 15
CG = 16
H_DIL, DG, DH = 12, 3, 4
DIL = ((128, 1), (512, 4), (2048, 16))

SLOT = 2048
SLOTS, AHEAD = 4, 2
BW = 384

_SIZES = [("A", 1, 1536), ("QA", 1, 2048), ("XBC", 12, 2048), ("Z", 8, 2048), ("GATE_A", 1, 2048),
          ("UQ", 2, 1536), ("UKV", 1, 2048), ("GATE_B", 7, 2048), ("SSDP", 8, 2048),
          ("MLAP", 4, 2048), ("WO", 4, 2048), ("UP", 22, 2048),
          ("DOWN", 16, 1408), ("CKV", 2, 2048), ("TM_A", 6, 2048), ("TM_G", 1, 512), ("CW1", 4, 2048),
          ("TM_B", 9, 2048), ("GATE2", 8, 2048),
          ("OA", 4, 1536), ("OB", 1, 2048), ("WOUT", 4, 2048), ("UP2", 16, 2048), ("DOWN2", 16, 2048)]
SEC = {}
_c = 0
for _name, _n, _used in _SIZES:
    SEC[_name] = (_c, _n, _used)
    _c += _n
NCHUNK = _c


def _rows(w, kt):
    return w.reshape(kt, P, -1).transpose(1, 0, 2)


def _chunks(w, kt, cols):
    r = _rows(w, kt)
    n = r.shape[2] // cols
    return r.reshape(P, kt, n, cols).transpose(2, 0, 1, 3).reshape(n, P, kt * cols)


def pack_stream(a):
    w1, w2 = a["w_in"][0], a["w_in_2"][0]
    out = np.zeros((NCHUNK, P, SLOT), np.float32)

    def put(sec, part, at=0):
        c0 = SEC[sec][0] + at
        out[c0:c0 + part.shape[0], :, :part.shape[2]] = part

    first = np.concatenate([w1[:, OFF_DT:OFF_QA], w1[:, OFF_KR:OFF_G], w1[:, OFF_KVA:OFF_KR]], axis=1)
    put("A", _chunks(first, KD, 192))
    put("QA", _chunks(w1[:, OFF_QA:OFF_KVA], KD, 256))
    put("XBC", _chunks(w1[:, OFF_XBC:OFF_DT], KD, 256))
    put("Z", _chunks(w1[:, :DI], KD, 256))
    put("UQ", _chunks(a["w_uq"][0], 2, 768))
    put("UKV", _chunks(a["w_ukv"][0], 1, 2048))
    gates = _chunks(w1[:, OFF_G:], KD, 256)
    put("GATE_A", gates[:1])
    put("GATE_B", gates[1:])
    put("SSDP", _chunks(a["w_ssd_proj"][0], 16, 128))
    put("MLAP", _chunks(a["w_mla_proj"][0], KD, 256))
    put("WO", _chunks(a["w_o"][0], KD, 256))
    up = a["w_up"][0].reshape(D, 2, FF // P, P).transpose(0, 2, 1, 3).reshape(D, 2 * FF)
    put("UP", _chunks(up, KD, 256))
    dn = _rows(a["w_down"][0], 22).reshape(P, 2, 11, KD, P).transpose(3, 1, 0, 2, 4).reshape(16, P, 11 * P)
    put("DOWN", dn)
    put("CKV", _chunks(w2[:, 768:1024], KD, 256))
    put("CKV", _chunks(w2[:, 1024:1152], KD, 128), 1)
    for n, w in enumerate((a["cmp_k_w1_2"][0], a["cmp_v_w1_2"][0])):
        put("CW1", _chunks(w[:1024], KD, 256), 2 * n)
        put("CW1", _chunks(w[1024:], KD, 256), 2 * n + 1)
    tm = np.concatenate([w2[:, 0:768], w2[:, 1152:1344], w2[:, 1536:1728], w2[:, 1344:1536], w2[:, 1728:1920],
                         w2[:, 1956:4260]], axis=1)
    tm = _chunks(tm, KD, 256)
    put("TM_A", tm[:6])
    put("TM_B", tm[6:])
    g = np.zeros((D, 64), np.float32)
    g[:, :36] = w2[:, 1920:1956]
    put("TM_G", _chunks(g, KD, 64))
    put("GATE2", _chunks(w2[:, 4260:], KD, 256))
    put("OA", _chunks(a["w_o_a_2"][0], 6, 256))
    put("OB", _chunks(a["w_o_b_2"][0], 2, D))
    put("WOUT", _chunks(a["w_out_2"][0], KD, 256))
    put("UP2", _chunks(a["w_up_2"][0], KD, 256))
    dn = _rows(a["w_down_2"][0], 32).reshape(P, 2, 16, KD, P).transpose(3, 1, 0, 2, 4).reshape(16, P, 16 * P)
    put("DOWN2", dn)
    return out


def _col(v, tiles):
    return v.reshape(tiles, P).T


def _bc(v):
    return np.broadcast_to(v.reshape(1, -1), (P, v.size))


def _tables(dim, pos, power=False):
    inv = np.float32(1.0) / (np.float32(10000.0) ** (np.arange(0, dim, 2, dtype=np.float32) / np.float32(dim)))
    if power:
        inv = np.power(np.float32(10000.0), -np.arange(dim // 2, dtype=np.float32) / np.float32(dim // 2))
    ang = np.asarray(pos, np.float32)[:, None] * inv[None, :].astype(np.float32)
    return np.cos(ang).astype(np.float32), np.sin(ang).astype(np.float32)


def _tok(t):
    return t.reshape(TT, P, -1).transpose(1, 0, 2).reshape(P, -1)


def _blocks(m):
    return np.concatenate([m[:P, :P], m[P:, :]], axis=1)


PA, PB = {}, {}


def pack_params(a):
    q, k = np.arange(T)[:, None], np.arange(T)[None, :]
    tri = (np.arange(P)[:, None] <= np.arange(P)[None, :]).astype(np.float32)
    one = np.ones((P, P), np.float32)
    c16, s16 = _tables(ROPE, np.arange(T))
    add = lambda ok: np.where(ok, 0.0, NEG).astype(np.float32)
    cw = a["conv_ssd_w"][0].reshape(4, 24, P).transpose(2, 1, 0).reshape(P, -1)
    fw = a["conv_ffn_w"][0].reshape(3, 2, 22, P).transpose(3, 2, 1, 0).reshape(P, -1)
    fb = a["conv_ffn_b"][0].reshape(2, 22, P).transpose(2, 1, 0).reshape(P, -1)
    ds = np.repeat(a["d_skip"][0], HD_SSD)
    early = [
        ("eps", _bc(np.array([EPS, 4 * EPS], np.float32))), ("g_mix", _col(a["norm_mix_g"][0], KD)),
        ("ones", one), ("ident", np.eye(P, dtype=np.float32)),
        ("cw", cw), ("cb", _col(a["conv_ssd_b"][0], 24)), ("g_qa", _col(a["q_a_norm_g"][0], 2)),
        ("g_kva", _col(a["kv_a_norm_g"][0], 1)), ("dtb", _bc(a["dt_bias"][0])), ("alog", _bc(a["a_log"][0])),
        ("keep", np.concatenate([tri, one, tri], axis=1)), ("dskip", _col(ds, 16)),
        ("g_ssd", _col(a["ssd_norm_g"][0], 16)), ("gate_b", _col(a["gate_b"][0], 16)),
        ("g_q", _bc(a["q_norm_g"][0])), ("g_k", _bc(a["k_norm_g"][0])), ("cos16", _tok(c16)), ("sin16", _tok(s16)),
        ("causal", _blocks(add(k <= q))), ("g_ffn", _col(a["norm_ffn_g"][0], KD)), ("fw", fw), ("fb", fb),
        ("g1", _col(a["norm1_g_2"][0], KD)), ("g2", _col(a["norm2_g_2"][0], KD)),
    ]
    cend = np.arange(CG) * 16 + 31
    ok = (cend[None, :] <= np.arange(T)[:, None]) & (np.arange(CG)[None, :] < NC)
    c32, s32 = _tables(HD, np.arange(T), True)
    cc, sc = _tables(HD, cend, True)
    pad = lambda t: np.concatenate([t, np.zeros((P - CG, t.shape[1]), np.float32)], axis=0)
    pos = lambda v: v.reshape(16, 2 * HD).T
    late = [
        ("pos_k", pos(a["cmp_k_pos_2"][0])), ("pos_v", pos(a["cmp_v_pos_2"][0])),
        ("w2_k", _rows(a["cmp_k_w2_2"][0], 2).reshape(P, -1)), ("w2_v", _rows(a["cmp_v_w2_2"][0], 2).reshape(P, -1)),
        ("g_kc", _bc(a["k_norm_cmp_2"][0])), ("g_qa2", _bc(a["q_norm_a_2"][0])), ("g_k", _bc(np.concatenate(
            [np.tile(a["k_norm_slc_2"][0], 3), np.tile(a["k_norm_win_2"][0], 3)]))),
        ("g_qb", _bc(a["q_norm_b_2"][0])), ("g_kb", _bc(a["k_norm_b_2"][0])),
        ("cos32", _tok(c32)), ("sin32", _tok(s32)), ("cosc", pad(cc)), ("sinc", pad(sc)),
        ("cmp_add", _tok(add(ok))), ("cmp_any", _tok(ok.any(1, keepdims=True).astype(np.float32))),
        ("cmp_none", _tok((~ok.any(1, keepdims=True)).astype(np.float32))),
        ("dil", np.concatenate([_blocks(add((k <= q) & (q - k <= w) & ((q - k) % d == 0))) for w, d in DIL], axis=1)),
    ]
    packed = []
    for parts, where in ((early, PA), (late, PB)):
        at = 0
        for name, p in parts:
            where[name] = (at, p.shape[1])
            at += p.shape[1]
        packed.append(np.ascontiguousarray(np.concatenate([p for _, p in parts], axis=1), dtype=np.float32))
    return packed


NORMS = {"x": (8, 8, 2, 8), "qa": (2, 2, 2, 4), "kva": (1, 1, 1, 4), "y": (16, 4, 2, 4), "ffn": (8, 8, 2, 8),
         "x2": (8, 8, 2, 8), "ffn2": (8, 8, 2, 8)}
NORM_AT = {}
_p = _g = 0
for _name, (_t, _gw, _w, _s) in NORMS.items():
    NORM_AT[_name] = (_p, _g)
    _p += _t // _w
    _g += _t // _gw


RS_AT = {"kva": 1}
ADDED = ("x", "ffn", "x2", "ffn2")
NORM_ORDER = list(NORMS)


def norm_groups(name):
    t, gw, _, _ = NORMS[name]
    return NORM_AT[name][1] + t // gw


def norm_end(name):
    t, _, w, _ = NORMS[name]
    return NORM_AT[name][0] + t // w


class Tally:

    def __init__(self, eng, sem):
        self.eng, self.sem, self.n = eng, sem, 0

    def sig(self, ins):
        ins.then_inc(self.sem, 1)
        self.n = self.n + 1

    def wait(self):
        self.eng.wait_ge(self.sem, self.n)

    def behind(self, k):
        self.eng.wait_ge(self.sem, self.n - k)

    def link(self, ins):
        self.sig(ins)
        self.wait()


FFN_LINKS = 3


def rotation(own, eng, x1, x2, cosb, sinb, t0, t1, done=None):
    own.sig(eng.tensor_tensor(t0, x1, sinb, ALU.mult))
    own.sig(eng.tensor_tensor(t1, x2, sinb, ALU.mult))
    own.behind(1)
    own.sig(eng.tensor_tensor(x1, x1, cosb, ALU.mult))
    own.behind(1)
    own.sig(eng.tensor_tensor(x2, x2, cosb, ALU.mult))
    own.behind(1)
    own.sig(eng.tensor_tensor(x1, x1, t1, ALU.subtract))
    own.behind(1)
    last = eng.tensor_tensor(x2, x2, t0, ALU.add)
    if done is None:
        own.sig(last)
    else:
        last.then_inc(done, 1)


def blocks_kernel(nc, wstream, x_t, params_a, params_b, out_t):
    with ExitStack() as ctx:
        def sem(name):
            return ctx.enter_context(nc.semaphore(name))

        cursor = [(nc.sbuf_base + 63) // 64 * 64]

        def fixed(name, shape, dt=F32):
            t = nc.alloc_sbuf_tensor_at(name, shape, dt, offset=cursor[0])
            cursor[0] += (int(np.prod(shape[1:])) * 4 + 31) // 32 * 32
            return t

        ring = cursor[0]
        raw = fixed("raw", [P, SLOTS, SLOT])
        w_hi = fixed("w_hi", [P, SLOTS, SLOT], F32R)
        w_lo = nc.alloc_sbuf_tensor_at("w_lo", [P, SLOTS, SLOT], F32R, offset=ring)
        xT = fixed("xT", [P, KD, T])
        h_hi = fixed("h_hi", [P, KD, T], F32R)
        h_lo = fixed("h_lo", [P, KD, T], F32R)
        pa = fixed("pa", [P, params_a.shape[1]])
        rs = fixed("rs", [P, TT, 4])
        ry = fixed("ry", [P, 4, T])
        small = cursor[0]
        expa = fixed("expa", [P, NH_SSD])
        a_tok = fixed("a_tok", [P, TT, NH_SSD])
        acum = fixed("acum", [P, TT, NH_SSD])
        krr = fixed("krr", [P, TT, ROPE])
        sskr = fixed("sskr", [P, TT])
        ssq = fixed("ssq", [P, 2, TT, H_MLA])
        rqk = fixed("rqk", [P, 2, TT, H_MLA])
        qsc = fixed("qsc", [P, 2, TT, H_MLA])
        mx = fixed("mx", [P, 3, 8])
        cwh = fixed("cwh", [P, 24, 5])
        fwh = fixed("fwh", [P, 44, 4])
        gbh = fixed("gbh", [P, 16])
        end_first, cursor[0] = cursor[0], small
        ss2 = fixed("ss2", [P, TT, 42])
        r2 = fixed("r2", [P, TT, 42])
        qs2 = fixed("qs2", [P, 2, TT, 42])
        m2 = fixed("m2", [P, 3, 4, 6])
        md = fixed("md", [P, 2, 2])
        ssc = fixed("ssc", [CG, 2, 3])
        vc = fixed("vc", [CG, 3, HD])
        kcT = fixed("kcT", [HD, 3, CG])
        cursor[0] = max(cursor[0], end_first)
        ARENA, LIMIT = cursor[0], nc.sbuf_usable_end

        def at(name, kib, shape, dt=F32):
            off = ARENA + int(kib * 1024)
            assert off + int(np.prod(shape[1:])) * 4 <= LIMIT, (name, off, LIMIT)
            return nc.alloc_sbuf_tensor_at(name, shape, dt, offset=off)

        def A(name):
            o, n = PA[name]
            return pa[:, o:o + n]

        xbcT = at("xbcT", 0, [P, 24, T])
        xdt = at("xdt", 24, [P, TT, DI])
        scM = at("scM", 40, [P, NG_SSD, BW])
        Rb = at("Rb", 46, [P, 2, 4, T])
        seg = at("seg", 54, [P, 4, BW])
        Mt = at("Mt", 60, [P, 2, 4, BW])
        zs = at("zs", 78, [P, 2, 2, T])
        cacc = at("cacc", 98, [P, 2, 2, T])
        qn_hi = at("qn_hi", 84, [P, 3, T], F32R)
        qn_lo = at("qn_lo", 87, [P, 3, T], F32R)
        qaT = at("qaT", 90, [P, 3, T])
        tb = at("tb", 93, [P, 2, 2, T])
        dtw = at("dtw", 76, [P, 8, 2 * NH_SSD])
        acumT = at("acumT", 97, [NH_SSD, T])
        dk = at("dk", 104.5, [64, T])
        kr = at("kr", 82, [P, TT, ROPE])
        krg = at("krg", 82.25, [P, TT, ROPE])
        krt = at("krt", 82.5, [P, 4, TT, ROPE // 2])
        ohi = at("ohi", 0, [P, 8, T], F32R)
        olo = at("olo", 8, [P, 8, T], F32R)
        vS = at("vS", 16, [P, TT, H_MLA, VD])
        y_hi = at("y_hi", 24, [P, 16, T], F32R)
        y_lo = at("y_lo", 40, [P, 16, T], F32R)
        k96 = at("k96", 56, [P, TT, H_MLA, QK])
        q96 = at("q96", 68, [P, TT, H_MLA, QK])
        sqt = at("sqt", 80, [P, 2, 384])
        qkT = at("qkT", 80, [P, 2, 2 * T])
        rot = at("rot", 84, [P, 2, TT, H_MLA, ROPE // 2])
        Sm = at("Sm", 84, [P, 3, BW])
        PTs = at("PTs", 88.5, [P, BW])
        gT = at("gT", 90, [P, 16, T])
        mixa = at("mixa", 56, [P, KD, T])
        g_hi = at("g_hi", 0, [P, 22, T], F32R)
        g_lo = at("g_lo", 22, [P, 22, T], F32R)
        xg_hi = at("xg_hi", 44, [P, KD, T], F32R)
        xg_lo = at("xg_lo", 52, [P, KD, T], F32R)
        fub = at("fub", 92, [P, 2, 2, T])
        facc = at("facc", 84, [P, 2, 2, T])
        ftg = at("ftg", 88, [P, 2, T])
        fg = at("fg", 90, [P, 2, T])
        tm = at("tm", 0, [P, TT, 3840])
        gnsa = at("gnsa", 30, [P, TT, 3 * H_NSA])
        gnT = at("gnT", 90.375, [64, T])
        gT2 = at("gT2", 31, [P, 16, T])
        o2_hi = at("o2_hi", 47, [P, 8, T], F32R)
        o2_lo = at("o2_lo", 55, [P, 8, T], F32R)
        ckv = at("ckv", 63, [P, 3, T])
        cblk = at("cblk", 66, [P, 6, T])
        bT_hi = at("bT_hi", 72, [P, 2, 16, 3, CG], F32R)
        bT_lo = at("bT_lo", 78, [P, 2, 16, 3, CG], F32R)
        bT = at("bT", 84, [P, 2, 16, 3, CG])
        hid = at("hid", 84, [3 * CG, 2, 2, 256])
        hidT = at("hidT", 69, [P, 2, 2, 3 * CG])
        cn = at("cn", 88, [CG, 3, 3, HD])
        kswT = at("kswT", 63, [HD, 6, T])
        SN = at("SN", 69, [P, 3, 768 + 2 * CG])
        SD = at("SD", 69, [P, 2, 1152])
        PT2 = at("PT2", 78.375, [P, 4, BW])
        qkT2 = at("qkT2", 84.375, [HD, 2, 2 * T])
        pcT = at("pcT", 88.375, [CG, 2, T])
        rt = at("rt", 90.375, [P, 2, TT, 4, HD // 2])
        sqt2 = at("sqt2", 92.375, [P, 2, TT * 4, HD])
        pb = at("pb", 96.5, [P, params_b.shape[1]])
        mix2 = at("mix2", 0, [P, KD, T])
        s_hi = at("s_hi", 0, [P, 32, T], F32R)
        s_lo = at("s_lo", 32, [P, 32, T], F32R)
        xg2_hi = at("xg2_hi", 88, [P, KD, T], F32R)
        xg2_lo = at("xg2_lo", 96, [P, KD, T], F32R)
        srl = at("srl", 80, [P, 2, 2, T])
        ssqr = at("ssqr", 84, [P, 2, 2, T])

        def Bp(name):
            o, n = PB[name]
            return pb[:, o:o + n]

        sqb = {"x": at("sq_x", 0, [P, 8, T]), "qa": at("sq_qa", 24, [P, 4, T]), "y": at("sq_y", 98, [P, 4, T]),
               "ffn": at("sq_ffn", 64, [P, 8, T]), "x2": at("sq_x2", 47, [P, 8, T]),
               "ffn2": at("sq_ffn2", 64, [P, 8, T])}
        hfb = {"x": at("hf_x", 8, [P, 8, T]), "qa": at("hf_qa", 28, [P, 4, T]), "y": at("hf_y", 102, [P, 4, T]),
               "ffn": at("hf_ffn", 72, [P, 8, T]), "x2": at("hf_x2", 55, [P, 8, T]),
               "ffn2": at("hf_ffn2", 72, [P, 8, T])}
        sqb["kva"], hfb["kva"] = sqb["qa"], hfb["qa"]
        dgb = {"x": at("dg_x", 102, [P, 2, P]), "qa": at("dg_qa", 103, [P, 4, P]), "y": at("dg_y", 80, [P, 8, P]),
               "ffn": at("dg_ffn", 80, [P, 2, P]), "x2": at("dg_x2", 63, [P, 2, P]),
               "ffn2": at("dg_ffn2", 80, [P, 2, P])}
        dgb["kva"] = dgb["qa"]
        NORM_IO = {"x": (xT, 0, "g_mix", h_hi, h_lo), "qa": (qaT, 0, "g_qa", qn_hi, qn_lo),
                   "kva": (qaT, 2, "g_kva", qn_hi, qn_lo), "y": (xbcT, 0, "g_ssd", y_hi, y_lo),
                   "ffn": (xT, 0, "g_ffn", xg_hi, xg_lo), "x2": (xT, 0, "g1", h_hi, h_lo),
                   "ffn2": (xT, 0, "g2", xg2_hi, xg2_lo)}

        banks = [ctx.enter_context(nc.psum_tensor(f"bank{i}", [P, 512], F32)) for i in range(8)]
        G = banks[0:2]
        B = banks[2:8]
        HEAD_BANKS = [G[0], G[1], B[2], B[3]]

        scr = nc.dram_tensor("acum_rows", [NH_SSD, T], F32, kind="Internal").ap()

        landed = [sem(f"landed{r}") for r in range(SLOTS)]
        hi_done = sem("hi_done")
        lo_done = sem("lo_done")
        lo_shared = sem("lo_shared")
        chunk_used = sem("chunk_used")
        bank_free = sem("bank_free")
        x_in, pa_first, pa_in, pb_in = sem("x_in"), sem("pa_first"), sem("pa_in"), sem("pb_in")
        act_own, dve_own, pool_own = sem("act_own"), sem("dve_own"), sem("pool_own")
        n_sq = sem("norm_sq")
        n_add = sem("norm_squares_added")
        n_sum = sem("norm_sum")
        n_rs = sem("norm_root")
        n_dg = sem("norm_diag")
        n_bc = sem("norm_bcast")
        n_f = sem("norm_f")
        n_hi = sem("norm_hi")
        n_lo = sem("norm_lo")
        y_rs = sem("y_rs")
        dk_ps = sem("dk_ps")
        dtr_ready, sp_exp, sp_u, sp_ln = sem("dtr_ready"), sem("sp_exp"), sem("sp_u"), sem("sp_ln")
        a_ready, cum_ps, acumT_sb = sem("a_ready"), sem("cum_ps"), sem("acumT_sb")
        rows_out, rows_in0, rows_in1 = sem("rows_out"), sem("rows_in0"), sem("rows_in1")
        conv_u, conv_t, xbc_ready = sem("conv_u"), sem("conv_t"), sem("xbc_ready")
        xs_tr, xdt_ready = sem("xs_tr"), sem("xdt_ready")
        score_ps, score_sb = sem("score_ps"), sem("score_sb")
        seg_ready, decay_ready, m_ready = sem("seg_ready"), sem("decay_ready"), sem("m_ready")
        y_ps, y_ready, z_t = sem("y_ps"), sem("y_ready"), sem("z_t")
        u_ps, u_sq = sem("u_ps"), sem("u_sq")
        kq_ss, kq_rs, kq_ready = sem("kq_ss"), sem("kq_rs"), sem("kq_ready")
        qkT_ps, qkT_sb = sem("qkT_ps"), sem("qkT_sb")
        s_ps, sm_ready, p_exp, p_ready = sem("s_ps"), sem("sm_ready"), sem("p_exp"), sem("p_ready")
        pt_ps, pt_sb = sem("pt_ps"), sem("pt_sb")
        o_ps, o_hi, o_lo = sem("o_ps"), sem("o_hi"), sem("o_lo")
        mix_ready, mix_hi, mix_lo = sem("mix_ready"), sem("mix_hi"), sem("mix_lo")
        f_u, f_acc, f_t, f_g, f_hi, f_lo = sem("f_u"), sem("f_acc"), sem("f_t"), sem("f_g"), sem("f_hi"), sem("f_lo")
        cblk_in, b_ready, b_hi, b_lo = sem("cblk_in"), sem("b_ready"), sem("b_hi"), sem("b_lo")
        ge_in, ge_t, ge_done = sem("ge_in"), sem("ge_t"), sem("ge_done")
        hT_ps, hT_sb, c_ps = sem("hT_ps"), sem("hT_sb"), sem("c_ps")
        c_ss, c_rs, cn_ready = sem("c_ss"), sem("c_rs"), sem("cn_ready")
        cT_ps, cT_sb, gn_ps = sem("cT_ps"), sem("cT_sb"), sem("gn_ps")
        t_sq, t_free = sem("t_sq"), sem("t_free")
        ss_ready, rs_ready, k_ready = sem("ss_ready"), sem("rs_ready"), sem("k_ready")
        kT_ps, kT_sb = sem("kT_ps"), sem("kT_sb")
        nq_ps, nq_sb = sem("nsa_qT_ps"), sem("nsa_qT_sb")
        ns_ps, nm_ready = sem("nsa_s_ps"), sem("nsa_max_ready")
        n_exp, np_ready = sem("nsa_exp"), sem("nsa_p_ready")
        npt_ps, npt_sb = sem("nsa_pT_ps"), sem("nsa_pT_sb")
        no_ps, no_hi, no_lo = sem("nsa_o_ps"), sem("nsa_o_hi"), sem("nsa_o_lo")
        dq_ps, dq_sb = sem("dil_qkT_ps"), sem("dil_qkT_sb")
        ds_ps, dm_part, dm_ready = sem("dil_s_ps"), sem("dil_max_part"), sem("dil_max_ready")
        d_exp, dp_ready = sem("dil_exp"), sem("dil_p_ready")
        dpt_ps, dpt_sb = sem("dil_pT_ps"), sem("dil_pT_sb")
        do_ps, do_hi, do_lo = sem("dil_o_ps"), sem("dil_o_hi"), sem("dil_o_lo")
        ob_ps = sem("ob_ps")
        mix2_ready, mix2_hi, mix2_lo = sem("mix2_ready"), sem("mix2_hi"), sem("mix2_lo")
        sq_f, sq_hi, sq_lo = sem("sq_f"), sem("sq_hi"), sem("sq_lo")
        out_done = sem("out_done")
        rows_in = [rows_in0, rows_in1]

        USES = [("A", 1), ("QA", 1), ("XBC", 12), ("Z", 8), ("GATE_A", 1), ("UQ", 8), ("UKV", 8), ("GATE_B", 7),
                ("SSDP", 8), ("MLAP", 4), ("WO", 4), ("UP", 22), ("DOWN", 8), ("CKV", 2), ("TM_A", 6), ("TM_G", 1),
                ("CW1", 2), ("TM_B", 9), ("GATE2", 8), ("OA", 4), ("OB", 4), ("WOUT", 4), ("UP2", 16), ("DOWN2", 8)]
        use0, at_use = {}, 0
        for s, n in USES:
            use0[s] = at_use
            at_use += n

        block = ctx.enter_context(nc.Block())

        @block.sync
        def _(sp):
            def load(c, slot, used):
                if not isinstance(c, int) or c >= SLOTS:
                    sp.wait_ge(chunk_used, c - SLOTS + 1)
                sp.dma_start(raw[:, slot, 0:used], wstream[c, :, 0:used]).then_inc(landed[slot], 16)

            sp.dma_start(xT[:, :, :], x_t).then_inc(x_in, 16)
            for name, (c0, n, used) in SEC.items():
                loops = n // 4 if n >= 8 and c0 >= SLOTS else 0
                if loops:
                    with sp.Fori(0, loops, 1) as i:
                        for j in range(4):
                            load(i * 4 + (c0 + j), (c0 + j) % SLOTS, used)
                for c in range(c0 + 4 * loops, c0 + n):
                    load(c, c % SLOTS, used)
            for k in range(0, KD, 2):
                sp.wait_ge(bank_free, use0["DOWN2"] + k + 2)
                sp.dma_start(out_t[:, k:k + 2, :], xT[:, k:k + 2, :]).then_inc(out_done, 16)
            sp.wait_ge(out_done, 16 * KD // 2)

        @block.gpsimd
        def _(pool):
            def split_lo(c, slot, used):
                pool.wait_ge(hi_done, c + 1)
                nc.gpsimd.tensor_tensor(w_lo[:, slot, 0:used], raw[:, slot, 0:used], w_hi[:, slot, 0:used],
                                        ALU.subtract).then_inc(lo_done, 1)

            own = Tally(pool, pool_own)

            def rotate_heads(i):
                pool.wait_ge(bank_free, use0["TM_B"] + i + 1)
                x = tm[:, :, 1536 + 256 * i:1792 + 256 * i].rearrange("p t (h d) -> p t h d", d=HD)
                if own.n:
                    own.wait()
                cosb, sinb = (Bp(t).rearrange("p (t n) -> p t n", t=2).unsqueeze(2).broadcast_to([P, TT, 4, HD // 2])
                              for t in ("cos32", "sin32"))
                rotation(own, nc.gpsimd, x[..., 0:HD // 2], x[..., HD // 2:HD], cosb, sinb, rt[:, 0], rt[:, 1])

            for name, (c0, n, used) in SEC.items():
                if name == "TM_B":
                    for i in range(n):
                        split_lo(c0 + i, (c0 + i) % SLOTS, used)
                        if 0 <= i - 2 < 6:
                            rotate_heads(i - 2)
                    continue
                if name == "CW1":
                    for c in range(c0, c0 + n):
                        split_lo(c, c % SLOTS, SLOT // 2)
                    continue
                loops = n // 4 if n >= 8 else 0
                if loops:
                    with pool.Fori(0, loops, 1) as i:
                        for j in range(4):
                            split_lo(i * 4 + (c0 + j), (c0 + j) % SLOTS, used)
                for c in range(c0 + 4 * loops, c0 + n):
                    split_lo(c, c % SLOTS, used)

        @block.tensor
        def _(pe):
            mm = nc.tensor.matmul

            def split_mm(out, w, x, kts, w_first, start=True, stop=True):
                last = None
                for n, (wp, xp) in enumerate(((0, 0), (1, 0), (0, 1))):
                    for kt in kts:
                        l, r = w(wp, kt), x(xp, kt)
                        if not w_first:
                            l, r = r, l
                        last = mm(out, l, r, start=start and n == 0 and kt == kts[0],
                                  stop=stop and n == 2 and kt == kts[-1])
                return last

            def wt(slot, cols, lo, width):
                return lambda part, kt: (w_hi, w_lo)[part][:, slot, kt * cols + lo:kt * cols + lo + width]

            def ch(hi, lo, t0=0):
                return lambda part, kt: (hi, lo)[part][:, t0 + kt, :]

            def tok(hi, lo, tt, t0=0):
                return lambda part, kt: (hi, lo)[part][:, t0 + kt, tt * P:(tt + 1) * P]

            def chunk_in(c):
                pe.wait_ge(lo_done, c + 1)

            def bank_in(u):
                if not isinstance(u, int) or u >= 2:
                    pe.wait_ge(bank_free, u - 1)

            def enter(name):
                pe.wait_ge(bank_free, use0[name])

            def normed(name):
                return n_hi, n_lo, NORM_AT[name][0]

            def half(c, slot, out, j, x, cols=256):
                return split_mm(out[:, j * T:(j + 1) * T], wt(slot, cols, j * P, P), x, range(KD), True)

            def arriving_chunk(tiles, x, counts, before_last=None):
                def products(p, parts, stop=False):
                    pe.wait_ge(counts[parts[0][1]], counts[2] + p + 1)
                    for n, (out, w) in enumerate(tiles):
                        for wp, xp in parts:
                            for kt in (2 * p, 2 * p + 1):
                                last = mm(out, w(wp, kt), x(xp, kt), start=n + kt + wp + xp == 0,
                                          stop=stop and n == len(tiles) - 1 and kt == KD - 1)
                    return last

                for p in range(KD // 2):
                    products(p, ((0, 0), (1, 0)))
                    if p:
                        products(p - 1, ((0, 1),))
                if before_last:
                    before_last()
                return products(KD // 2 - 1, ((0, 1),), stop=True)

            def two_tiles(slot, out):
                return [(out[:, j * T:(j + 1) * T], wt(slot, 256, j * P, P)) for j in range(2)]

            def norm_sums(name, groups=None):
                t, gw, w, slots = NORMS[name]
                p0, g0 = NORM_AT[name]
                if name in ADDED:
                    pe.wait_ge(n_add, ADDED.index(name) + 1)
                    gw = w
                for g in groups or range(t // gw if name not in ADDED else 1):
                    col = RS_AT.get(name, 0) + g
                    for k in range(gw):
                        tile = g * gw + k
                        if tile % w == 0 and name not in ADDED:
                            pe.wait_ge(n_sq, p0 + tile // w + 1)
                        for tt in range(TT):
                            last = mm(B[tt][:, col:col + 1], sqb[name][:, tile % slots, tt * P:(tt + 1) * P],
                                      A("ones")[:, 0:1], start=k == 0, stop=k == gw - 1)
                    last.then_inc(n_sum, 1)

            def norm_broadcast(*names):
                pe.wait_ge(n_dg, NORM_ORDER.index(names[-1]) + 1)
                for name in names:
                    t, gw, _, _ = NORMS[name]
                    for g in range(t // gw):
                        col = RS_AT.get(name, 0) + g
                        for tt in range(TT):
                            c0 = (col % 2) * T + tt * P
                            last = mm(B[col // 2][:, c0:c0 + P], A("ones"), dgb[name][:, 2 * col + tt, :], start=True,
                                      stop=True)
                    last.then_inc(n_bc, 1)

            pe.wait_ge(pa_first, 16)
            norm_sums("x")
            norm_broadcast("x")
            xh = ch(h_hi, h_lo)
            c = SEC["A"][0]
            chunk_in(c)
            arriving_chunk([(G[0][:, 0:T], wt(c % SLOTS, 192, 64, P))], xh, normed("x"))
            split_mm(G[0][0:64, T:2 * T], wt(c % SLOTS, 192, 0, 64), xh, range(KD), True).then_inc(chunk_used, 1)
            c = SEC["QA"][0]
            chunk_in(c)
            half(c, c % SLOTS, G[1], 0, xh)
            pe.wait_ge(bank_free, 1)
            for tt in range(TT):
                last = nc.tensor.transpose(B[4][:, tt * 64:tt * 64 + 64], dk[:, tt * P:(tt + 1) * P],
                                           A("ident")[0:64, 0:64])
            last.then_inc(dk_ps, 1)
            half(c, c % SLOTS, G[1], 1, xh).then_inc(chunk_used, 1)

            def transposes(i):
                pe.wait_ge(xbc_ready, i + 1)
                if i >= 2:
                    pe.wait_ge(xdt_ready, i - 1)
                for j in range(2):
                    for tt in range(TT):
                        last = nc.tensor.transpose(B[2 + i % 2][:, tt * T + j * P:tt * T + (j + 1) * P],
                                                   xbcT[:, 2 * i + j, tt * P:(tt + 1) * P], A("ident"))
                last.then_inc(xs_tr, 1)

            for i in range(12):
                c = SEC["XBC"][0] + i
                chunk_in(c)
                bank_in(use0["XBC"] + i)
                b = G[(use0["XBC"] + i) % 2]
                half(c, c % SLOTS, b, 0, xh)
                if i == 0:
                    enter("XBC")
                half(c, c % SLOTS, b, 1, xh).then_inc(chunk_used, 1)
                if i == 0:
                    norm_sums("qa")
                    norm_sums("kva")
                if i == 4:
                    norm_broadcast("qa", "kva")
                if i == 1:
                    pe.wait_ge(a_ready, 1)
                    keep = A("keep")
                    mm(B[4][:, 0:32], keep[:, 0:P], a_tok[:, 0, :], start=True, stop=True)
                    mm(B[4][:, 32:64], keep[:, P:T], a_tok[:, 0, :], start=True, stop=False)
                    mm(B[4][:, 32:64], keep[:, 0:P], a_tok[:, 1, :], start=False, stop=True)
                    mm(B[4][0:32, 128:384], a_tok[:, 0, :], keep[:, 0:T], start=True, stop=False)
                    mm(B[4][0:32, 256:384], a_tok[:, 1, :], keep[:, 0:P], start=False,
                       stop=True).then_inc(cum_ps, 1)
                if 2 <= i < 10:
                    transposes(i - 2)

            def scores(g):
                if g == 0:
                    pe.wait_ge(xbc_ready, 12)
                    pe.wait_ge(acumT_sb, 1)
                if g >= 2:
                    pe.wait_ge(score_sb, g - 1)
                b = B[4 + g % 2]
                mm(b[:, 0:T], xbcT[:, 16 + g, 0:P], xbcT[:, 20 + g, :], start=True, stop=True)
                mm(b[:, T:BW], xbcT[:, 16 + g, P:T], xbcT[:, 20 + g, P:T], start=True,
                   stop=True).then_inc(score_ps, 1)

            def y_heads(i):
                pe.wait_ge(m_ready, i + 1)
                if i == 0:
                    pe.wait_ge(score_sb, NG_SSD)
                    pe.wait_ge(xdt_ready, 8)
                if i >= 2:
                    pe.wait_ge(y_ready, i - 1)
                b = B[4 + i % 2]
                for h in range(4):
                    rows = slice((h % 2) * 64, (h % 2) * 64 + 64)
                    col = (4 * i + h) * HD_SSD
                    t0 = (h // 2) * T
                    mm(b[rows, t0:t0 + T], xdt[:, 0, col:col + 64], Mt[:, i % 2, h, 0:T], start=True, stop=False)
                    last = mm(b[rows, t0 + P:t0 + T], xdt[:, 1, col:col + 64], Mt[:, i % 2, h, T:BW], start=False,
                              stop=True)
                last.then_inc(y_ps, 1)

            for i in range(9):
                name, k = ("Z", i) if i < 8 else ("GATE_A", 0)
                c, u = SEC[name][0] + k, use0[name] + k
                if i in (5, 7):
                    norm_sums("y", [i // 2 - 2])
                chunk_in(c)
                bank_in(u)
                half(c, c % SLOTS, G[u % 2], 0, xh)
                if k == 0:
                    enter(name)
                half(c, c % SLOTS, G[u % 2], 1, xh).then_inc(chunk_used, 1)
                if i == 0:
                    for g in range(NG_SSD):
                        scores(g)
                if i >= 1:
                    y_heads(i - 1)

            norm_sums("y", [2])
            enter("UQ")
            pe.wait_ge(n_lo, norm_end("kva"))
            n = 0

            def head_bank_in(n):
                if n >= len(HEAD_BANKS):
                    pe.wait_ge(bank_free, use0["UQ"] + n - len(HEAD_BANKS) + 1)
                return HEAD_BANKS[n % len(HEAD_BANKS)]

            for k in range(2):
                c = SEC["UQ"][0] + k
                chunk_in(c)
                for hf in range(2):
                    for tt in range(TT):
                        bank = head_bank_in(n)
                        last = split_mm(bank[:, 0:384], wt(c % SLOTS, 768, hf * 384, 384), tok(qn_hi, qn_lo, tt),
                                        range(2), False)
                        last.then_inc(u_ps, 1) if not (hf and tt) else last.then_inc(chunk_used, 1)
                        n += 1
            c = SEC["UKV"][0]
            chunk_in(c)
            for quarter in range(4):
                for tt in range(TT):
                    bank = head_bank_in(n)
                    last = split_mm(bank[:, :], wt(c % SLOTS, 2048, quarter * 512, 512), tok(qn_hi, qn_lo, tt, 2),
                                    range(1), False)
                    last.then_inc(u_ps, 1) if quarter + tt < 4 else last.then_inc(chunk_used, 1)
                    n += 1

            def head_step(s):
                h = s
                if h < H_MLA:
                    if h == 0:
                        pe.wait_ge(kq_ready, 1)
                        pe.wait_ge(y_rs, 1)
                    if h >= 2:
                        pe.wait_ge(qkT_sb, h - 1)
                    b = B[h % 2]
                    for j, src in enumerate((q96, k96)):
                        for tt in range(TT):
                            last = nc.tensor.transpose(b[0:QK, j * T + tt * P:j * T + (tt + 1) * P],
                                                       src[:, tt, h, :], A("ident"))
                    last.then_inc(qkT_ps, 1)
                h = s - 1
                if 0 <= h < H_MLA:
                    pe.wait_ge(qkT_sb, h + 1)
                    if h >= 2:
                        pe.wait_ge(sm_ready, h - 1)
                    b, kq = B[2 + h % 2], qkT[0:QK, h % 2, :]
                    mm(b[:, 0:P], kq[:, 0:P], kq[:, T:T + P], start=True, stop=True)
                    mm(b[:, P:BW], kq[:, P:T], kq[:, T:2 * T], start=True, stop=True).then_inc(s_ps, 1)
                h = s - 4
                if 0 <= h < H_MLA:
                    pe.wait_ge(pt_sb, h + 1)
                    if h % 2 == 0 and h >= 2:
                        pe.wait_ge(o_lo, h // 2)
                    rows = slice((h % 2) * 64, (h % 2) * 64 + 64)
                    mm(B[5][rows, 0:T], vS[:, 0, h, :], PTs[:, 0:T], start=True, stop=False)
                    mm(B[5][rows, P:T], vS[:, 1, h, :], PTs[:, T:BW], start=False, stop=True).then_inc(o_ps, 1)
                h = s - 3
                if 0 <= h < H_MLA:
                    pe.wait_ge(p_ready, h + 1)
                    if h == 0:
                        pe.wait_ge(y_ready, 8)
                    if h >= 1:
                        pe.wait_ge(pt_sb, h)
                    for n in range(3):
                        last = nc.tensor.transpose(B[4][:, n * P:(n + 1) * P], Sm[:, h % 3, n * P:(n + 1) * P],
                                                   A("ident"))
                    last.then_inc(pt_ps, 1)

            step = 0
            for i in range(7):
                c, u = SEC["GATE_B"][0] + i, use0["GATE_B"] + i
                chunk_in(c)
                bank_in(u)
                half(c, c % SLOTS, G[u % 2], 0, xh)
                if i == 0:
                    enter("GATE_B")
                if i > 1:
                    head_step(step)
                    step += 1
                half(c, c % SLOTS, G[u % 2], 1, xh).then_inc(chunk_used, 1)
                if i == 1:
                    norm_broadcast("y")
                if i:
                    head_step(step)
                    step += 1
                else:
                    norm_sums("y", [3])
            pe.wait_ge(n_lo, norm_end("y"))
            for i in range(8):
                c, u = SEC["SSDP"][0] + i, use0["SSDP"] + i
                chunk_in(c)
                bank_in(u)
                out, x = G[u % 2][:, 0:T], ch(y_hi, y_lo)
                split_mm(out, wt(c % SLOTS, P, 0, P), x, range(8), True, stop=False)
                if i == 0:
                    enter("SSDP")
                if step < H_MLA + 4:
                    head_step(step)
                    step += 1
                split_mm(out, wt(c % SLOTS, P, 0, P), x, range(8, 16), True, start=False).then_inc(chunk_used, 1)
                if step < H_MLA + 4 and i >= 1:
                    head_step(step)
                    step += 1
            pe.wait_ge(o_lo, 8)
            for i in range(4):
                c, u = SEC["MLAP"][0] + i, use0["MLAP"] + i
                chunk_in(c)
                bank_in(u)
                half(c, c % SLOTS, G[u % 2], 0, ch(ohi, olo))
                half(c, c % SLOTS, G[u % 2], 1, ch(ohi, olo)).then_inc(chunk_used, 1)
            for i in range(4):
                c, u = SEC["WO"][0] + i, use0["WO"] + i
                chunk_in(c)
                bank_in(u)
                if i == 0:
                    arriving_chunk(two_tiles(c % SLOTS, G[u % 2]), xh, (mix_hi, mix_lo, 0)).then_inc(chunk_used, 1)
                    continue
                half(c, c % SLOTS, G[u % 2], 0, xh)
                half(c, c % SLOTS, G[u % 2], 1, xh).then_inc(chunk_used, 1)


            def channel_chunk(c, slot, u, bank, x=xh):
                chunk_in(c)
                bank_in(u)
                half(c, slot, G[bank], 0, x)
                half(c, slot, G[bank], 1, x).then_inc(chunk_used, 1)

            def channel_section(name, norm, x):
                c0, n, _ = SEC[name]
                u0 = use0[name]
                chunk_in(c0)
                bank_in(u0)

                def sums():
                    norm_sums(norm)
                    enter(name)

                arriving_chunk(two_tiles(c0 % SLOTS, G[u0 % 2]), x, normed(norm), sums).then_inc(chunk_used, 1)
                c, u = c0 + 1, u0 + 1
                chunk_in(c)
                bank_in(u)
                out, w = G[u % 2][:, 0:T], wt(c % SLOTS, 256, 0, P)
                split_mm(out, w, x, range(KD // 2), True, stop=False)
                norm_broadcast(norm)
                split_mm(out, w, x, range(KD // 2, KD), True, start=False)
                half(c, c % SLOTS, G[u % 2], 1, x).then_inc(chunk_used, 1)
                c0, u0, n = c0 + 2, u0 + 2, n - 2
                with pe.Fori(0, n // 4, 1) as i:
                    for j in range(4):
                        channel_chunk(i * 4 + (c0 + j), (c0 + j) % SLOTS, i * 4 + (u0 + j), (u0 + j) % 2, x)
                for k in range(n // 4 * 4, n):
                    channel_chunk(c0 + k, (c0 + k) % SLOTS, u0 + k, (u0 + k) % 2, x)

            channel_section("UP", "ffn", ch(xg_hi, xg_lo))
            def down_section(name, kts, hi, lo, ready, total):
                c0, n, _ = SEC[name]
                u0 = use0[name]

                def tile(k, it=None):
                    for j in range(2):
                        c = c0 + 2 * k + j
                        chunk_in(c if it is None else it * 4 + c)
                        if j == 0:
                            bank_in(u0 + k if it is None else it * 2 + (u0 + k))
                        out, w, x, early = G[(u0 + k) % 2][:, 0:T], wt(c % SLOTS, P, 0, P), ch(hi, lo, j * kts), 0
                        if k == 0 and j == 0:
                            pe.wait_ge(ready, total // 2)
                        elif k == 0:
                            enter(name)
                            pe.wait_ge(ready, total - 1)
                            early = kts - 2 * kts // total
                            split_mm(out, w, x, range(early), True, start=False, stop=False)
                            pe.wait_ge(ready, total)
                        split_mm(out, w, x, range(early, kts), True, start=j == 0, stop=j == 1).then_inc(chunk_used, 1)

                tile(0)
                with pe.Fori(0, (KD - 2) // 2, 1) as i:
                    tile(1, i)
                    tile(2, i)
                tile(KD - 1)

            down_section("DOWN", 11, g_hi, g_lo, f_lo, 22)

            norm_sums("x2")
            norm_broadcast("x2")
            c, u = SEC["CKV"][0], use0["CKV"]
            chunk_in(c)
            bank_in(u)
            arriving_chunk(two_tiles(c % SLOTS, G[u % 2]), xh, normed("x2"),
                           lambda: enter("CKV")).then_inc(chunk_used, 1)
            chunk_in(c + 1)
            bank_in(u + 1)
            half(c + 1, (c + 1) % SLOTS, G[(u + 1) % 2], 0, xh, P).then_inc(chunk_used, 1)

            def token_half(c, u, tt, cols=256):
                if tt == 0:
                    chunk_in(c)
                    bank_in(u)
                last = split_mm(G[u % 2][:, tt * cols:(tt + 1) * cols], wt(c % SLOTS, cols, 0, cols),
                                tok(h_hi, h_lo, tt), range(KD), False)
                if tt:
                    last.then_inc(chunk_used, 1)

            for i in range(6):
                for tt in range(TT):
                    if i == 0 and tt:
                        enter("TM_A")
                    token_half(SEC["TM_A"][0] + i, use0["TM_A"] + i, tt)
            c, u = SEC["TM_G"][0], use0["TM_G"]
            chunk_in(c)
            enter("TM_G")
            split_mm(G[u % 2][0:64, 0:T], wt(c % SLOTS, 64, 0, 64), xh, range(KD), True).then_inc(chunk_used, 1)
            pe.wait_ge(b_lo, 1)
            for i in range(4):
                kv, k_half = i // 2, i % 2
                c, u = SEC["CW1"][0] + i, use0["CW1"] + kv
                chunk_in(c)
                pe.wait_ge(lo_shared, i + 1)
                if k_half == 0:
                    bank_in(u)
                split_mm(G[u % 2][0:3 * CG, 0:256], wt(c % SLOTS, 256, 0, 256),
                         lambda part, kt: (bT_hi, bT_lo)[part][:, kv, 8 * k_half + kt].rearrange("p g n -> p (g n)"),
                         range(KD), False, start=k_half == 0, stop=k_half == 1).then_inc(chunk_used, 1)
                if i == 1:
                    pe.wait_ge(bank_free, use0["TM_G"] + 1)
                    for tt in range(TT):
                        last = nc.tensor.transpose(B[4][:, tt * 64:tt * 64 + 64], gnT[:, tt * P:(tt + 1) * P],
                                                   A("ident")[0:64, 0:64])
                    last.then_inc(gn_ps, 1)

            def hidden_transposes():
                pe.wait_ge(ge_done, 1)
                for kv in range(2):
                    for m in range(2):
                        last = nc.tensor.transpose(B[5][:, (2 * kv + m) * 3 * CG:(2 * kv + m + 1) * 3 * CG],
                                                   hid[:, 0, kv, m * P:(m + 1) * P], A("ident")[0:3 * CG, 0:3 * CG])
                last.then_inc(hT_ps, 1)

            def second_layer():
                pe.wait_ge(hT_sb, 1)
                for kv, name in enumerate(("w2_k", "w2_v")):
                    w2 = Bp(name).rearrange("p (m d) -> p m d", m=2)
                    for g in range(G_NSA):
                        for m in range(2):
                            last = mm(B[0][0:CG, (kv * 3 + g) * HD:(kv * 3 + g + 1) * HD],
                                      hidT[:, kv, m, g * CG:(g + 1) * CG], w2[:, m, :], start=m == 0, stop=m == 1)
                last.then_inc(c_ps, 1)

            def k_transposes():
                pe.wait_ge(k_ready, 1)
                for n in range(6):
                    for tt in range(TT):
                        last = nc.tensor.transpose(B[1 + n // 2][0:HD, (n % 2) * T + tt * P:(n % 2) * T + tt * P + P],
                                                   tm[:, tt, 768 + n * HD:768 + (n + 1) * HD], A("ident"))
                last.then_inc(kT_ps, 1)

            def kc_transposes():
                pe.wait_ge(cn_ready, 1)
                for g in range(G_NSA):
                    last = nc.tensor.transpose(B[5][0:HD, g * CG:(g + 1) * CG], cn[:, 0, g, :],
                                               A("ident")[0:CG, 0:CG])
                last.then_inc(cT_ps, 1)

            def nsa_step(s):
                h = s
                if s == 1:
                    pe.wait_ge(cT_sb, 1)
                    pe.wait_ge(kT_sb, 1)
                if h < H_NSA + 3 and h >= 1:
                    pe.wait_ge(nq_sb, h)
                if h < H_NSA:
                    for tt in range(TT):
                        last = nc.tensor.transpose(B[0][0:HD, tt * P:(tt + 1) * P], tm[:, tt, h * HD:(h + 1) * HD],
                                                   A("ident"))
                if 0 <= h - 3 < H_NSA:
                    pe.wait_ge(np_ready, h - 2)
                    for tt in range(TT):
                        last = nc.tensor.transpose(B[0][0:CG, T + tt * P:T + (tt + 1) * P],
                                                   SN[:, h % 3, 768 + tt * CG:768 + (tt + 1) * CG], A("ident"))
                if h < H_NSA + 3:
                    last.then_inc(nq_ps, 1)
                h = s - 1
                if 0 <= h < H_NSA:
                    pe.wait_ge(nq_sb, h + 1)
                    if h >= 1:
                        pe.wait_ge(nm_ready, h)
                    q, g = qkT2[:, h % 2, 0:T], h // HPG
                    for n, b in enumerate((B[1], B[2])):
                        kT = kswT[:, 3 * n + g, :]
                        mm(b[:, 0:P], q[:, 0:P], kT[:, 0:P], start=True, stop=True)
                        mm(b[:, P:BW], q[:, P:T], kT, start=True, stop=True)
                    for tt in range(TT):
                        last = mm(B[2][:, BW + tt * CG:BW + (tt + 1) * CG], q[:, tt * P:(tt + 1) * P], kcT[:, g, :],
                                  start=True, stop=True)
                    last.then_inc(ns_ps, 1)
                h = s - 3
                if 0 <= h < H_NSA:
                    if h >= 1:
                        pe.wait_ge(npt_sb, h)
                    for n in range(6):
                        last = nc.tensor.transpose(B[3 + n // 3][:, n % 3 * P:(n % 3 + 1) * P],
                                                   SN[:, h % 3, n * P:(n + 1) * P], A("ident"))
                    last.then_inc(npt_ps, 1)
                h = s - 4
                if 0 <= h < H_NSA:
                    pe.wait_ge(npt_sb, h + 1)
                    pe.wait_ge(nq_sb, h + 4)
                    if h % 2 == 0 and h >= 2:
                        pe.wait_ge(no_lo, h // 2)
                    g, out = h // HPG, B[5][(h % 2) * 64:(h % 2) * 64 + 64, :]
                    for n in range(2):
                        c0 = 1152 + 192 * n + g * HD
                        pt = PT2[:, 2 * (h % 2) + n, :]
                        mm(out[:, 0:T], tm[:, 0, c0:c0 + HD], pt[:, 0:T], start=n == 0, stop=False)
                        mm(out[:, P:T], tm[:, 1, c0:c0 + HD], pt[:, T:BW], start=False, stop=False)
                    mm(out[:, 0:T], vc[:, g, :], pcT[:, h % 2, :], start=False, stop=True).then_inc(no_ps, 1)

            def dil_step(s):
                u = s
                if u < H_DIL:
                    if u == 0:
                        pe.wait_ge(k_ready, 2)
                        pe.wait_ge(nq_sb, H_NSA + 3)
                    if u >= 1:
                        pe.wait_ge(dq_sb, u)
                    for j, c0 in enumerate((1536, 2304)):
                        col = c0 + (u % 3 * DH + u // 3) * HD
                        for tt in range(TT):
                            last = nc.tensor.transpose(B[0][0:HD, j * T + tt * P:j * T + (tt + 1) * P],
                                                       tm[:, tt, col:col + HD], A("ident"))
                    last.then_inc(dq_ps, 1)
                u = s - 1
                if 0 <= u < H_DIL:
                    pe.wait_ge(dq_sb, u + 1)
                    if u == 0:
                        pe.wait_ge(nm_ready, H_NSA)
                    if u >= 2:
                        pe.wait_ge(dm_part, u - 1)
                    b, q = B[1 + u % 2], qkT2[:, u % 2, :]
                    mm(b[:, 0:P], q[:, 0:P], q[:, T:T + P], start=True, stop=True)
                    mm(b[:, P:BW], q[:, P:T], q[:, T:2 * T], start=True, stop=True).then_inc(ds_ps, 1)
                u = s - 5
                if 0 <= u < H_DIL:
                    pe.wait_ge(dp_ready, u // 3 + 1)
                    if u == 0:
                        pe.wait_ge(npt_sb, H_NSA)
                    if u >= 2:
                        pe.wait_ge(dpt_sb, u - 1)
                    for n in range(3):
                        last = nc.tensor.transpose(B[3 + u % 2][:, n * P:(n + 1) * P],
                                                   SD[:, u // 3 % 2, u % 3 * BW + n * P:u % 3 * BW + (n + 1) * P],
                                                   A("ident"))
                    last.then_inc(dpt_ps, 1)
                u = s - 6
                if 0 <= u < H_DIL:
                    hh, g = u // 3, u % 3
                    pe.wait_ge(dpt_sb, u + 1)
                    if u == 0:
                        pe.wait_ge(no_lo, H_NSA // 2)
                    if hh == 2 and g == 0:
                        pe.wait_ge(do_lo, 1)
                    out, col = B[5][(hh % 2) * 64:(hh % 2) * 64 + 64, :], 3072 + (g * DH + hh) * HD
                    mm(out[:, 0:T], tm[:, 0, col:col + HD], PT2[:, u % 2, 0:T], start=g == 0, stop=False)
                    mm(out[:, P:T], tm[:, 1, col:col + HD], PT2[:, u % 2, T:BW], start=False,
                       stop=g == 2).then_inc(do_ps, 1)

            nsa = dil = 0
            for i in range(9):
                for tt in range(TT):
                    if i == 0 and tt:
                        enter("TM_B")
                    token_half(SEC["TM_B"][0] + i, use0["TM_B"] + i, tt)
                    if i == 0:
                        (k_transposes, hidden_transposes)[tt]()
                    if i == 1 and tt == 0:
                        second_layer()
                    if i == 2 and tt == 0:
                        kc_transposes()
                    if i >= 2:
                        nsa_step(nsa)
                        nsa += 1
            for i in range(8):
                c, u = SEC["GATE2"][0] + i, use0["GATE2"] + i
                chunk_in(c)
                bank_in(u)
                for j in range(2):
                    if i == 0 and j:
                        enter("GATE2")
                    last = half(c, c % SLOTS, G[u % 2], j, xh)
                    if j:
                        last.then_inc(chunk_used, 1)
                    if nsa < H_NSA + 4:
                        nsa_step(nsa)
                        nsa += 1
                    else:
                        dil_step(dil)
                        dil += 1
            pe.wait_ge(no_lo, 6)
            for i in range(4):
                c, u = SEC["OA"][0] + i, use0["OA"] + i
                chunk_in(c)
                bank_in(u)
                for j in range(2):
                    if i == 0 and j:
                        enter("OA")
                    last = split_mm(G[u % 2][:, j * T:(j + 1) * T], wt(c % SLOTS, 256, j * P, P), ch(o2_hi, o2_lo),
                                    range(6), True)
                    if j:
                        last.then_inc(chunk_used, 1)
                    if dil < H_DIL + 6:
                        dil_step(dil)
                        dil += 1
            while dil < H_DIL + 6:
                dil_step(dil)
                dil += 1
            pe.wait_ge(do_lo, 2)
            c = SEC["OB"][0]
            chunk_in(c)
            for i in range(4):
                u = use0["OB"] + i
                bank_in(u)
                for j in range(2):
                    last = split_mm(G[u % 2][:, j * T:(j + 1) * T], wt(c % SLOTS, D, (2 * i + j) * P, P),
                                    ch(o2_hi, o2_lo, 6), range(2), True)
                last.then_inc(chunk_used if i == 3 else ob_ps, 1)
            for i in range(4):
                c, u = SEC["WOUT"][0] + i, use0["WOUT"] + i
                if i:
                    channel_chunk(c, c % SLOTS, u, u % 2)
                else:
                    chunk_in(c)
                    bank_in(u)
                    arriving_chunk(two_tiles(c % SLOTS, G[u % 2]), xh, (mix2_hi, mix2_lo, 0)).then_inc(chunk_used, 1)
            channel_section("UP2", "ffn2", ch(xg2_hi, xg2_lo))
            down_section("DOWN2", 16, s_hi, s_lo, sq_lo, 16)

        @block.scalar
        def _(act):
            fn = nc.scalar.activation
            own = Tally(act, act_own)

            def hi_of(c, it=None):
                used = next(u for c0, n, u in SEC.values() if c0 <= c < c0 + n)
                slot = c % SLOTS
                rounds = c // SLOTS + 1
                if it is None:
                    act.wait_ge(landed[slot], 16 * rounds)
                    if c >= SLOTS:
                        act.wait_ge(chunk_used, c - SLOTS + 1)
                else:
                    act.wait_ge(landed[slot], it * 16 + 16 * rounds)
                    act.wait_ge(chunk_used, it * 4 + (c - SLOTS + 1))
                fn(w_hi[:, slot, 0:used], raw[:, slot, 0:used], ACT.Copy).then_inc(hi_done, 1)

            LAST = NCHUNK - 1

            def ahead(c, it=None):
                if c + AHEAD <= LAST:
                    hi_of(c + AHEAD, it)

            def norm_squares(name, pieces=None):
                t, gw, w, slots = NORMS[name]
                p0, g0 = NORM_AT[name]
                src, s0 = NORM_IO[name][:2]
                for p in pieces or range(t // w):
                    k = p * w
                    g = k // gw
                    if k >= slots:
                        act.wait_ge(n_sum, g0 + g)
                    fn(sqb[name][:, k % slots:k % slots + w, :], src[:, s0 + k:s0 + k + w, :],
                       ACT.Square).then_inc(n_sq, 1)

            def norm_root(name):
                t, gw, _, _ = NORMS[name]
                n, r0 = t // gw, RS_AT.get(name, 0)
                eps = A("eps")[:, 1:2] if name == "y" else A("eps")[:, 0:1]
                act.wait_ge(n_sum, norm_groups(name))
                for tt in range(TT):
                    ins = fn(rs[:, tt, r0:r0 + n], B[tt][:, r0:r0 + n], ACT.Sqrt, scale=1.0 / (gw * P), bias=eps)
                ins.then_inc(n_rs, 1)

            def norm_hi(name, pieces=None):
                t, gw, w, slots = NORMS[name]
                p0, _ = NORM_AT[name]
                _, s0, _, hi, _ = NORM_IO[name]
                for p in pieces or range(t // w):
                    act.wait_ge(n_f, p0 + p + 1)
                    k = p * w
                    fn(hi[:, s0 + k:s0 + k + w, :], hfb[name][:, k % slots:k % slots + w, :],
                       ACT.Copy).then_inc(n_hi, 1)

            first = PA["cw"][0]
            act.dma_start(pa[:, 0:first], params_a[:, 0:first]).then_inc(pa_first, 16)
            act.wait_ge(x_in, 16)
            norm_squares("x")
            act.dma_start(pa[:, first:], params_a[:, first:]).then_inc(pa_in, 16)
            hi_of(0)
            act.wait_ge(pa_first, 16)
            norm_root("x")
            hi_of(1)
            norm_hi("x")
            hi_of(2)
            hi_of(3)
            act.wait_ge(dtr_ready, 1)
            own.link(fn(dtw[:, 1, :], dtw[:, 0, :], ACT.Abs))
            fn(dtw[:, 2, :], dtw[:, 1, :], ACT.Exp, scale=-1.0).then_inc(sp_exp, 1)
            fn(expa[:, :], A("alog"), ACT.Exp).then_inc(sp_exp, 1)
            act.wait_ge(sp_u, 1)
            fn(dtw[:, 4, :], dtw[:, 3, :], ACT.Ln).then_inc(sp_ln, 1)
            act.wait_ge(bank_free, 2)
            norm_squares("qa")
            act.wait_ge(n_sum, norm_groups("qa"))
            norm_squares("kva")
            x0 = SEC["XBC"][0]

            def conv_tap(i):
                act.wait_ge(chunk_used, x0 + i + 1)
                if i >= 2:
                    act.wait_ge(xbc_ready, i - 1)
                for j in range(2):
                    m = 2 * i + j
                    ins = fn(cacc[:, i % 2, j], G[(use0["XBC"] + i) % 2][:, j * T:(j + 1) * T], ACT.Identity,
                             scale=cwh[:, m, 3:4], bias=cwh[:, m, 4:5])
                ins.then_inc(conv_u, 1)

            def conv_tanh(i):
                act.wait_ge(bank_free, use0["XBC"] + i + 1)
                if i >= 2:
                    act.wait_ge(xbc_ready, i - 1)
                fn(tb[:, i % 2], cacc[:, i % 2], ACT.Tanh).then_inc(conv_t, 1)

            def rows(i):
                if i >= 2:
                    act.wait_ge(seg_ready, i - 1)
                act.dma_start(Rb[:, i % 2], scr[4 * i:4 * i + 4, :].rearrange("(o h) t -> o h t", o=1)
                              .broadcast_to([P, 4, T])).then_inc(rows_in[i % 2], 16)

            for i in range(12):
                ahead(x0 + i)
                if i >= 1:
                    conv_tanh(i - 1)
                conv_tap(i)
                if i == 2:
                    norm_root("qa")
                    norm_root("kva")
                if i == 4:
                    norm_hi("qa")
                if i == 5:
                    norm_hi("kva")
                if i == 5:
                    act.wait_ge(acumT_sb, 1)
                    act.dma_start(scr, acumT[:, :]).then_inc(rows_out, 16)
                if i == 7:
                    act.wait_ge(rows_out, 16)
                    rows(0)
                    rows(1)
            conv_tanh(11)

            def gate_tanh(name, i, m):
                c, u = SEC[name][0] + i, use0[name] + i
                act.wait_ge(chunk_used, c + 1)
                for j in range(2):
                    ins = fn(gT[:, m + j, :], G[u % 2][:, j * T:(j + 1) * T], ACT.Tanh, scale=0.5,
                             bias=gbh[:, m + j:m + j + 1])
                ins.then_inc(bank_free, 1)

            for i in range(8):
                c = SEC["Z"][0] + i
                ahead(c)
                act.wait_ge(seg_ready, i + 1)
                if i >= 1:
                    act.wait_ge(m_ready, i)
                fn(seg[:, :, :], seg[:, :, :], ACT.Exp).then_inc(decay_ready, 1)
                if i + 2 < 8:
                    rows(i + 2)
                act.wait_ge(chunk_used, c + 1)
                if i >= 2:
                    act.wait_ge(bank_free, use0["Z"] + i - 1)
                fn(tb[:, i % 2], G[(use0["Z"] + i) % 2][:, :].rearrange("p (j t) -> p j t", j=2), ACT.Tanh,
                   scale=0.5).then_inc(z_t, 1)
                if i >= 3:
                    act.wait_ge(y_ready, i - 2)
                    norm_squares("y", [i - 3])
            ahead(SEC["GATE_A"][0])
            gate_tanh("GATE_A", 0, 0)
            act.wait_ge(y_ready, 6)
            norm_squares("y", [5])

            c_uq = SEC["UQ"][0]
            act.wait_ge(y_ready, 8)
            for n in range(16):
                if n in (0, 4, 8):
                    ahead(c_uq + n // 4)
                if n in (3, 7, 15):
                    act.wait_ge(chunk_used, c_uq + n // 4 + 1 if n < 8 else c_uq + 3)
                else:
                    act.wait_ge(u_ps, n + 1 - (n > 3) - (n > 7))
                if n >= 2:
                    act.wait_ge(bank_free, use0["UQ"] + n - 1)
                bank = HEAD_BANKS[n % len(HEAD_BANKS)]
                if n < 8:
                    fn(sqt[:, n % 2, 0:384], bank[:, 0:384], ACT.Square).then_inc(u_sq, 1)
                else:
                    kv = bank[:, :].rearrange("p (h d) -> p h d", h=4)
                    fn(sqt[:, n % 2, 0:256].rearrange("p (h d) -> p h d", h=4), kv[:, :, 0:NOPE], ACT.Square)
                    fn(vS[:, n % 2, 4 * (n // 2 % 4):4 * (n // 2 % 4) + 4, :], kv[:, :, NOPE:],
                       ACT.Copy).then_inc(u_sq, 1)
            norm_squares("y", [6, 7])
            act.wait_ge(kq_ss, 1)
            fn(rqk[:, :, :, :], rqk[:, :, :, :], ACT.Sqrt).then_inc(kq_rs, 1)

            def head_step(s):
                h = s
                if h < H_MLA:
                    act.wait_ge(qkT_ps, h + 1)
                    if h >= 2:
                        act.wait_ge(s_ps, h - 1)
                    fn(qkT[0:QK, h % 2, :], B[h % 2][0:QK, :], ACT.Copy).then_inc(qkT_sb, 1)
                h = s - 1
                if 0 <= h < H_MLA:
                    act.wait_ge(sm_ready, h + 1)
                    for tt, (a, b) in enumerate(((0, P), (P, BW))):
                        ins = fn(Sm[:, h % 3, a:b], Sm[:, h % 3, a:b], ACT.Exp, scale=qsc[:, 0, tt, h:h + 1],
                                 bias=mx[:, h % 3, 2 + tt:3 + tt], accum_out=mx[:, h % 3, 4 + tt:5 + tt])
                        ins.then_inc(p_exp, 1)
                h = s - 4
                if 0 <= h < H_MLA and h % 2:
                    act.wait_ge(o_ps, h + 1)
                    fn(ohi[:, h // 2, :], B[5][:, 0:T], ACT.Copy).then_inc(o_hi, 1)

            step = 0
            for i in range(7):
                ahead(SEC["GATE_B"][0] + i)
                if i == 0:
                    act.wait_ge(y_ready, 8)
                    norm_root("y")
                    gate_tanh("GATE_B", i, 2)
                    act.wait_ge(n_bc, NORM_ORDER.index("y") + 1)
                    for b in range(2):
                        ins = fn(ry[:, 2 * b:2 * b + 2, :], B[b][:, :].rearrange("p (g t) -> p g t", g=2), ACT.Copy)
                    ins.then_inc(y_rs, 1)
                    norm_hi("y", range(0, 2))
                    continue
                if i > 1:
                    head_step(step)
                    step += 1
                gate_tanh("GATE_B", i, 2 + 2 * i)
                head_step(step)
                step += 1
                if i < 4:
                    norm_hi("y", range(2 * i, 2 * i + 2))
            for i in range(8):
                ahead(SEC["SSDP"][0] + i)
                for _ in range(1 if i == 0 else 2):
                    if step < H_MLA + 4:
                        head_step(step)
                        step += 1
            for i in range(4):
                ahead(SEC["MLAP"][0] + i)
                if i == 0:
                    act.wait_ge(chunk_used, SEC["GATE_B"][0] + 7)
                act.wait_ge(mix_ready, i + 1)
                fn(h_hi[:, 2 * i:2 * i + 2, :], mixa[:, 2 * i:2 * i + 2, :], ACT.Copy).then_inc(mix_hi, 1)
            for i in range(4):
                ahead(SEC["WO"][0] + i)
                act.wait_ge(bank_free, use0["WO"] + i + 1)
                fn(sqb["ffn"][:, 2 * i:2 * i + 2, :], xT[:, 2 * i:2 * i + 2, :], ACT.Square).then_inc(n_sq, 1)
                norm_hi("ffn", [i])

            def root_row(name):
                norm_root(name)
                act.wait_ge(n_bc, NORM_ORDER.index(name) + 1)
                fn(ry[:, 0, :], B[0][:, 0:T], ACT.Copy).then_inc(y_rs, 1)

            c0, u0 = SEC["UP"][0], use0["UP"]

            def ffn_tap(k, par, it=None):
                kk = k if it is None else it * 4 + k
                act.wait_ge(bank_free, kk + (u0 + 1))
                if k >= 2 or it is not None:
                    act.wait_ge(f_g, kk - 1)
                for j in range(2):
                    w = fwh[:, bass.ds(kk * 2 + j, 1), :].rearrange("p a b -> p (a b)")
                    ins = fn(facc[:, par, j], fub[:, par, j], ACT.Identity, scale=w[:, 2:3], bias=w[:, 3:4])
                ins.then_inc(f_u, 1)

            def ffn_tanh(k, par, it=None):
                kk = k if it is None else it * 4 + k
                act.wait_ge(f_acc, kk + 1)
                if k >= 2 or it is not None:
                    act.wait_ge(f_g, kk - 1)
                fn(ftg[:, par], facc[:, par, 0, :], ACT.Tanh).then_inc(f_t, 1)

            def ffn_hi(k, par, it=None):
                kk = k if it is None else it * 4 + k
                act.wait_ge(f_g, kk + 1)
                fn(g_hi[:, kk, :], fg[:, par], ACT.Copy).then_inc(f_hi, 1)

            ahead(c0)
            root_row("ffn")
            ffn_tap(0, 0)
            ahead(c0 + 1)
            ffn_tanh(0, 0)

            def ffn_step(k, it=None):
                ffn_tap(k, k % 2, it)
                ffn_hi(k - 1, (k - 1) % 2, it)
                ahead(c0 + k + 1, it)
                ffn_tanh(k, k % 2, it)

            for k in (1, 2):
                ffn_step(k)
            with act.Fori(0, 4, 1) as i:
                for j in range(4):
                    ffn_step(3 + j, i)
            for k in range(19, 22):
                ffn_step(k)
            ffn_hi(21, 1)
            act.dma_start(pb[:, :], params_b).then_inc(pb_in, 16)
            c0 = SEC["DOWN"][0]
            for k in range(1, 16):
                ahead(c0 + k)
                if k >= 5 and k % 4 == 1:
                    act.wait_ge(bank_free, use0["DOWN"] + k // 2)
                    norm_squares("x2", [k // 4 - 1])

            act.wait_ge(bank_free, use0["CKV"])
            norm_squares("x2", [3])
            norm_root("x2")
            norm_hi("x2")
            for i in range(2):
                c = SEC["CKV"][0] + i
                ahead(c)
                act.wait_ge(chunk_used, c + 1)
                w = 512 >> i
                fn(ckv[:, 2 * i:2 * i + 2 - i, :], G[(use0["CKV"] + i) % 2][:, 0:w]
                   .rearrange("p (j t) -> p j t", j=2 - i), ACT.Copy).then_inc(bank_free, 1)
            act.wait_ge(bank_free, use0["CKV"] + 2)
            for r in range(2):
                for sh in range(2):
                    act.dma_start(cblk[sh * 64:sh * 64 + 64, r:6:2, 0:T - sh],
                                  ckv[r * 64:r * 64 + 64, :, sh:T]).then_inc(cblk_in, 16)

            def token_squares(n, name, i, heads):
                c, u = SEC[name][0] + i, use0[name] + i
                act.wait_ge(chunk_used, c + 1)
                if n >= 2:
                    act.wait_ge(t_free, n - 1)
                src = G[u % 2][:, :].rearrange("p (t h d) -> p t h d", t=2, d=HD)[:, :, 0:heads, :]
                fn(sqt2[:, n % 2].rearrange("p (t h) d -> p t h d", t=2)[:, :, 0:heads, :], src,
                   ACT.Square).then_inc(t_sq, 1)

            for i in range(6):
                ahead(SEC["TM_A"][0] + i)
                if i < 5:
                    token_squares(i, "TM_A", i, 2 if i == 4 else 4)
                if i == 3:
                    act.wait_ge(b_ready, 1)
                    fn(bT_hi[:, :, :, :, :].rearrange("p a b g n -> p (a b g n)"),
                       bT[:, :, :, :, :].rearrange("p a b g n -> p (a b g n)"), ACT.Copy).then_inc(b_hi, 1)
            ahead(SEC["TM_G"][0])
            act.wait_ge(chunk_used, SEC["TM_G"][0] + 1)
            fn(gnT[:, :], G[use0["TM_G"] % 2][0:64, 0:T], ACT.Tanh, scale=0.5).then_inc(bank_free, 1)
            act.wait_ge(ss_ready, 1)
            fn(r2[:, :, 0:18], ss2[:, :, 0:18], ACT.Sqrt).then_inc(rs_ready, 1)
            for i in range(4):
                c = SEC["CW1"][0] + i
                ahead(c)
                if i % 2:
                    act.wait_ge(chunk_used, c + 1)
                    fn(hid[:, 0, i // 2, :], G[(use0["CW1"] + i // 2) % 2][0:3 * CG, 0:256],
                       ACT.Copy).then_inc(bank_free, 1)
            act.wait_ge(ge_in, 1)
            fn(hid[:, 1], hid[:, 1], ACT.Tanh, scale=(2.0 / np.pi) ** 0.5).then_inc(ge_t, 1)

            def nsa_step(s):
                h = s
                if h < H_NSA + 3:
                    act.wait_ge(nq_ps, h + 1)
                    if h < H_NSA:
                        if h >= 2:
                            act.wait_ge(ns_ps, h - 1)
                        ins = fn(qkT2[:, h % 2, 0:T], B[0][0:HD, 0:T], ACT.Copy)
                    if h >= 3:
                        if h < H_NSA:
                            own.sig(ins)
                        if h >= 5:
                            act.wait_ge(no_ps, h - 4)
                        ins = fn(pcT[:, (h - 3) % 2, :], B[0][0:CG, T:2 * T], ACT.Copy)
                    ins.then_inc(nq_sb, 1)
                h = s - 1
                if 0 <= h < H_NSA:
                    act.wait_ge(nm_ready, h + 1)
                    m, sc = m2[:, h % 3], qs2[:, 0, :, h]
                    for b, c0, w0, w1 in ((1, 0, P, T), (2, BW, P, T), (0, 768, CG, CG)):
                        for tt in range(TT):
                            lo = c0 + tt * w0
                            x = SN[:, h % 3, lo:lo + (w1 if tt else w0)]
                            fn(x, x, ACT.Exp, scale=sc[:, tt:tt + 1], bias=m[:, 1, 2 * b + tt:2 * b + tt + 1],
                               accum_out=m[:, 2, 2 * b + tt:2 * b + tt + 1]).then_inc(n_exp, 1)
                h = s - 4
                if 0 <= h < H_NSA and h % 2:
                    act.wait_ge(no_ps, h + 1)
                    fn(o2_hi[:, h // 2, :], B[5][:, 0:T], ACT.Copy).then_inc(no_hi, 1)

            def dil_step(s):
                u = s
                if u < H_DIL:
                    act.wait_ge(dq_ps, u + 1)
                    if u >= 2:
                        act.wait_ge(ds_ps, u - 1)
                    elif u == 0:
                        act.wait_ge(ns_ps, H_NSA)
                    fn(qkT2[:, u % 2, :], B[0][0:HD, :], ACT.Copy).then_inc(dq_sb, 1)
                u = s - 1
                if 0 <= u < H_DIL and u % 3 == 2:
                    hh = u // 3
                    act.wait_ge(dm_ready, hh + 1)
                    for g in range(DG):
                        for tt, (a, b) in enumerate(((0, P), (P, BW))):
                            x = SD[:, hh % 2, g * BW + a:g * BW + b]
                            head = 18 + g * DH + hh
                            fn(x, x, ACT.Exp, scale=qs2[:, 0, tt, head:head + 1], bias=md[:, 0, tt:tt + 1],
                               accum_out=m2[:, hh % 2, 2, 2 * g + tt:2 * g + tt + 1]).then_inc(d_exp, 1)
                u = s - 6
                if 0 <= u < H_DIL and u % 6 == 5:
                    act.wait_ge(do_ps, u + 1)
                    fn(o2_hi[:, 6 + u // 6, :], B[5][:, 0:T], ACT.Copy).then_inc(do_hi, 1)

            nsa = dil = 0
            for i in range(9):
                ahead(SEC["TM_B"][0] + i)
                if i == 1:
                    act.wait_ge(c_ss, 1)
                    fn(ssc[:, 1, :], ssc[:, 0, :], ACT.Sqrt).then_inc(c_rs, 1)
                if i == 2:
                    act.wait_ge(cT_ps, 1)
                    fn(kcT[:, :, :], B[5][0:HD, 0:3 * CG].rearrange("p (g n) -> p g n", g=3),
                       ACT.Copy).then_inc(cT_sb, 1)
                    nsa_step(nsa)
                if i > 2:
                    nsa_step(nsa)
                if i < 6:
                    token_squares(5 + i, "TM_B", i, 4)
                if i == 0:
                    act.wait_ge(kT_ps, 1)
                    for n in range(3):
                        ins = fn(kswT[:, 2 * n:2 * n + 2, :], B[1 + n][0:HD, :].rearrange("p (j t) -> p j t", j=2),
                                 ACT.Copy)
                    ins.then_inc(kT_sb, 1)
                    act.wait_ge(hT_ps, 1)
                    fn(hidT[:, :, :, :].rearrange("p a b n -> p (a b n)"), B[5][:, 0:12 * CG],
                       ACT.Copy).then_inc(hT_sb, 1)
                if i >= 2:
                    nsa_step(nsa + 1)
                    nsa += 2
            for i in range(8):
                c, u = SEC["GATE2"][0] + i, use0["GATE2"] + i
                ahead(c)
                for j in range(2):
                    if j == 1:
                        if i == 0:
                            act.wait_ge(ss_ready, 2)
                            fn(r2[:, :, 18:42], ss2[:, :, 18:42], ACT.Sqrt).then_inc(rs_ready, 1)
                        act.wait_ge(chunk_used, c + 1)
                        fn(gT2[:, 2 * i:2 * i + 2, :], G[u % 2][:, :].rearrange("p (j t) -> p j t", j=2), ACT.Tanh,
                           scale=0.5).then_inc(bank_free, 1)
                    if nsa < H_NSA + 4:
                        nsa_step(nsa)
                        nsa += 1
                    else:
                        dil_step(dil)
                        dil += 1
            for i in range(4):
                ahead(SEC["OA"][0] + i)
                for j in range(2):
                    if dil < H_DIL + 6:
                        dil_step(dil)
                        dil += 1
            while dil < H_DIL + 6:
                dil_step(dil)
                dil += 1
            ahead(SEC["OB"][0])
            act.wait_ge(chunk_used, SEC["OA"][0])
            for i in range(4):
                act.wait_ge(mix2_ready, i + 1)
                fn(h_hi[:, 2 * i:2 * i + 2, :], mix2[:, 2 * i:2 * i + 2, :], ACT.Copy).then_inc(mix2_hi, 1)
            for i in range(4):
                ahead(SEC["WOUT"][0] + i)
                act.wait_ge(bank_free, use0["WOUT"] + i + 1)
                fn(sqb["ffn2"][:, 2 * i:2 * i + 2, :], xT[:, 2 * i:2 * i + 2, :], ACT.Square).then_inc(n_sq, 1)
                norm_hi("ffn2", [i])
            c0, u0 = SEC["UP2"][0], use0["UP2"]

            def relu(k, par, bank, it=None):
                kk = k if it is None else it * 4 + k
                act.wait_ge(chunk_used, kk + (c0 + 1))
                if k >= 2 or it is not None:
                    act.wait_ge(sq_f, kk - 1)
                fn(srl[:, par], G[bank][:, :].rearrange("p (j t) -> p j t", j=2), ACT.Relu).then_inc(bank_free, 1)

            def square_hi(k, par, it=None):
                kk = k if it is None else it * 4 + k
                act.wait_ge(sq_f, kk + 1)
                fn(s_hi[:, bass.ds(kk * 2, 2), :], ssqr[:, par], ACT.Copy).then_inc(sq_hi, 1)

            ahead(c0)
            root_row("ffn2")
            relu(0, 0, u0 % 2)
            ahead(c0 + 1)
            relu(1, 1, (u0 + 1) % 2)
            square_hi(0, 0)
            with act.Fori(0, 3, 1) as i:
                for j in range(4):
                    k = 2 + j
                    ahead(c0 + k, i)
                    relu(k, k % 2, (u0 + k) % 2, i)
                    square_hi(k - 1, (k - 1) % 2, i)
            for k in range(14, 16):
                ahead(c0 + k)
                relu(k, k % 2, (u0 + k) % 2)
                square_hi(k - 1, (k - 1) % 2)
            square_hi(15, 1)
            c0 = SEC["DOWN2"][0]
            with act.Fori(0, 3, 1) as i:
                for j in range(4):
                    ahead(c0 + j, i)
            for k in range(12, 16):
                ahead(c0 + k)

        @block.vector
        def _(dve):
            v = nc.vector
            own = Tally(dve, dve_own)
            link = own.link

            def half_of(dst, src):
                return v.tensor_scalar(dst, src, 0.5, None, ALU.mult)

            def norm_inverse(name):
                t, gw, _, _ = NORMS[name]
                r0 = RS_AT.get(name, 0)
                dve.wait_ge(n_rs, NORM_ORDER.index(name) + 1)
                n = t // gw
                link(v.reciprocal(rs[:, :, r0:r0 + n], rs[:, :, r0:r0 + n]))
                for g in range(r0, r0 + n):
                    for tt in range(TT):
                        ins = v.tensor_scalar(dgb[name][:, 2 * g + tt, :], A("ident"), rs[:, tt, g:g + 1], None,
                                              ALU.mult)
                ins.then_inc(n_dg, 1)

            def add_squares(name, p):
                w = NORMS[name][2]
                dve.wait_ge(n_sq, NORM_AT[name][0] + p + 1)
                total = sqb[name][:, 0:w, :]
                ins = v.tensor_tensor(total, total, sqb[name][:, p * w:p * w + w, :], ALU.add)
                if p < 3:
                    link(ins)
                else:
                    ins.then_inc(n_add, 1)

            def scale_piece(name, p):
                t, gw, w, slots = NORMS[name]
                p0, _ = NORM_AT[name]
                src, s0, gain = NORM_IO[name][:3]
                r0 = RS_AT.get(name, 0)
                if p * w >= slots:
                    dve.wait_ge(n_lo, p0 + p - slots // w + 1)
                for k in range(p * w, p * w + w):
                    out, x, g = hfb[name][:, k % slots, :], src[:, s0 + k, :], A(gain)[:, k:k + 1]
                    if name in ("ffn", "ffn2"):
                        ins = v.tensor_scalar(out, x, g, None, ALU.mult)
                    else:
                        row = ry[:, k // gw, :] if name == "y" else B[0][:, (r0 + k // gw) * T:(r0 + k // gw + 1) * T]
                        ins = v.scalar_tensor_tensor(out=out, in0=x, scalar=g, in1=row, op0=ALU.mult, op1=ALU.mult)
                ins.then_inc(n_f, 1)

            def low_piece(name, p):
                _, _, w, slots = NORMS[name]
                p0, _ = NORM_AT[name]
                _, s0, _, hi, lo = NORM_IO[name]
                dve.wait_ge(n_hi, p0 + p + 1)
                k = p * w
                v.tensor_tensor(lo[:, s0 + k:s0 + k + w, :], hfb[name][:, k % slots:k % slots + w, :],
                                hi[:, s0 + k:s0 + k + w, :], ALU.subtract).then_inc(n_lo, 1)

            def norm_scale(name, pieces=None):
                t, _, w, slots = NORMS[name]
                if name == "y":
                    dve.wait_ge(y_rs, 1)
                else:
                    dve.wait_ge(n_bc, NORM_ORDER.index("kva" if name == "qa" else name) + 1)
                pieces = list(pieces or range(t // w))
                for n, p in enumerate(pieces):
                    scale_piece(name, p)
                    if n:
                        low_piece(name, pieces[n - 1])
                low_piece(name, pieces[-1])

            dve.wait_ge(pa_first, 16)
            dve.wait_ge(x_in, 16)
            for p in range(1, 4):
                add_squares("x", p)
            norm_inverse("x")
            norm_scale("x")
            dve.wait_ge(pa_in, 16)
            link(half_of(cwh[:, :, 0:4], A("cw").rearrange("p (m j) -> p m j", j=4)))
            link(half_of(cwh[:, :, 4:5], A("cb").rearrange("p (m j) -> p m j", j=1)))
            link(half_of(gbh[:, :], A("gate_b")))
            fw4, fb4 = A("fw").rearrange("p (m j) -> p m j", j=3), A("fb").rearrange("p (m j) -> p m j", j=1)
            link(v.tensor_copy(fwh[:, :, 0:3], fw4))
            link(v.tensor_copy(fwh[:, :, 3:4], fb4))
            link(half_of(fwh[:, 0:44:2, 0:4], fwh[:, 0:44:2, 0:4]))

            dve.wait_ge(chunk_used, 1)
            own.sig(v.tensor_copy(qaT[:, 2, :], G[0][:, 0:T]))
            v.tensor_copy(dk[:, :], G[0][0:64, T:2 * T]).then_inc(bank_free, 1)
            dve.wait_ge(dk_ps, 1)
            tokm = B[4][:, 0:2 * 64].rearrange("p (t n) -> p t n", t=2)
            dt2 = dtw[:, 0, :].rearrange("p (t n) -> p t n", t=2)
            v.tensor_tensor(dt2, tokm[:, :, 0:32], A("dtb").unsqueeze(1).broadcast_to([P, TT, 32]),
                            ALU.add).then_inc(dtr_ready, 1)
            link(v.tensor_copy(kr[:, :, :], tokm[:, :, 32:64]))
            dve.wait_ge(chunk_used, 2)
            v.tensor_copy(qaT[:, 0:2, :], G[1][:, :].rearrange("p (j t) -> p j t", j=2)).then_inc(bank_free, 1)
            dve.wait_ge(bank_free, 2)
            dve.wait_ge(sp_exp, 2)
            v.tensor_scalar(dtw[:, 3, :], dtw[:, 2, :], 1.0, None, ALU.add).then_inc(sp_u, 1)
            dve.wait_ge(sp_u, 1)
            link(v.tensor_scalar(dtw[:, 5, :], dtw[:, 3, :], -1.0, None, ALU.add))
            link(v.tensor_tensor(dtw[:, 6, :], dtw[:, 2, :], dtw[:, 5, :], ALU.subtract))
            link(v.reciprocal(dtw[:, 7, :], dtw[:, 3, :]))
            link(v.tensor_tensor(dtw[:, 6, :], dtw[:, 6, :], dtw[:, 7, :], ALU.mult))
            dve.wait_ge(sp_ln, 1)
            link(v.tensor_tensor(dtw[:, 6, :], dtw[:, 6, :], dtw[:, 4, :], ALU.add))
            link(v.scalar_tensor_tensor(out=dtw[:, 0, :], in0=dtw[:, 0, :], scalar=0.0, in1=dtw[:, 6, :], op0=ALU.max,
                                        op1=ALU.add))
            link(v.scalar_tensor_tensor(out=a_tok[:, 0, :], in0=dt2[:, 0, :], scalar=-1.0, in1=expa[:, :],
                                        op0=ALU.mult, op1=ALU.mult))
            v.scalar_tensor_tensor(out=a_tok[:, 1, :], in0=dt2[:, 1, :], scalar=-1.0, in1=expa[:, :],
                                   op0=ALU.mult, op1=ALU.mult).then_inc(a_ready, 1)
            for tt in range(TT):
                link(v.tensor_tensor_reduce(out=krt[:, 0:2, tt, :].rearrange("p a b -> p a b"), in0=kr[:, tt, :]
                                            .rearrange("p (a b) -> p a b", a=2), in1=kr[:, tt, :]
                                            .rearrange("p (a b) -> p a b", a=2), scale=1.0, scalar=0.0,
                                            op0=ALU.mult, op1=ALU.add, accum_out=sskr[:, tt:tt + 1]))
            link(v.tensor_tensor(krg[:, :, :], kr[:, :, :], A("g_k")[:, NOPE:QK].unsqueeze(1)
                                 .broadcast_to([P, TT, ROPE]), ALU.mult))
            cos, sin = (A(n).rearrange("p (t n) -> p t n", t=2) for n in ("cos16", "sin16"))
            HR = ROPE // 2
            link(v.tensor_tensor(krt[:, 0], krg[:, :, 0:HR], cos, ALU.mult))
            link(v.tensor_tensor(krt[:, 1], krg[:, :, HR:ROPE], sin, ALU.mult))
            link(v.tensor_tensor(krt[:, 2], krg[:, :, 0:HR], sin, ALU.mult))
            link(v.tensor_tensor(krt[:, 3], krg[:, :, HR:ROPE], cos, ALU.mult))
            link(v.tensor_tensor(krr[:, :, 0:HR], krt[:, 0], krt[:, 1], ALU.subtract))
            link(v.tensor_tensor(krr[:, :, HR:ROPE], krt[:, 2], krt[:, 3], ALU.add))

            def conv(i):
                dve.wait_ge(conv_u, i + 1)
                bank = G[(use0["XBC"] + i) % 2]
                for d in (1, 2, 3):
                    for j in range(2):
                        m, c = 2 * i + j, cacc[:, i % 2, j]
                        if d > 1:
                            own.behind(1)
                        ins = v.scalar_tensor_tensor(out=c[:, d:T], in0=bank[:, j * T:(j + 1) * T - d],
                                                     scalar=cwh[:, m, 3 - d:4 - d], in1=c[:, d:T], op0=ALU.mult,
                                                     op1=ALU.add)
                        if d < 3 or j == 0:
                            own.sig(ins)
                ins.then_inc(bank_free, 1)

            def conv_silu(i):
                dve.wait_ge(conv_t, i + 1)
                v.scalar_tensor_tensor(out=xbcT[:, 2 * i:2 * i + 2, :], in0=tb[:, i % 2], scalar=1.0,
                                       in1=cacc[:, i % 2], op0=ALU.add, op1=ALU.mult).then_inc(xbc_ready, 1)

            def scale_by_dt(i):
                dve.wait_ge(xs_tr, i + 1)
                v.tensor_tensor(xdt[:, :, 256 * i:256 * i + 256].rearrange("p t (h d) -> p t h d", d=HD_SSD),
                                B[2 + i % 2][:, :].rearrange("p (t h d) -> p t h d", t=2, d=HD_SSD),
                                dt2[:, :, 4 * i:4 * i + 4].unsqueeze(3).broadcast_to([P, TT, 4, HD_SSD]),
                                ALU.mult).then_inc(xdt_ready, 1)

            for i in range(12):
                conv(i)
                if i >= 1:
                    conv_silu(i - 1)
                if i == 2:
                    norm_inverse("qa")
                    norm_inverse("kva")
                if i == 4:
                    norm_scale("qa")
                if i == 5:
                    dve.wait_ge(n_lo, norm_end("qa"))
                    norm_scale("kva")
                if i == 2:
                    dve.wait_ge(cum_ps, 1)
                    link(v.tensor_copy(acum[:, :, :], B[4][:, 0:64].rearrange("p (t n) -> p t n", t=2)))
                    v.tensor_copy(acumT[:, :], B[4][0:32, 128:384]).then_inc(acumT_sb, 1)
                if 3 <= i < 11:
                    scale_by_dt(i - 3)
            conv_silu(11)

            keep = A("keep")

            def seg_step(i):
                dve.wait_ge(rows_in[i % 2], 16 * (i // 2 + 1))
                if i >= 1:
                    dve.wait_ge(m_ready, i)
                for h in range(4):
                    for tt, (a, b, lo) in enumerate(((0, T, 0), (T, BW, P))):
                        ins = v.tensor_scalar(seg[:, h, a:b], Rb[:, i % 2, h, lo:T],
                                              acum[:, tt, 4 * i + h:4 * i + h + 1], 0.0, ALU.subtract, ALU.min)
                ins.then_inc(seg_ready, 1)

            def m_step(i):
                dve.wait_ge(decay_ready, i + 1)
                if i >= 2:
                    dve.wait_ge(y_ps, i - 1)
                v.tensor_tensor(Mt[:, i % 2], seg[:, :, :], scM[:, i // 2].unsqueeze(1).broadcast_to([P, 4, BW]),
                                ALU.mult).then_inc(m_ready, 1)

            def y_step(i):
                dve.wait_ge(y_ps, i + 1)
                dve.wait_ge(bank_free, use0["Z"] + i + 1)
                for j in range(2):
                    m = 2 * i + j
                    link(v.scalar_tensor_tensor(out=xbcT[:, m, :], in0=xbcT[:, m, :], scalar=A("dskip")[:, m:m + 1],
                                                in1=B[4 + i % 2][:, j * T:(j + 1) * T], op0=ALU.mult, op1=ALU.add))
                v.tensor_tensor(xbcT[:, 2 * i:2 * i + 2, :], xbcT[:, 2 * i:2 * i + 2, :], zs[:, i % 2],
                                ALU.mult).then_inc(y_ready, 1)

            def z_step(i):
                dve.wait_ge(z_t, i + 1)
                if i >= 2:
                    dve.wait_ge(y_ready, i - 1)
                v.scalar_tensor_tensor(out=zs[:, i % 2], in0=tb[:, i % 2], scalar=1.0,
                                       in1=G[(use0["Z"] + i) % 2][:, :].rearrange("p (j t) -> p j t", j=2),
                                       op0=ALU.add, op1=ALU.mult).then_inc(bank_free, 1)

            for i in range(8):
                seg_step(i)
                if i == 0:
                    for g in range(NG_SSD):
                        dve.wait_ge(score_ps, g + 1)
                        v.tensor_tensor(scM[:, g], B[4 + g % 2][:, 0:BW], keep, ALU.mult).then_inc(score_sb, 1)
                    dve.wait_ge(score_sb, NG_SSD)
                m_step(i)
                if i >= 1:
                    y_step(i - 1)
                z_step(i)
            y_step(7)

            c_uq = SEC["UQ"][0]
            hd = lambda t: t.rearrange("p (h d) -> p h d", h=4)
            for n in range(16):
                dve.wait_ge(u_sq, n + 1)
                tt, h0 = n % 2, 4 * (n // 2 % 4)
                bank = HEAD_BANKS[n % len(HEAD_BANKS)]
                hs = slice(h0, h0 + 4)
                if n < 8:
                    own.sig(v.tensor_reduce(ssq[:, 0, tt, hs], hd(sqt[:, n % 2, 0:384]), AX_X, ALU.add))
                    v.tensor_tensor(q96[:, tt, hs, :], hd(bank[:, 0:384]),
                                    A("g_q").unsqueeze(1).broadcast_to([P, 4, QK]), ALU.mult).then_inc(bank_free, 1)
                else:
                    own.sig(v.tensor_reduce(ssq[:, 1, tt, hs], hd(sqt[:, n % 2, 0:256]), AX_X, ALU.add))
                    v.tensor_tensor(k96[:, tt, hs, 0:NOPE], hd(bank[:, :])[:, :, 0:NOPE],
                                    A("g_k")[:, 0:NOPE].unsqueeze(1).broadcast_to([P, 4, NOPE]),
                                    ALU.mult).then_inc(bank_free, 1)
            dve.wait_ge(bank_free, use0["GATE_B"])
            link(v.tensor_tensor(ssq[:, 1], ssq[:, 1], sskr[:, :].unsqueeze(2).broadcast_to([P, TT, H_MLA]), ALU.add))
            link(v.tensor_scalar(rqk[:, :, :, :], ssq[:, :, :, :], 1.0 / QK, EPS, ALU.mult, ALU.add))
            v.reciprocal(rqk[:, :, :, :], rqk[:, :, :, :]).then_inc(kq_ss, 1)
            cosb, sinb = (t.unsqueeze(2).broadcast_to([P, TT, H_MLA, HR]) for t in (cos, sin))
            x1, x2 = q96[:, :, :, NOPE:NOPE + HR], q96[:, :, :, NOPE + HR:QK]
            rotation(own, v, x1, x2, cosb, sinb, rot[:, 0], rot[:, 1])
            own.wait()
            dve.wait_ge(kq_rs, 1)
            link(v.tensor_scalar(qsc[:, 0], rqk[:, 0], QK ** -0.5, None, ALU.mult))
            link(v.tensor_scalar(qsc[:, 1], rqk[:, 0], -QK ** -0.5, None, ALU.mult))
            for tt in range(TT):
                rk = rqk[:, 1, tt, :].unsqueeze(2)
                link(v.tensor_tensor(k96[:, tt, :, 0:NOPE], k96[:, tt, :, 0:NOPE], rk.broadcast_to([P, H_MLA, NOPE]),
                                     ALU.mult))
                ins = v.tensor_tensor(k96[:, tt, :, NOPE:QK], krr[:, tt, :].unsqueeze(1).broadcast_to([P, H_MLA, ROPE]),
                                      rk.broadcast_to([P, H_MLA, ROPE]), ALU.mult)
                if tt == 0:
                    link(ins)
            ins.then_inc(kq_ready, 1)
            dve.wait_ge(kq_ready, 1)

            causal = A("causal")

            def head_step(s):
                h = s - 1
                if 0 <= h < H_MLA:
                    dve.wait_ge(s_ps, h + 1)
                    if h >= 3:
                        dve.wait_ge(pt_ps, h - 2)
                    m, b = mx[:, h % 3, :], B[2 + h % 2]
                    for tt, (lo, hi) in enumerate(((0, P), (P, BW))):
                        own.sig(v.tensor_tensor_reduce(out=Sm[:, h % 3, lo:hi], in0=b[:, lo:hi], in1=causal[:, lo:hi],
                                                       scale=1.0, scalar=NEG, op0=ALU.add, op1=ALU.max,
                                                       accum_out=m[:, tt:tt + 1]))
                    own.wait()
                    v.tensor_tensor(m[:, 2:4], m[:, 0:2], qsc[:, 1, :, h], ALU.mult).then_inc(sm_ready, 1)
                h = s - 3
                if 0 <= h < H_MLA:
                    dve.wait_ge(pt_ps, h + 1)
                    if h >= 1:
                        dve.wait_ge(o_ps, h)
                    v.tensor_copy(PTs[:, :], B[4][:, 0:BW]).then_inc(pt_sb, 1)
                h = s - 2
                if 0 <= h < H_MLA:
                    dve.wait_ge(p_exp, 2 * h + 2)
                    m = mx[:, h % 3, :]
                    link(v.reciprocal(m[:, 6:8], m[:, 4:6]))
                    v.tensor_scalar(Sm[:, h % 3, 0:P], Sm[:, h % 3, 0:P], m[:, 6:7], None, ALU.mult)
                    v.tensor_scalar(Sm[:, h % 3, P:BW], Sm[:, h % 3, P:BW], m[:, 7:8], None,
                                    ALU.mult).then_inc(p_ready, 1)
                h = s - 4
                if 0 <= h < H_MLA and h % 2:
                    dve.wait_ge(o_hi, h // 2 + 1)
                    v.tensor_tensor(olo[:, h // 2, :], B[5][:, 0:T], ohi[:, h // 2, :],
                                    ALU.subtract).then_inc(o_lo, 1)

            step = 0
            for i in range(7):
                if i == 0:
                    norm_inverse("y")
                    norm_scale("y", range(0, 2))
                    continue
                for _ in range(1 if i == 1 else 2):
                    head_step(step)
                    step += 1
                if i < 4:
                    norm_scale("y", range(2 * i, 2 * i + 2))
            dve.wait_ge(bank_free, use0["SSDP"])
            for i in range(8):
                if step < H_MLA + 4:
                    head_step(step)
                    step += 1
                dve.wait_ge(chunk_used, SEC["SSDP"][0] + i + 1)
                v.scalar_tensor_tensor(out=gT[:, i, :], in0=gT[:, i, :], scalar=1.0,
                                       in1=G[(use0["SSDP"] + i) % 2][:, 0:T], op0=ALU.add,
                                       op1=ALU.mult).then_inc(bank_free, 1)
                if step < H_MLA + 4 and i >= 1:
                    head_step(step)
                    step += 1
            two = lambda t: t.rearrange("p (j t) -> p j t", j=2)

            def mix_low(k, mix, hi_done_of, lo_done_of):
                dve.wait_ge(hi_done_of, k + 1)
                tiles = slice(2 * k, 2 * k + 2)
                v.tensor_tensor(h_lo[:, tiles, :], mix[:, tiles, :], h_hi[:, tiles, :],
                                ALU.subtract).then_inc(lo_done_of, 1)

            for i in range(4):
                dve.wait_ge(chunk_used, SEC["MLAP"][0] + i + 1)
                gm, ma = gT[:, 8 + 2 * i:10 + 2 * i, :], mixa[:, 2 * i:2 * i + 2, :]
                v.scalar_tensor_tensor(out=gm, in0=gm, scalar=1.0, in1=two(G[(use0["MLAP"] + i) % 2][:, :]),
                                       op0=ALU.add, op1=ALU.mult).then_inc(bank_free, 1)
                dve.wait_ge(bank_free, use0["MLAP"] + i + 1)
                if i == 0:
                    dve.wait_ge(qkT_sb, H_MLA)
                v.tensor_tensor(ma, gT[:, 2 * i:2 * i + 2, :], gm, ALU.add).then_inc(mix_ready, 1)
                for k in range(max(i - 1, 0), i + i // 3):
                    mix_low(k, mixa, mix_hi, mix_lo)
            for i in range(4):
                dve.wait_ge(chunk_used, SEC["WO"][0] + i + 1)
                x = xT[:, 2 * i:2 * i + 2, :]
                v.scalar_tensor_tensor(out=x, in0=two(G[(use0["WO"] + i) % 2][:, :]), scalar=0.5, in1=x, op0=ALU.mult,
                                       op1=ALU.add).then_inc(bank_free, 1)
                dve.wait_ge(bank_free, use0["WO"] + i + 1)
                scale_piece("ffn", i)
                if i:
                    low_piece("ffn", i - 1)
                    add_squares("ffn", i)
            low_piece("ffn", 3)
            norm_inverse("ffn")
            dve.wait_ge(y_rs, 2)
            root2 = ry[:, 0:1, :].broadcast_to([P, 2, T])

            u0, c0 = use0["UP"], SEC["UP"][0]

            def ffn_root(k, par, bank, it=None):
                kk = k if it is None else it * 4 + k
                dve.wait_ge(chunk_used, kk + (c0 + 1))
                if k >= 2 or it is not None:
                    dve.wait_ge(f_acc, kk - 1)
                    dve.wait_ge(f_u, kk - 1)
                v.tensor_tensor(fub[:, par], two(G[bank][:, :]), root2, ALU.mult).then_inc(bank_free, 1)

            def ffn_conv(k, par, it=None):
                kk = k if it is None else it * 4 + k
                dve.wait_ge(f_u, kk + 1)
                for d in (1, 2):
                    for j in range(2):
                        w = fwh[:, bass.ds(kk * 2 + j, 1), :].rearrange("p a b -> p (a b)")
                        c = facc[:, par, j]
                        if d == 2:
                            own.behind(1 - j)
                        ins = v.scalar_tensor_tensor(out=c[:, d:T], in0=fub[:, par, j, 0:T - d],
                                                     scalar=w[:, 2 - d:3 - d], in1=c[:, d:T], op0=ALU.mult,
                                                     op1=ALU.add)
                        if d == 1:
                            own.sig(ins)
                ins.then_inc(f_acc, 1)

            def ffn_product(k, par, it=None):
                kk = k if it is None else it * 4 + k
                dve.wait_ge(f_t, kk + 1)
                if k >= 2 or it is not None:
                    dve.wait_ge(f_lo, kk - 1)
                link(v.scalar_tensor_tensor(out=ftg[:, par], in0=ftg[:, par], scalar=1.0, in1=facc[:, par, 0],
                                            op0=ALU.add, op1=ALU.mult))
                v.tensor_tensor(fg[:, par], ftg[:, par], facc[:, par, 1], ALU.mult).then_inc(f_g, 1)

            def ffn_lo(k, par, it=None):
                kk = k if it is None else it * 4 + k
                dve.wait_ge(f_hi, kk + 1)
                v.tensor_tensor(g_lo[:, kk, :], fg[:, par], g_hi[:, kk, :], ALU.subtract).then_inc(f_lo, 1)

            ffn_root(0, 0, u0 % 2)
            ffn_conv(0, 0)

            def ffn_step(k, it=None):
                ffn_root(k, k % 2, (u0 + k) % 2, it)
                ffn_product(k - 1, (k - 1) % 2, it)
                ffn_conv(k, k % 2, it)
                ffn_lo(k - 1, (k - 1) % 2, it)

            for k in (1, 2):
                ffn_step(k)
            base = own.n
            with dve.Fori(0, 4, 1) as i:
                own.n = i * (4 * FFN_LINKS) + base
                for j in range(4):
                    ffn_step(3 + j, i)
            own.n = base + 16 * FFN_LINKS
            for k in range(19, 22):
                ffn_step(k)
            ffn_product(21, 1)
            ffn_lo(21, 1)
            u0, c0 = use0["DOWN"], SEC["DOWN"][0]
            for k in range(KD):
                dve.wait_ge(chunk_used, c0 + 2 * k + 2)
                x = xT[:, k, :]
                v.tensor_tensor(x, G[(u0 + k) % 2][:, 0:T], x, ALU.add).then_inc(bank_free, 1)
                if k >= 4 and k % 2:
                    add_squares("x2", (k - 3) // 2)

            add_squares("x2", 3)
            dve.wait_ge(bank_free, use0["CKV"])
            norm_inverse("x2")
            norm_scale("x2")
            dve.wait_ge(pb_in, 16)
            dve.wait_ge(n_hi, norm_end("x2"))
            link(v.memset(bT[:, :, :, :, :], 0.0))
            dve.wait_ge(cblk_in, 64)
            for kv, name in enumerate(("pos_k", "pos_v")):
                tokens = cblk[:, 3 * kv:3 * kv + 3, :].rearrange("p g (n b two) -> p g n b two", b=8, two=2)
                for half_block in range(2):
                    ins = v.tensor_tensor(
                        bT[:, kv, 8 * half_block:8 * half_block + 8, :, 0:NC].rearrange("p b g n -> p g n b"),
                        tokens[:, :, half_block:half_block + NC, :, 0],
                        Bp(name)[:, 8 * half_block:8 * half_block + 8].unsqueeze(1).unsqueeze(1)
                        .broadcast_to([P, 3, NC, 8]), ALU.add)
                    if kv + half_block < 2:
                        link(ins)
            ins.then_inc(b_ready, 1)

            cos32, sin32 = (Bp(n).rearrange("p (t n) -> p t n", t=2) for n in ("cos32", "sin32"))
            HH = HD // 2

            def rotate(x, n, cosb, sinb, t0, t1):
                x1, x2 = x[..., 0:HH], x[..., HH:HD]
                rotation(own, v, x1, x2, cosb, sinb, t0, t1)
                own.wait()

            def token_heads(n, name, i, heads, head0, gain):
                u = use0[name] + i
                dve.wait_ge(t_sq, n + 1)
                src = G[u % 2][:, :].rearrange("p (t h d) -> p t h d", t=2, d=HD)
                c0 = i * 256 if name == "TM_A" else 1536 + i * 256
                dst = tm[:, :, c0:c0 + 256].rearrange("p t (h d) -> p t h d", d=HD)
                v.tensor_reduce(ss2[:, :, head0:head0 + heads], sqt2[:, n % 2].rearrange("p (t h) d -> p t h d", t=2)
                                [:, :, 0:heads, :], AX_X, ALU.add).then_inc(t_free, 1)
                if heads < 4:
                    link(v.tensor_copy(dst[:, :, heads:4, :], src[:, :, heads:4, :]))
                v.tensor_tensor(dst[:, :, 0:heads, :], src[:, :, 0:heads, :], gain, ALU.mult).then_inc(bank_free, 1)
                dve.wait_ge(bank_free, u + 1)
                bc = lambda t: t.unsqueeze(2).broadcast_to([P, TT, heads, HH])
                if name == "TM_A":
                    rotate(dst[:, :, 0:heads, :], heads, bc(cos32), bc(sin32), rt[:, 0, :, 0:heads],
                           rt[:, 1, :, 0:heads])

            def same_gain(name):
                return Bp(name).unsqueeze(1).unsqueeze(1).broadcast_to([P, TT, 4, HD])

            def k_gain(h0, n):
                return (Bp("g_k")[:, h0 * HD:(h0 + n) * HD].rearrange("p (h d) -> p h d", d=HD).unsqueeze(1)
                        .broadcast_to([P, TT, n, HD]))

            for i in range(6):
                if i < 3:
                    token_heads(i, "TM_A", i, 4, 4 * i, same_gain("g_qa2"))
                elif i < 5:
                    token_heads(i, "TM_A", i, 4 if i == 3 else 2, 4 * i, k_gain(4 * (i - 3), 4 if i == 3 else 2))
                else:
                    u = use0["TM_A"] + i
                    dve.wait_ge(chunk_used, SEC["TM_A"][0] + i + 1)
                    v.tensor_copy(tm[:, :, 1280:1536], G[u % 2][:, :].rearrange("p (t n) -> p t n", t=2)
                                  ).then_inc(bank_free, 1)
                if i == 3:
                    dve.wait_ge(b_hi, 1)
                    flat = lambda t: t[:, :, :, :, :].rearrange("p a b g n -> p (a b g n)")
                    v.tensor_tensor(flat(bT_lo), flat(bT), flat(bT_hi), ALU.subtract).then_inc(b_lo, 1)

            def roots(lo, hi, n, k_lo, k_cols):
                link(v.tensor_scalar(ss2[:, :, lo:hi], ss2[:, :, lo:hi], 1.0 / HD, EPS, ALU.mult, ALU.add))
                v.reciprocal(ss2[:, :, lo:hi], ss2[:, :, lo:hi]).then_inc(ss_ready, 1)
                dve.wait_ge(rs_ready, n)
                link(v.tensor_scalar(qs2[:, 0, :, lo:hi], r2[:, :, lo:hi], HD ** -0.5, None, ALU.mult))
                link(v.tensor_scalar(qs2[:, 1, :, lo:hi], r2[:, :, lo:hi], -HD ** -0.5, None, ALU.mult))
                k = tm[:, :, k_cols:k_cols + (hi - k_lo) * HD].rearrange("p t (h d) -> p t h d", d=HD)
                v.tensor_tensor(k, k, r2[:, :, k_lo:hi].unsqueeze(3).broadcast_to([P, TT, hi - k_lo, HD]),
                                ALU.mult).then_inc(k_ready, 1)

            for i in range(4):
                c = SEC["CW1"][0] + i
                dve.wait_ge(hi_done, c + 1)
                cols = slice(SLOT // 2, SLOT)
                v.tensor_tensor(w_lo[:, c % SLOTS, cols], raw[:, c % SLOTS, cols], w_hi[:, c % SLOTS, cols],
                                ALU.subtract).then_inc(lo_shared, 1)
                if i == 0:
                    roots(0, 18, 1, 12, 768)
            dve.wait_ge(gn_ps, 1)
            link(v.tensor_scalar(gnsa[:, :, :], B[4][:, 0:P].rearrange("p (t n) -> p t n", t=2)[:, :, 0:36], 0.5, 0.5,
                                 ALU.mult, ALU.add))
            dve.wait_ge(bank_free, use0["CW1"] + 2)
            link(v.tensor_tensor(hid[:, 1], hid[:, 0], hid[:, 0], ALU.mult))
            link(v.tensor_scalar(hid[:, 1], hid[:, 1], 0.044715, 1.0, ALU.mult, ALU.add))
            v.tensor_tensor(hid[:, 1], hid[:, 1], hid[:, 0], ALU.mult).then_inc(ge_in, 1)
            dve.wait_ge(ge_t, 1)
            link(v.tensor_scalar(hid[:, 1], hid[:, 1], 0.5, 0.5, ALU.mult, ALU.add))
            v.tensor_tensor(hid[:, 0], hid[:, 0], hid[:, 1], ALU.mult).then_inc(ge_done, 1)

            def compressed_keys():
                dve.wait_ge(c_ps, 1)
                ps = B[0][0:CG, 0:6 * HD].rearrange("p (k g d) -> p k g d", k=2, g=3)
                link(v.tensor_copy(vc[:, :, :], ps[:, 1]))
                link(v.tensor_copy(cn[:, 0], ps[:, 0]))
                link(v.tensor_tensor(cn[:, 1], cn[:, 0], cn[:, 0], ALU.mult))
                link(v.tensor_reduce(ssc[:, 0, :], cn[:, 1], AX_X, ALU.add))
                link(v.tensor_scalar(ssc[:, 0, :], ssc[:, 0, :], 1.0 / HD, EPS, ALU.mult, ALU.add))
                v.reciprocal(ssc[:, 0, :], ssc[:, 0, :]).then_inc(c_ss, 1)
                dve.wait_ge(c_rs, 1)
                link(v.tensor_tensor(cn[:, 0], cn[:, 0], ssc[:, 1, :].unsqueeze(2).broadcast_to([CG, 3, HD]),
                                     ALU.mult))
                link(v.tensor_tensor(cn[:, 0], cn[:, 0], Bp("g_kc")[0:CG].unsqueeze(1).broadcast_to([CG, 3, HD]),
                                     ALU.mult))
                bc = lambda name: Bp(name)[0:CG].unsqueeze(1).broadcast_to([CG, 3, HH])
                rotation(own, v, cn[:, 0, :, 0:HH], cn[:, 0, :, HH:HD], bc("cosc"), bc("sinc"), cn[:, 1, :, 0:HH],
                         cn[:, 2, :, 0:HH], cn_ready)

            any_key, no_key, cmp_add = Bp("cmp_any"), Bp("cmp_none"), Bp("cmp_add")

            def nsa_step(s):
                h = s - 1
                if 0 <= h < H_NSA:
                    dve.wait_ge(ns_ps, h + 1)
                    if h >= 3:
                        dve.wait_ge(npt_ps, h - 2)
                        dve.wait_ge(nq_ps, h + 1)
                    m = m2[:, h % 3]
                    for b, src, s0, c0, w0, w1, mask in ((0, B[2], BW, 768, CG, CG, cmp_add),
                                                         (1, B[1], 0, 0, P, T, causal), (2, B[2], 0, BW, P, T, causal)):
                        for tt in range(TT):
                            w, o = (w1 if tt else w0), tt * w0
                            own.sig(v.tensor_tensor_reduce(
                                out=SN[:, h % 3, c0 + o:c0 + o + w], in0=src[:, s0 + o:s0 + o + w],
                                in1=mask[:, o:o + w], scale=1.0, scalar=NEG, op0=ALU.add, op1=ALU.max,
                                accum_out=m[:, 0, 2 * b + tt:2 * b + tt + 1]))
                    own.wait()
                    link(v.tensor_tensor(m[:, 0, 0:2], m[:, 0, 0:2], any_key, ALU.mult))
                    v.tensor_tensor(m[:, 1].rearrange("p (b t) -> p b t", t=2),
                                    m[:, 0].rearrange("p (b t) -> p b t", t=2),
                                    qs2[:, 1, :, h].unsqueeze(1).broadcast_to([P, 3, TT]),
                                    ALU.mult).then_inc(nm_ready, 1)
                h = s - 2
                if 0 <= h < H_NSA:
                    dve.wait_ge(n_exp, 6 * h + 6)
                    m = m2[:, h % 3]
                    link(v.tensor_tensor(m[:, 2, 0:2], m[:, 2, 0:2], no_key, ALU.add))
                    link(v.reciprocal(m[:, 3], m[:, 2]))
                    link(v.tensor_tensor(m[:, 3].rearrange("p (b t) -> p t b", t=2),
                                         m[:, 3].rearrange("p (b t) -> p t b", t=2),
                                         gnsa[:, :, 3 * h:3 * h + 3], ALU.mult))
                    for b, c0, w0, w1 in ((1, 0, P, T), (2, BW, P, T), (0, 768, CG, CG)):
                        for tt in range(TT):
                            w, o = (w1 if tt else w0), c0 + tt * w0
                            x = SN[:, h % 3, o:o + w]
                            ins = v.tensor_scalar(x, x, m[:, 3, 2 * b + tt:2 * b + tt + 1], None, ALU.mult)
                    ins.then_inc(np_ready, 1)
                h = s - 3
                if 0 <= h < H_NSA:
                    dve.wait_ge(npt_ps, h + 1)
                    if h >= 2:
                        dve.wait_ge(no_ps, h - 1)
                    own.sig(v.tensor_copy(PT2[:, 2 * (h % 2), :], B[3][:, 0:BW]))
                    v.tensor_copy(PT2[:, 2 * (h % 2) + 1, :], B[4][:, 0:BW]).then_inc(npt_sb, 1)
                h = s - 4
                if 0 <= h < H_NSA and h % 2:
                    dve.wait_ge(no_hi, h // 2 + 1)
                    v.tensor_tensor(o2_lo[:, h // 2, :], B[5][:, 0:T], o2_hi[:, h // 2, :],
                                    ALU.subtract).then_inc(no_lo, 1)

            dil_mask = Bp("dil")

            def dil_step(s):
                u = s - 1
                if 0 <= u < H_DIL:
                    hh, g = u // 3, u % 3
                    dve.wait_ge(ds_ps, u + 1)
                    if g == 0 and hh >= 2:
                        dve.wait_ge(dpt_ps, 3 * hh - 3)
                    if u == 0:
                        dve.wait_ge(npt_ps, H_NSA)
                        dve.wait_ge(nq_ps, H_NSA + 3)
                    m = m2[:, hh % 2]
                    for tt, (a, b) in enumerate(((0, P), (P, BW))):
                        link(v.tensor_tensor_reduce(
                            out=SD[:, hh % 2, g * BW + a:g * BW + b], in0=B[1 + u % 2][:, a:b],
                            in1=dil_mask[:, g * BW + a:g * BW + b], scale=1.0, scalar=NEG, op0=ALU.add, op1=ALU.max,
                            accum_out=m[:, 0, 2 * g + tt:2 * g + tt + 1]))
                    v.tensor_tensor(m[:, 1, 2 * g:2 * g + 2], m[:, 0, 2 * g:2 * g + 2],
                                    qs2[:, 1, :, 18 + g * DH + hh], ALU.mult).then_inc(dm_part, 1)
                    if g == 2:
                        dve.wait_ge(dm_part, u + 1)
                        v.tensor_reduce(md[:, 0, :], m[:, 1].rearrange("p (b t) -> p t b", t=2), AX_X,
                                        ALU.min).then_inc(dm_ready, 1)
                u = s - 5
                if 0 <= u < H_DIL:
                    dve.wait_ge(dpt_ps, u + 1)
                    if u >= 2:
                        dve.wait_ge(do_ps, u - 1)
                    if u == 0:
                        dve.wait_ge(no_ps, H_NSA)
                    v.tensor_copy(PT2[:, u % 2, :], B[3 + u % 2][:, 0:BW]).then_inc(dpt_sb, 1)
                u = s - 2
                if 0 <= u < H_DIL and u % 3 == 2:
                    hh = u // 3
                    dve.wait_ge(d_exp, 6 * hh + 6)
                    m = m2[:, hh % 2]
                    link(v.tensor_reduce(md[:, 1, :], m[:, 2].rearrange("p (b t) -> p t b", t=2), AX_X, ALU.add))
                    link(v.reciprocal(md[:, 1, :], md[:, 1, :]))
                    x = SD[:, hh % 2, :].rearrange("p (g n) -> p g n", g=3)
                    link(v.tensor_scalar(x[:, :, 0:P], x[:, :, 0:P], md[:, 1, 0:1], None, ALU.mult))
                    v.tensor_scalar(x[:, :, P:BW], x[:, :, P:BW], md[:, 1, 1:2], None,
                                    ALU.mult).then_inc(dp_ready, 1)
                u = s - 6
                if 0 <= u < H_DIL and u % 6 == 5:
                    dve.wait_ge(do_hi, u // 6 + 1)
                    v.tensor_tensor(o2_lo[:, 6 + u // 6, :], B[5][:, 0:T], o2_hi[:, 6 + u // 6, :],
                                    ALU.subtract).then_inc(do_lo, 1)

            nsa = dil = 0
            for i in range(9):
                if i == 1:
                    compressed_keys()
                if i >= 2:
                    nsa_step(nsa)
                if i >= 2:
                    nsa_step(nsa + 1)
                    nsa += 2
                if i < 6:
                    token_heads(5 + i, "TM_B", i, 4, 18 + 4 * i, same_gain("g_qb" if i < 3 else "g_kb"))
                else:
                    u = use0["TM_B"] + i
                    dve.wait_ge(chunk_used, SEC["TM_B"][0] + i + 1)
                    v.tensor_copy(tm[:, :, 1536 + 256 * i:1792 + 256 * i], G[u % 2][:, :]
                                  .rearrange("p (t n) -> p t n", t=2)).then_inc(bank_free, 1)
            for i in range(8):
                for j in range(2):
                    if i == 0 and j == 1:
                        dve.wait_ge(pool_own, 36)
                        roots(18, 42, 2, 30, 2304)
                    if nsa < H_NSA + 4:
                        nsa_step(nsa)
                        nsa += 1
                    else:
                        dil_step(dil)
                        dil += 1
            def gate(i, first, bank):
                g = gT2[:, first + 2 * i:first + 2 * i + 2, :]
                v.scalar_tensor_tensor(out=g, in0=g, scalar=1.0, in1=two(bank[:, :]), op0=ALU.add,
                                       op1=ALU.mult).then_inc(bank_free, 1)

            for i in range(4):
                for j in range(2):
                    if j:
                        if i == 0:
                            dve.wait_ge(bank_free, use0["OA"])
                        dve.wait_ge(chunk_used, SEC["OA"][0] + i + 1)
                        gate(i, 0, G[(use0["OA"] + i) % 2])
                    if dil < H_DIL + 6:
                        dil_step(dil)
                        dil += 1
            while dil < H_DIL + 6:
                dil_step(dil)
                dil += 1
            for i in range(4):
                u = use0["OB"] + i
                if i < 3:
                    dve.wait_ge(ob_ps, i + 1)
                else:
                    dve.wait_ge(chunk_used, SEC["OB"][0] + 1)
                gate(i, 8, G[u % 2])
                dve.wait_ge(bank_free, u + 1)
                ma = mix2[:, 2 * i:2 * i + 2, :]
                v.tensor_tensor(ma, gT2[:, 2 * i:2 * i + 2, :], gT2[:, 8 + 2 * i:10 + 2 * i, :],
                                ALU.add).then_inc(mix2_ready, 1)
                for k in range(max(i - 1, 0), i + i // 3):
                    mix_low(k, mix2, mix2_hi, mix2_lo)
            for i in range(4):
                dve.wait_ge(chunk_used, SEC["WOUT"][0] + i + 1)
                x = xT[:, 2 * i:2 * i + 2, :]
                v.scalar_tensor_tensor(out=x, in0=two(G[(use0["WOUT"] + i) % 2][:, :]), scalar=0.5, in1=x,
                                       op0=ALU.mult, op1=ALU.add).then_inc(bank_free, 1)
                dve.wait_ge(bank_free, use0["WOUT"] + i + 1)
                scale_piece("ffn2", i)
                if i:
                    low_piece("ffn2", i - 1)
                    add_squares("ffn2", i)
            low_piece("ffn2", 3)
            norm_inverse("ffn2")
            dve.wait_ge(y_rs, 3)
            u0 = use0["UP2"]

            def square(k, par, it=None):
                kk = k if it is None else it * 4 + k
                dve.wait_ge(bank_free, kk + (u0 + 1))
                if k >= 2 or it is not None:
                    dve.wait_ge(sq_lo, kk - 1)
                link(v.tensor_tensor(srl[:, par], srl[:, par], root2, ALU.mult))
                v.tensor_tensor(ssqr[:, par], srl[:, par], srl[:, par], ALU.mult).then_inc(sq_f, 1)
                dve.wait_ge(sq_hi, kk + 1)
                v.tensor_tensor(s_lo[:, bass.ds(kk * 2, 2), :], ssqr[:, par], s_hi[:, bass.ds(kk * 2, 2), :],
                                ALU.subtract).then_inc(sq_lo, 1)

            for k in range(2):
                square(k, k % 2)
            base = own.n
            with dve.Fori(0, 3, 1) as i:
                own.n = i * 4 + base
                for j in range(4):
                    square(2 + j, j % 2, i)
            own.n = base + 12
            for k in range(14, 16):
                square(k, k % 2)
            u0, c0 = use0["DOWN2"], SEC["DOWN2"][0]
            with dve.Fori(0, 4, 1) as i:
                for j in range(2):
                    dve.wait_ge(chunk_used, i * 4 + (c0 + 2 * j + 2))
                    x = xT[:, i * 2 + j, :]
                    v.tensor_tensor(x, G[(u0 + j) % 2][:, 0:T], x, ALU.add).then_inc(bank_free, 1)


def kernel(**inputs):
    import concourse.bacc as bacc
    from concourse.bass_utils import run_bass_kernel_spmd

    a = {n: np.asarray(v) for n, v in inputs.items()}
    x = a["x"].reshape(T, D)
    pa, pb = pack_params(a)
    arrays = {"wstream": pack_stream(a), "x_t": np.ascontiguousarray(_rows(x.T, KD)), "params_a": pa, "params_b": pb}
    nc = bacc.Bacc("TRN2", target_bir_lowering=False, num_devices=1)
    args = [nc.dram_tensor(n, v.shape, F32, kind="ExternalInput").ap() for n, v in arrays.items()]
    out = nc.dram_tensor("out_t", (P, KD, T), F32, kind="ExternalOutput").ap()
    blocks_kernel(nc, *args, out)
    r = run_bass_kernel_spmd(nc, [arrays], core_ids=[0])
    y = r.results[0]["out_t"]
    return np.ascontiguousarray(y.transpose(2, 1, 0).reshape(1, T, D))
```
